# Optimizing a Trainium2 kernel written in Bass

```python
import math
import jax, jax.numpy as jnp
from jax import lax
import numpy as np

D_MODEL = 1024
BATCH = 1
SEQ = 512
DEPTH = 1

HEAD_DIM = 64
SC_WIDTH = D_MODEL
SC_HEADS = SC_WIDTH // HEAD_DIM
SC_WIN = 3
SSM_WIDTH = D_MODEL
SSM_HEADS = SSM_WIDTH // HEAD_DIM
SSM_GROUPS = 2
SSM_STATE = 128
SSM_CONV = 4
SSM_CHUNK = 128
SSM_GN = SSM_GROUPS * SSM_STATE
SSM_CONV_DIM = SSM_WIDTH + 2 * SSM_GN
MIX_WIDTH = SC_WIDTH + SSM_WIDTH
IN_WIDTH = 3 * SC_WIDTH + SSM_WIDTH + SSM_CONV_DIM + SSM_HEADS
IN_SPLITS = [SC_WIDTH, 2 * SC_WIDTH, 3 * SC_WIDTH, 3 * SC_WIDTH + SSM_WIDTH,
             3 * SC_WIDTH + SSM_WIDTH + SSM_CONV_DIM]
PEER_HEADS = 8
PEER_NKEYS = 128
PEER_EXPERTS = PEER_NKEYS * PEER_NKEYS
PEER_TOPK = 16
PEER_DKEY = 256
PEER_HALF = PEER_DKEY // 2
PEER_BLOCK = 128
DEEPNORM_ALPHA = (2.0 * DEPTH) ** 0.25
DEEPNORM_BETA = (8.0 * DEPTH) ** -0.25
LN_EPS = 1e-5
RMS_EPS = 1e-6

kernel_name = "hymba_conv_ssd_peer_deepnorm_adaln"

def layer_norm(x, g, b):
    xf = x.astype(jnp.float32)
    mu = jnp.mean(xf, -1, keepdims=True)
    var = jnp.mean(jnp.square(xf - mu), -1, keepdims=True)
    return ((xf - mu) * lax.rsqrt(var + LN_EPS) * g + b).astype(x.dtype)

def group_rms_norm(x, w, n_groups):
    shp = x.shape
    xf = x.astype(jnp.float32).reshape(shp[:-1] + (n_groups, shp[-1] // n_groups))
    xf = xf * lax.rsqrt(jnp.mean(jnp.square(xf), -1, keepdims=True) + RMS_EPS)
    return (xf.reshape(shp) * w).astype(x.dtype)

def causal_dwconv(x, w):
    k, ch = w.shape
    return lax.conv_general_dilated(x, w[:, None, :], window_strides=(1,), padding=[(k - 1, 0)],
                                    dimension_numbers=('NWC', 'WIO', 'NWC'), feature_group_count=ch)

def ssd_chunked(x, dt, a, b_in, c_in):
    bsz, seqlen, n_heads, hd = x.shape
    g = b_in.shape[2]
    r = n_heads // g
    L = SSM_CHUNK
    nc = seqlen // L
    xdt = (x * dt[..., None].astype(x.dtype)).reshape(bsz, nc, L, g, r, hd)
    a_dt = (dt * a).reshape(bsz, nc, L, g, r)
    a_dt = jnp.transpose(a_dt, (0, 3, 4, 1, 2))
    bc = b_in.reshape(bsz, nc, L, g, -1)
    cc = c_in.reshape(bsz, nc, L, g, -1)
    a_cum = jnp.cumsum(a_dt, -1)
    seg = a_cum[..., :, None] - a_cum[..., None, :]
    causal = jnp.tril(jnp.ones((L, L), dtype=bool))
    decay_in = jnp.where(causal, jnp.exp(jnp.where(causal, seg, 0.0)), 0.0).astype(x.dtype)
    cb = jnp.einsum('bclgn,bcsgn->bgcls', cc, bc)
    y_diag = jnp.einsum('bgcls,bgrcls,bcsgrp->bclgrp', cb, decay_in, xdt)
    decay_to_end = jnp.exp(a_cum[..., -1:] - a_cum).astype(x.dtype)
    chunk_states = jnp.einsum('bclgn,bgrcl,bclgrp->cbgrpn', bc, decay_to_end, xdt)
    chunk_decay = jnp.moveaxis(jnp.exp(a_cum[..., -1]), -1, 0).astype(x.dtype)

    def step(h, inp):
        s_c, d_c = inp
        return h * d_c[..., None, None] + s_c, h

    h0 = jnp.zeros(chunk_states.shape[1:], x.dtype)
    _, prev_states = lax.scan(step, h0, (chunk_states, chunk_decay))
    decay_from_start = jnp.exp(a_cum).astype(x.dtype)
    y_off = jnp.einsum('bclgn,cbgrpn,bgrcl->bclgrp', cc, prev_states, decay_from_start)
    return (y_diag + y_off).reshape(bsz, seqlen, n_heads, hd)

def hybrid_mixer(u, w_in, sc_conv_w, ssm_conv_w, ssm_conv_b, dt_bias, a_log, d_skip,
                 sc_norm_w, ssm_norm_w, w_out):
    bsz, seqlen, _ = u.shape
    proj = u @ w_in
    sc_b, sc_c, sc_h, z, xbc, dt = jnp.split(proj, IN_SPLITS, axis=-1)
    y_sc = sc_b * causal_dwconv(sc_c * sc_h, sc_conv_w)
    y_sc = group_rms_norm(y_sc, sc_norm_w, SC_HEADS)
    xbc = jax.nn.silu(causal_dwconv(xbc, ssm_conv_w) + ssm_conv_b)
    xs, bs, cs = jnp.split(xbc, [SSM_WIDTH, SSM_WIDTH + SSM_GN], axis=-1)
    dt = jax.nn.softplus(dt.astype(jnp.float32) + dt_bias.astype(jnp.float32))
    a = -jnp.exp(a_log.astype(jnp.float32))
    xh = xs.reshape(bsz, seqlen, SSM_HEADS, HEAD_DIM)
    y = ssd_chunked(xh, dt, a,
                    bs.reshape(bsz, seqlen, SSM_GROUPS, SSM_STATE),
                    cs.reshape(bsz, seqlen, SSM_GROUPS, SSM_STATE))
    y = (y + xh * d_skip[:, None]).reshape(bsz, seqlen, SSM_WIDTH)
    y_ssm = group_rms_norm(y * jax.nn.silu(z), ssm_norm_w, SSM_GROUPS)
    return jnp.concatenate([y_sc, y_ssm], axis=-1) @ w_out

def peer_ffn(u, w_query, sub_keys1, sub_keys2, expert_u, expert_v):
    bsz, seqlen, d = u.shape
    q = (u @ w_query).reshape(bsz, seqlen, PEER_HEADS, 2, PEER_HALF)
    s1 = jnp.einsum('bshk,hnk->bshn', q[..., 0, :], sub_keys1).astype(jnp.float32)
    s2 = jnp.einsum('bshk,hnk->bshn', q[..., 1, :], sub_keys2).astype(jnp.float32)
    v1, i1 = lax.top_k(s1, PEER_TOPK)
    v2, i2 = lax.top_k(s2, PEER_TOPK)
    cand = (v1[..., :, None] + v2[..., None, :]).reshape(bsz, seqlen, PEER_HEADS, PEER_TOPK * PEER_TOPK)
    top_s, top_ij = lax.top_k(cand, PEER_TOPK)
    e_idx = (jnp.take_along_axis(i1, top_ij // PEER_TOPK, axis=-1) * PEER_NKEYS
             + jnp.take_along_axis(i2, top_ij % PEER_TOPK, axis=-1))
    gate = jax.nn.softmax(top_s, axis=-1).astype(u.dtype)
    nb = (bsz * seqlen) // PEER_BLOCK
    ub = u.reshape(nb, PEER_BLOCK, d)
    eb = e_idx.reshape(nb, PEER_BLOCK, PEER_HEADS, PEER_TOPK)
    gb = gate.reshape(nb, PEER_BLOCK, PEER_HEADS, PEER_TOPK)

    def block(args):
        xt, et, gt = args
        h = jnp.einsum('td,thkd->thk', xt, expert_u[et])
        act = jax.nn.gelu(h, approximate=False) * gt
        return jnp.einsum('thk,thkd->td', act, expert_v[et])

    return lax.map(block, (ub, eb, gb)).reshape(bsz, seqlen, d)

def setup_inputs(seed: int = 0) -> dict:
    key = jax.random.key(seed)
    ks = jax.random.split(key, 24)
    f32 = jnp.float32
    nrm = lambda k, shp, s: jax.random.normal(k, shp, f32) * s
    dt0 = jnp.exp(jax.random.uniform(ks[9], (DEPTH, SSM_HEADS), f32, math.log(1e-3), math.log(1e-1)))
    return {
        "x": nrm(ks[0], (BATCH, SEQ, D_MODEL), 1.0),
        "c": nrm(ks[1], (BATCH, D_MODEL), 1.0),
        "w_cond": nrm(ks[2], (DEPTH, D_MODEL, 6 * D_MODEL), 0.2 * D_MODEL ** -0.5),
        "b_cond": nrm(ks[3], (DEPTH, 6 * D_MODEL), 0.02),
        "w_in": nrm(ks[4], (DEPTH, D_MODEL, IN_WIDTH), D_MODEL ** -0.5),
        "sc_conv_w": nrm(ks[5], (DEPTH, SC_WIN, SC_WIDTH), SC_WIN ** -0.5),
        "ssm_conv_w": nrm(ks[6], (DEPTH, SSM_CONV, SSM_CONV_DIM), SSM_CONV ** -0.5),
        "ssm_conv_b": nrm(ks[7], (DEPTH, SSM_CONV_DIM), 0.02),
        "dt_bias": dt0 + jnp.log(-jnp.expm1(-dt0)),
        "a_log": jnp.log(jax.random.uniform(ks[10], (DEPTH, SSM_HEADS), f32, 1.0, 16.0)),
        "d_skip": 1.0 + nrm(ks[11], (DEPTH, SSM_HEADS), 0.02),
        "sc_norm_w": 1.0 + nrm(ks[12], (DEPTH, SC_WIDTH), 0.02),
        "ssm_norm_w": 1.0 + nrm(ks[13], (DEPTH, SSM_WIDTH), 0.02),
        "w_out": nrm(ks[14], (DEPTH, MIX_WIDTH, D_MODEL), DEEPNORM_BETA * MIX_WIDTH ** -0.5),
        "ln1_g": 1.0 + nrm(ks[15], (DEPTH, D_MODEL), 0.02),
        "ln1_b": nrm(ks[16], (DEPTH, D_MODEL), 0.02),
        "w_query": nrm(ks[17], (DEPTH, D_MODEL, PEER_HEADS * PEER_DKEY), D_MODEL ** -0.5),
        "sub_keys1": nrm(ks[18], (DEPTH, PEER_HEADS, PEER_NKEYS, PEER_HALF), PEER_HALF ** -0.5),
        "sub_keys2": nrm(ks[19], (DEPTH, PEER_HEADS, PEER_NKEYS, PEER_HALF), PEER_HALF ** -0.5),
        "expert_u": nrm(ks[20], (DEPTH, PEER_EXPERTS, D_MODEL), D_MODEL ** -0.5),
        "expert_v": nrm(ks[21], (DEPTH, PEER_EXPERTS, D_MODEL), DEEPNORM_BETA),
        "ln2_g": 1.0 + nrm(ks[22], (DEPTH, D_MODEL), 0.02),
        "ln2_b": nrm(ks[23], (DEPTH, D_MODEL), 0.02),
    }

def reference(x, c, w_cond, b_cond, w_in, sc_conv_w, ssm_conv_w, ssm_conv_b, dt_bias, a_log,
              d_skip, sc_norm_w, ssm_norm_w, w_out, ln1_g, ln1_b, w_query, sub_keys1, sub_keys2,
              expert_u, expert_v, ln2_g, ln2_b):
    c_act = jax.nn.silu(c)
    for l in range(DEPTH):
        cond = (c_act @ w_cond[l] + b_cond[l])[:, None, :]
        shift1, scale1, gate1, shift2, scale2, gate2 = jnp.split(cond, 6, axis=-1)
        u1 = x * (1.0 + scale1) + shift1
        mix = hybrid_mixer(u1, w_in[l], sc_conv_w[l], ssm_conv_w[l], ssm_conv_b[l], dt_bias[l],
                           a_log[l], d_skip[l], sc_norm_w[l], ssm_norm_w[l], w_out[l])
        x = layer_norm(DEEPNORM_ALPHA * x + (1.0 + gate1) * mix, ln1_g[l], ln1_b[l])
        u2 = x * (1.0 + scale2) + shift2
        ffn = peer_ffn(u2, w_query[l], sub_keys1[l], sub_keys2[l], expert_u[l], expert_v[l])
        x = layer_norm(DEEPNORM_ALPHA * x + (1.0 + gate2) * ffn, ln2_g[l], ln2_b[l])
    return x


_drawn_inputs = setup_inputs


def setup_inputs(seed=0):
    import zlib

    import numpy as np

    out = dict(_drawn_inputs(seed))
    spreads = {}
    factors = {'d_skip': 2.868, 'ln2_g': 2.82, 'ln2_b': 2.909}
    for name, (base, spread) in spreads.items():
        noise = np.random.default_rng([zlib.crc32(name.encode()), seed]).standard_normal(out[name].shape)
        drawn = base * np.exp(spread * noise) if base else spread * noise
        out[name] = __import__('jax').numpy.asarray(drawn.astype(out[name].dtype))
    for name, factor in factors.items():
        out[name] = (out[name] * factor).astype(out[name].dtype)
    return out
```

```python
from contextlib import ExitStack

import concourse.bass as bass
from concourse import mybir

F32 = mybir.dt.float32
F32R = mybir.dt.float32r
U32 = mybir.dt.uint32
ALU = mybir.AluOpType
ACT = mybir.ActivationFunctionType
AX_X = mybir.AxisListType.X

P = 128
T, D = 512, 1024
TT, KD = T // P, D // P
HD = 64
SH = 16
NG = 2
HPG = SH // NG
GW = HPG * HD
KX = 12
NSC = 8
K_SC, K_SSM = 3, 4
HEADS, TOPK, NKEYS = 8, 16, 128
PICKS = HEADS * TOPK
LN_EPS, RMS_EPS = 1e-5, 1e-6
ALPHA = 2.0 ** 0.25
FLOOR = -3.0e38


def mixer(nc, a, x_tm, cond, ident, eps_tile):
    with ExitStack() as ctx:
        def sb(name, shape, dt=F32):
            return ctx.enter_context(nc.sbuf_tensor(name, shape, dt))

        def sem(name):
            return ctx.enter_context(nc.semaphore(name))

        bank = [ctx.enter_context(nc.psum_tensor(f"mix_bank{i}", [P, 512], F32)) for i in range(8)]
        u1T = sb("u1T", [P, KD, T])
        ring = sb("weight_ring", [P, 2, KD * 512])
        xbcT = sb("xbcT", [P, KX, T])
        ymixT = sb("ymixT", [P, 16, T])
        zs = sb("z_silu", [P, TT, D])
        decay = sb("decay", [P, SH, P])
        x_c = sb("x_chunk", [P, D])
        xdt = sb("x_dt", [P, D])
        xde = sb("x_dt_end", [P, D])
        state = sb("ssm_state", [P, 2, D])
        y = sb("y_chunk", [P, D])
        ysquare = sb("y_square", [P, D])
        btm = sb("b_tokens", [P, NG * P])
        cbm = sb("cb_masked", [P, NG, P])
        pad = sb("conv_in", [P, 2, T + K_SSM - 1])
        conv = sb("conv_out", [P, 2, T])
        csb = sb("sc_c_copy", [P, T])
        ysq = sb("sc_square", [P, 2, T])
        rs = sb("sc_rstd", [P, T])
        tri = sb("causal", [P, P])
        ones = sb("ones", [P, P])
        grp = sb("head_mean", [P, P])
        cact = sb("c_act", [P, 2, KD])
        bcond = sb("b_cond", [P, 48])
        scw = sb("sc_conv_w", [P, NSC, K_SC])
        ssw = sb("ssm_conv_w", [P, KX, K_SSM])
        ssb = sb("ssm_conv_b", [P, KX])
        scn = sb("sc_norm_w", [P, NSC])
        ssn = sb("ssm_norm_w", [P, NSC])
        wdt = sb("w_dt", [P, KD, SH])
        rows = sb("head_rows", [P, 3, SH])
        dtb = sb("dt_work", [P, 8, TT, SH])
        dt = sb("dt", [P, TT, SH])
        adt = sb("a_dt", [P, TT, SH])
        cums = sb("cums", [P, 3, TT, SH])
        ecums = sb("exp_cums", [P, 3, TT, SH])
        ssum = sb("y_square_sum", [P, 2, NG])

        w_loaded = [sem(f"w_loaded{i}") for i in range(2)]
        s = {n: sem("m_" + n) for n in (
            "xT_in", "x_in", "c_in", "par_in", "consts", "pads_zero", "cact", "cond_mm", "cond_out", "u1", "xbc_mm",
            "xbc_copied", "conv_done", "xbc_act", "dt_mm", "dt_x", "dt_exp", "dt_w", "dt_ln", "adt", "z_mm", "z_out",
            "cum_mm", "cums", "ecums", "c_mm", "h_mm", "b_mm", "c_copied", "h_used", "ysc", "ysq", "mean_mm",
            "mean_out", "rstd", "ysc_norm", "xtr_mm", "x_copied", "xdt", "xde", "xskip", "row_mm", "seg", "dexp",
            "btr_mm", "btm", "cb_mm", "cbm", "weights", "st_mm", "st_out", "yd_mm", "yo_mm", "yo_out", "y_gated",
            "ysum", "yln", "yrstd", "yn", "ytr_mm", "yT", "gate_mm", "gate", "out_mm", "out", "chain", "act_chain")}

        stream = [("cond", i) for i in range(4)] + [("xbc", i) for i in range(3)] + [("z", i) for i in range(2)]
        stream += [("sc", i) for i in range(NSC)] + [("cond", i) for i in range(4, 12)] + [("out", i) for i in range(4)]
        place = {w: n for n, w in enumerate(stream)}
        dram = {"cond": a["w_cond"], "xbc": a["w_xbc"], "z": a["w_z"], "sc": a["w_sc"], "out": a["w_out"]}

        def last_read(kind, i):
            return {"cond": (s["cond_mm"], i + 1), "xbc": (s["xbc_mm"], 4 * i + 4), "z": (s["z_mm"], 4 * i + 4),
                    "sc": (s["b_mm"], i + 1), "out": (s["out_mm"], i + 1)}[kind]

        def weights(pe, kind, i, cols=512):
            n = place[kind, i]
            pe.wait_ge(w_loaded[n % 2], 16 * (n // 2 + 1))
            return ring[:, n % 2, 0:KD * cols].rearrange("p (k n) -> p k n", k=KD)

        def cs(c):
            return slice(c * P, (c + 1) * P)

        def per_head(ap, c, g):
            return ap[:, c, g * HPG:(g + 1) * HPG].unsqueeze(2).to_broadcast([P, HPG, HD])

        def heads(ap):
            return ap.rearrange("p (h d) -> p h d", d=HD)

        with nc.Block() as block:
            @block.sync
            def _(sp):
                sp.dma_start(cact[:, 0, :], a["cT"]).then_inc(s["c_in"], 16)
                for n, (kind, i) in enumerate(stream):
                    if n >= 2:
                        sp.wait_ge(*last_read(*stream[n - 2]))
                    width = KD * (384 if kind == "sc" else 512)
                    sp.dma_start(ring[:, n % 2, 0:width], dram[kind][i].rearrange("p k n -> p (k n)"))\
                        .then_inc(w_loaded[n % 2], 16)

            @block.gpsimd
            def _(pool):
                pool.memset(ident[:, :], 0.0).then_inc(s["consts"], 1)
                pool.memset(tri[:, :], 1.0).then_inc(s["consts"], 1)
                pool.memset(ones[:, :], 1.0).then_inc(s["consts"], 1)
                pool.memset(grp[:, :], 0.0).then_inc(s["consts"], 1)
                pool.wait_ge(s["consts"], 4)
                pool.memset(grp[0:HD, 0:HD], 1.0 / HD).then_inc(s["consts"], 1)
                pool.wait_ge(s["consts"], 5)
                pool.memset(grp[HD:P, HD:P], 1.0 / HD).then_inc(s["consts"], 1)
                pool.wait_ge(s["consts"], 6)
                pool.affine_select(out=ident[:, :], in_=ident[:, :], compare_op=ALU.not_equal, fill=1.0, base=0,
                                   pattern=[[-1, P]], channel_multiplier=1).then_inc(s["consts"], 1)
                pool.affine_select(out=tri[:, :], in_=tri[:, :], compare_op=ALU.is_ge, fill=0.0, base=0,
                                   pattern=[[1, P]], channel_multiplier=-1).then_inc(s["consts"], 1)
                pool.wait_ge(s["ecums"], 1)
                pool.wait_ge(s["par_in"], 16 * 9)
                for c in range(TT):
                    pool.wait_ge(s["xdt"], 2 * c + 2)
                    if c:
                        pool.wait_ge(s["st_mm"], 2 * c)
                    for g in range(NG):
                        pool.tensor_tensor(heads(xde[:, g * GW:(g + 1) * GW]), heads(xdt[:, g * GW:(g + 1) * GW]),
                                           per_head(ecums[:, 2], c, g), ALU.mult).then_inc(s["xde"], 1)
                    pool.wait_ge(s["x_copied"], 2 * c + 2)
                    for g in range(NG):
                        pool.tensor_tensor(heads(x_c[:, g * GW:(g + 1) * GW]), heads(x_c[:, g * GW:(g + 1) * GW]),
                                           rows[:, 2, g * HPG:(g + 1) * HPG].unsqueeze(2).to_broadcast([P, HPG, HD]),
                                           ALU.mult).then_inc(s["xskip"], 1)

            @block.scalar
            def _(act):
                act.dma_start(u1T[:, :, :], a["xT"]).then_inc(s["xT_in"], 16)
                act.dma_start(bcond[:, :], a["b_condT"]).then_inc(s["par_in"], 16)
                act.dma_start(scw[:, :, :], a["sc_conv_wT"]).then_inc(s["par_in"], 16)
                act.dma_start(ssw[:, :, :], a["ssm_conv_wT"]).then_inc(s["par_in"], 16)
                act.dma_start(ssb[:, :], a["ssm_conv_bT"]).then_inc(s["par_in"], 16)
                act.dma_start(scn[:, :], a["sc_norm_wT"]).then_inc(s["par_in"], 16)
                act.dma_start(ssn[:, :], a["ssm_norm_wT"]).then_inc(s["par_in"], 16)
                for r, name in enumerate(("dt_bias", "a_log", "d_skip")):
                    act.dma_start(rows[:, r, :], a[name][0, :].partition_broadcast(P)).then_inc(s["par_in"], 16)
                act.dma_start(wdt[:, :, :], a["w_dt"]).then_inc(s["x_in"], 16)
                act.dma_start(x_tm[:, :, :], a["x"].rearrange("b (c p) d -> p (b c) d", p=P)).then_inc(s["x_in"], 16)
                act.wait_ge(s["c_in"], 16)
                act.activation(cact[:, 1, :], cact[:, 0, :], ACT.Silu).then_inc(s["cact"], 1)
                act.wait_ge(s["par_in"], 16 * 9)

                def conv_silu(m):
                    act.wait_ge(s["conv_done"], m + 1)
                    act.activation(xbcT[:, m, :], conv[:, m % 2, :], ACT.Silu, bias=ssb[:, m:m + 1])\
                        .then_inc(s["xbc_act"], 1)

                act.wait_ge(s["pads_zero"], 1)
                for m in range(KX):
                    act.wait_ge(s["xbc_mm"], m + 1)
                    if m >= 2:
                        act.wait_ge(s["conv_done"], m - 1)
                    act.activation(pad[:, m % 2, K_SSM - 1:], bank[m % 4][:, :], ACT.Copy).then_inc(s["xbc_copied"], 1)
                    if m:
                        conv_silu(m - 1)
                conv_silu(KX - 1)
                for n in range(NG * TT):
                    act.wait_ge(s["z_mm"], n + 1)
                    act.activation(zs[:, n % TT, (n // TT) * 512:(n // TT + 1) * 512], bank[n % 4][:, :], ACT.Silu)\
                        .then_inc(s["z_out"], 1)
                act.wait_ge(s["dt_x"], 2)
                act.activation(dtb[:, 2], dtb[:, 1], ACT.Exp).then_inc(s["dt_exp"], 1)
                act.activation(dtb[:, 7, 0, :], rows[:, 1, :], ACT.Exp).then_inc(s["dt_exp"], 1)
                act.wait_ge(s["dt_w"], 1)
                act.activation(dtb[:, 4], dtb[:, 3], ACT.Ln).then_inc(s["dt_ln"], 1)

                def sc_act(j):
                    act.wait_ge(s["c_mm"], j + 1)
                    if j:
                        act.wait_ge(s["h_used"], j)
                    act.activation(csb[:, :], bank[1][:, :], ACT.Copy).then_inc(s["c_copied"], 1)
                    act.wait_ge(s["ysc"], j + 1)
                    if j >= 2:
                        act.wait_ge(s["mean_mm"], j - 1)
                    act.activation(ysq[:, j % 2, :], ymixT[:, j, :], ACT.Square).then_inc(s["ysq"], 1)

                def sc_rstd(j):
                    act.wait_ge(s["mean_mm"], j + 1)
                    if j:
                        act.wait_ge(s["ysc_norm"], j)
                    act.activation(rs[:, :], bank[5][:, :], ACT.Ln, bias=eps_rms).then_inc(s["mean_out"], 1)
                    act.wait_ge(s["mean_out"], j + 1)
                    act.activation(rs[:, :], rs[:, :], ACT.Exp, scale=-0.5).then_inc(s["rstd"], 1)

                def part1(c):
                    for g in range(NG):
                        act.wait_ge(s["xtr_mm"], NG * c + g + 1)
                        if c:
                            act.wait_ge(s["y_gated"], c)
                        act.activation(x_c[:, g * 512:(g + 1) * 512], bank[3 + g][:, :], ACT.Copy)\
                            .then_inc(s["x_copied"], 1)
                    act.wait_ge(s["btr_mm"], c + 1)
                    act.wait_ge(s["cb_mm"], c + 1)
                    if c:
                        act.wait_ge(s["st_mm"], NG * c)
                    act.activation(btm[:, :], bank[5][:, 0:NG * P], ACT.Copy).then_inc(s["btm"], 1)
                    for q in range(4):
                        act.wait_ge(s["seg"], 4 * c + q + 1)
                        act.activation(decay[:, 4 * q:4 * q + 4, :], decay[:, 4 * q:4 * q + 4, :], ACT.Exp)\
                            .then_inc(s["dexp"], 1)

                def part2(c):
                    act.wait_ge(s["y_gated"], c + 1)
                    for g in range(NG):
                        if c or g:
                            act.wait_ge(s["ysum"], NG * c + g)
                        act.activation(ysquare[:, g * GW:(g + 1) * GW], y[:, g * GW:(g + 1) * GW], ACT.Square,
                                       accum_out=ssum[:, 0, g:g + 1]).then_inc(s["ysum"], 1)
                    act.wait_ge(s["ysum"], NG * c + NG)
                    if c:
                        act.wait_ge(s["yn"], c)
                    act.activation(ssum[:, 1, :], ssum[:, 0, :], ACT.Ln, scale=1.0 / GW, bias=eps_rms)\
                        .then_inc(s["yln"], 1)
                    act.wait_ge(s["yln"], c + 1)
                    act.activation(ssum[:, 1, :], ssum[:, 1, :], ACT.Exp, scale=-0.5).then_inc(s["yrstd"], 1)

                eps_rms = eps_tile[:, 0:1]
                for j in range(NSC):
                    sc_act(j)
                    if j == 0:
                        act.wait_ge(s["cums"], 2)
                        act.activation(ecums[:, :, :, :], cums[:, :, :, :], ACT.Exp).then_inc(s["ecums"], 1)
                    else:
                        sc_rstd(j - 1)
                    part1(j // 2) if j % 2 == 0 else part2(j // 2)
                sc_rstd(NSC - 1)
                for h in range(2):
                    act.wait_ge(s["gate_mm"], h + 1)
                    act.activation(state[:, 0, h * 512:(h + 1) * 512], bank[6 + h][:, :], ACT.Copy)\
                        .then_inc(s["gate"], 1)

            @block.vector
            def _(dve):
                links = [0]

                def link(ins):
                    links[0] += 1
                    ins.then_inc(s["chain"], 1)
                    dve.wait_ge(s["chain"], links[0])

                link(dve.memset(eps_tile[:, 0:1], RMS_EPS))
                link(dve.memset(eps_tile[:, 1:2], LN_EPS))
                dve.memset(pad[:, :, 0:K_SSM - 1], 0.0).then_inc(s["pads_zero"], 1)
                dve.wait_ge(s["par_in"], 16 * 9)
                dve.wait_ge(s["cond_mm"], 4)
                dve.tensor_tensor(cond[:, 0:16], bank[5][:, 0:16], bcond[:, 0:16], ALU.add).then_inc(s["cond_out"], 1)
                dve.wait_ge(s["cond_out"], 1)
                link(dve.tensor_scalar(cond[:, 8:16], cond[:, 8:16], 1.0, None, ALU.add))
                dve.wait_ge(s["xT_in"], 16)
                for k in range(KD):
                    dve.tensor_scalar(u1T[:, k, :], u1T[:, k, :], cond[:, 8 + k:9 + k], cond[:, k:k + 1],
                                      ALU.mult, ALU.add).then_inc(s["u1"], 1)
                for m in range(KX):
                    dve.wait_ge(s["xbc_copied"], m + 1)
                    if m >= 2:
                        dve.wait_ge(s["xbc_act"], m - 1)
                    o = conv[:, m % 2, :]
                    link(dve.tensor_scalar(o, pad[:, m % 2, 0:T], ssw[:, m, 0:1], None, ALU.mult))
                    for k in range(1, K_SSM):
                        ins = dve.scalar_tensor_tensor(out=o, in0=pad[:, m % 2, k:k + T], scalar=ssw[:, m, k:k + 1],
                                                       in1=o, op0=ALU.mult, op1=ALU.add)
                        if k < K_SSM - 1:
                            link(ins)
                    ins.then_inc(s["conv_done"], 1)
                dve.wait_ge(s["dt_mm"], 1)
                link(dve.tensor_tensor(dtb[:, 0], bank[4][:, 0:TT * SH].rearrange("p (c h) -> p c h", h=SH),
                                       rows[:, 0:1, :].to_broadcast([P, TT, SH]), ALU.add))
                dve.tensor_scalar(dtb[:, 5], dtb[:, 0], -1.0, None, ALU.mult).then_inc(s["dt_x"], 1)
                dve.wait_ge(s["dt_x"], 1)
                dve.tensor_tensor(dtb[:, 1], dtb[:, 0], dtb[:, 5], ALU.min).then_inc(s["dt_x"], 1)
                dve.wait_ge(s["dt_exp"], 2)
                dve.tensor_scalar(dtb[:, 3], dtb[:, 2], 1.0, None, ALU.add).then_inc(s["dt_w"], 1)
                dve.wait_ge(s["dt_w"], 1)
                link(dve.tensor_scalar(dtb[:, 5], dtb[:, 3], -1.0, None, ALU.add))
                link(dve.tensor_tensor(dtb[:, 6], dtb[:, 2], dtb[:, 5], ALU.subtract))
                link(dve.reciprocal(dtb[:, 5], dtb[:, 3]))
                link(dve.tensor_tensor(dtb[:, 6], dtb[:, 6], dtb[:, 5], ALU.mult))
                link(dve.tensor_scalar(dtb[:, 5], dtb[:, 0], 0.0, None, ALU.max))
                link(dve.tensor_tensor(dtb[:, 6], dtb[:, 6], dtb[:, 5], ALU.add))
                dve.wait_ge(s["dt_ln"], 1)
                link(dve.tensor_tensor(dt[:, :, :], dtb[:, 4], dtb[:, 6], ALU.add))
                link(dve.tensor_tensor(dtb[:, 5], dt[:, :, :], dtb[:, 7, 0:1, :].to_broadcast([P, TT, SH]), ALU.mult))
                dve.tensor_scalar(adt[:, :, :], dtb[:, 5], -1.0, None, ALU.mult).then_inc(s["adt"], 1)

                def sc_conv(j):
                    dve.wait_ge(s["h_mm"], j + 1)
                    dve.wait_ge(s["c_copied"], j + 1)
                    dve.tensor_tensor(pad[:, j % 2, K_SSM - 1:], bank[2][:, :], csb[:, :], ALU.mult)\
                        .then_inc(s["h_used"], 1)
                    dve.wait_ge(s["h_used"], j + 1)
                    o = conv[:, j % 2, :]
                    for k in range(K_SC):
                        src = pad[:, j % 2, K_SSM - K_SC + k:K_SSM - K_SC + k + T]
                        if k == 0:
                            link(dve.tensor_scalar(o, src, scw[:, j, 0:1], None, ALU.mult))
                        else:
                            link(dve.scalar_tensor_tensor(out=o, in0=src, scalar=scw[:, j, k:k + 1], in1=o,
                                                          op0=ALU.mult, op1=ALU.add))
                    dve.wait_ge(s["b_mm"], j + 1)
                    dve.tensor_tensor(ymixT[:, j, :], bank[0][:, :], o, ALU.mult).then_inc(s["ysc"], 1)

                def sc_norm(j):
                    dve.wait_ge(s["rstd"], j + 1)
                    dve.scalar_tensor_tensor(out=ymixT[:, j, :], in0=ymixT[:, j, :], scalar=scn[:, j:j + 1],
                                             in1=rs[:, :], op0=ALU.mult, op1=ALU.mult).then_inc(s["ysc_norm"], 1)

                def part1(c):
                    for g in range(NG):
                        dve.wait_ge(s["x_copied"], NG * c + g + 1)
                        if c:
                            dve.wait_ge(s["yd_mm"], NG * c)
                            dve.wait_ge(s["xde"], NG * c)
                        dve.tensor_tensor(heads(xdt[:, g * GW:(g + 1) * GW]), heads(x_c[:, g * GW:(g + 1) * GW]),
                                          per_head(dt, c, g), ALU.mult).then_inc(s["xdt"], 1)
                    for q in range(4):
                        dve.wait_ge(s["row_mm"], 4 * c + q + 1)
                        if c:
                            dve.wait_ge(s["yd_mm"], NG * c)
                        for r in range(4):
                            h = 4 * q + r
                            ins = dve.tensor_scalar(decay[:, h, :], bank[6 + q % 2][:, r * P:(r + 1) * P],
                                                    cums[:, 0, c, h:h + 1], 0.0, ALU.subtract, ALU.min)
                        ins.then_inc(s["seg"], 1)
                    dve.wait_ge(s["btm"], c + 1)
                    dve.tensor_tensor(cbm[:, :, :], bank[5][:, 256:512].rearrange("p (g l) -> p g l", g=NG),
                                      tri[:, :].unsqueeze(1).to_broadcast([P, NG, P]), ALU.mult)\
                        .then_inc(s["cbm"], 1)
                    dve.wait_ge(s["cbm"], c + 1)
                    for g in range(NG):
                        dve.wait_ge(s["dexp"], 4 * c + 2 * g + 2)
                        dg = decay[:, g * HPG:(g + 1) * HPG, :]
                        dve.tensor_tensor(dg, dg, cbm[:, g, :].unsqueeze(1).to_broadcast([P, HPG, P]), ALU.mult)\
                            .then_inc(s["weights"], 1)

                def state_update(c, g):
                    dve.wait_ge(s["st_mm"], NG * c + g + 1)
                    new = state[:, (c + 1) % 2, g * GW:(g + 1) * GW]
                    if c:
                        if c >= 2:
                            dve.wait_ge(s["yo_mm"], NG * (c - 1))
                        link(dve.tensor_tensor(heads(new), heads(state[:, c % 2, g * GW:(g + 1) * GW]),
                                               per_head(ecums[:, 1], c, g), ALU.mult))
                        dve.tensor_tensor(new, new, bank[5][:, :], ALU.add).then_inc(s["st_out"], 1)
                    else:
                        dve.tensor_copy(new, bank[5][:, :]).then_inc(s["st_out"], 1)
                    dve.wait_ge(s["st_out"], NG * c + g + 1)

                def part2(c):
                    if c < TT - 1:
                        state_update(c, 0)
                    if c:
                        dve.wait_ge(s["ytr_mm"], NG * c)
                        for g in range(NG):
                            dve.wait_ge(s["yo_mm"], NG * (c - 1) + g + 1)
                            dve.tensor_tensor(heads(y[:, g * GW:(g + 1) * GW]), heads(bank[6 + g][:, :]),
                                              per_head(ecums[:, 0], c, g), ALU.mult).then_inc(s["yo_out"], 1)
                        dve.wait_ge(s["yo_out"], NG * c)
                        for g in range(NG):
                            dve.wait_ge(s["yd_mm"], NG * c + g + 1)
                            yg = y[:, g * GW:(g + 1) * GW]
                            link(dve.tensor_tensor(yg, yg, bank[3 + g][:, :], ALU.add))
                    else:
                        for g in range(NG):
                            dve.wait_ge(s["yd_mm"], g + 1)
                            link(dve.tensor_copy(y[:, g * GW:(g + 1) * GW], bank[3 + g][:, :]))
                    dve.wait_ge(s["xskip"], NG * c + NG)
                    link(dve.tensor_tensor(y[:, :], y[:, :], x_c[:, :], ALU.add))
                    dve.tensor_tensor(y[:, :], y[:, :], zs[:, c, :], ALU.mult).then_inc(s["y_gated"], 1)
                    dve.wait_ge(s["y_gated"], c + 1)
                    if c < TT - 1:
                        state_update(c, 1)
                    dve.wait_ge(s["yrstd"], c + 1)
                    link(dve.tensor_scalar(y[:, 0:GW], y[:, 0:GW], ssum[:, 1, 0:1], None, ALU.mult))
                    dve.tensor_scalar(y[:, GW:D], y[:, GW:D], ssum[:, 1, 1:2], None, ALU.mult).then_inc(s["yn"], 1)

                def part3(c):
                    for g in range(NG):
                        dve.wait_ge(s["ytr_mm"], NG * c + g + 1)
                        dve.tensor_tensor(ymixT[:, 8 + 4 * g:12 + 4 * g, cs(c)],
                                          bank[3 + g][:, :].rearrange("p (j t) -> p j t", t=P),
                                          ssn[:, 4 * g:4 * g + 4].unsqueeze(2).to_broadcast([P, 4, P]), ALU.mult)\
                            .then_inc(s["yT"], 1)

                for j in range(NSC):
                    sc_conv(j)
                    if j == 0:
                        dve.wait_ge(s["cum_mm"], 2)
                        dve.tensor_copy(cums[:, 0:2, :, :], bank[7][:, 0:2 * TT * SH]
                                        .rearrange("p (r c h) -> p r c h", r=2, h=SH)).then_inc(s["cums"], 1)
                        dve.wait_ge(s["cums"], 1)
                        dve.tensor_tensor(cums[:, 2], cums[:, 1], cums[:, 0], ALU.subtract).then_inc(s["cums"], 1)
                        dve.wait_ge(s["ecums"], 1)
                    else:
                        sc_norm(j - 1)
                    if j % 2 == 0:
                        if j:
                            part3(j // 2 - 1)
                        part1(j // 2)
                    else:
                        part2(j // 2)
                sc_norm(NSC - 1)
                dve.wait_ge(s["cond_mm"], 12)
                dve.tensor_tensor(cond[:, 16:48], bank[5][:, 16:48], bcond[:, 16:48], ALU.add).then_inc(s["cond_out"], 1)
                dve.wait_ge(s["cond_out"], 2)
                for lo in (16, 32, 40):
                    dve.tensor_scalar(cond[:, lo:lo + 8], cond[:, lo:lo + 8], 1.0, None, ALU.add)\
                        .then_inc(s["cond_out"], 1)
                part3(TT - 1)
                dve.wait_ge(s["x_in"], 32)
                dve.wait_ge(s["gate"], 2)
                for h in range(2):
                    for c in range(TT):
                        dve.wait_ge(s["out_mm"], 2 * h + 2)
                        xs = x_tm[:, c, h * 512:(h + 1) * 512]
                        t = y[:, (c % 2) * 512:(c % 2 + 1) * 512]
                        link(dve.tensor_tensor(t, bank[4 * h + c][:, :], state[:, 0, h * 512:(h + 1) * 512], ALU.mult))
                        dve.scalar_tensor_tensor(out=xs, in0=xs, scalar=ALPHA, in1=t, op0=ALU.mult, op1=ALU.add)\
                            .then_inc(s["out"], 1)
                        dve.wait_ge(s["out"], 4 * h + c + 1)

            @block.tensor
            def _(pe):
                pe.wait_ge(s["cact"], 1)
                pe.wait_ge(s["consts"], 8)

                def cond_block(i):
                    w = weights(pe, "cond", i)
                    for j in range(4):
                        for k in range(KD):
                            ins = pe.matmul(bank[5][:, 4 * i + j:4 * i + j + 1], w[:, k, j * P:(j + 1) * P],
                                            cact[:, 1, k:k + 1], start=(k == 0), stop=(k == KD - 1))
                    ins.then_inc(s["cond_mm"], 1)

                for i in range(4):
                    cond_block(i)
                pe.wait_ge(s["u1"], KD)
                for m in range(KX):
                    w = weights(pe, "xbc", m // 4)
                    if m >= 4:
                        pe.wait_ge(s["xbc_copied"], m - 3)
                    for k in range(KD):
                        ins = pe.matmul(bank[m % 4][:, :], w[:, k, (m % 4) * P:(m % 4 + 1) * P], u1T[:, k, :],
                                        start=(k == 0), stop=(k == KD - 1))
                    ins.then_inc(s["xbc_mm"], 1)
                pe.wait_ge(s["x_in"], 32)
                for c in range(TT):
                    for k in range(KD):
                        ins = pe.matmul(bank[4][:, c * SH:(c + 1) * SH], u1T[:, k, cs(c)], wdt[:, k, :],
                                        start=(k == 0), stop=(k == KD - 1))
                ins.then_inc(s["dt_mm"], 1)
                for n in range(NG * TT):
                    w = weights(pe, "z", n // TT)
                    if n < 4:
                        pe.wait_ge(s["xbc_copied"], KX - 3 + n)
                    else:
                        pe.wait_ge(s["z_out"], n - 3)
                    for k in range(KD):
                        ins = pe.matmul(bank[n % 4][:, :], u1T[:, k, cs(n % TT)], w[:, k, :],
                                        start=(k == 0), stop=(k == KD - 1))
                    ins.then_inc(s["z_mm"], 1)
                pe.wait_ge(s["z_out"], NG * TT)

                def sc_products(j):
                    w = weights(pe, "sc", j, 384)
                    for r, b, free, done in ((1, 1, "c_copied", "c_mm"), (2, 2, "h_used", "h_mm"), (0, 0, "ysc", "b_mm")):
                        if j:
                            pe.wait_ge(s[free], j)
                        for k in range(KD):
                            ins = pe.matmul(bank[b][:, :], w[:, k, r * P:(r + 1) * P], u1T[:, k, :],
                                            start=(k == 0), stop=(k == KD - 1))
                        ins.then_inc(s[done], 1)

                def sc_mean(j):
                    pe.wait_ge(s["ysq"], j + 1)
                    if j % 2 == 0:
                        pe.wait_ge(s["btm"], j // 2 + 1)
                        pe.wait_ge(s["cbm"], j // 2 + 1)
                    elif j < NSC - 1:
                        pe.wait_ge(s["st_out"], NG * (j // 2) + NG)
                    pe.matmul(bank[5][:, :], grp[:, :], ysq[:, j % 2, :], start=True, stop=True)\
                        .then_inc(s["mean_mm"], 1)

                def part1(c):
                    for g in range(NG):
                        if c:
                            pe.wait_ge(s["yT"], NG * (c - 1) + g + 1)
                        for j in range(4):
                            ins = pe.transpose(bank[3 + g][:, j * P:(j + 1) * P], xbcT[:, 4 * g + j, cs(c)], ident[:, :])
                        ins.then_inc(s["xtr_mm"], 1)
                    for q in range(4):
                        if q >= 2:
                            pe.wait_ge(s["seg"], 4 * c + q - 1)
                        elif c >= 2:
                            pe.wait_ge(s["yo_out"], NG * (c - 1))
                        elif c == 1:
                            pe.wait_ge(s["seg"], 4)
                        for r in range(4):
                            ins = pe.matmul(bank[6 + q % 2][:, r * P:(r + 1) * P],
                                            adt[:, c, 4 * q + r:4 * q + r + 1].to_broadcast([P, P]), tri[:, :],
                                            start=True, stop=True)
                        ins.then_inc(s["row_mm"], 1)
                    if c:
                        pe.wait_ge(s["mean_out"], 2 * c)
                    for g in range(NG):
                        ins = pe.transpose(bank[5][:, g * P:(g + 1) * P], xbcT[:, 8 + g, cs(c)], ident[:, :])
                    ins.then_inc(s["btr_mm"], 1)
                    for g in range(NG):
                        ins = pe.matmul(bank[5][:, 256 + g * P:256 + (g + 1) * P], xbcT[:, 8 + g, cs(c)],
                                        xbcT[:, 10 + g, cs(c)], start=True, stop=True)
                    ins.then_inc(s["cb_mm"], 1)

                def chunk_state(c, g):
                    pe.matmul(bank[5][:, :], btm[:, g * P:(g + 1) * P], xde[:, g * GW:(g + 1) * GW],
                              start=True, stop=True).then_inc(s["st_mm"], 1)

                def part2(c):
                    pe.wait_ge(s["mean_out"], 2 * c + 1)
                    if c < TT - 1:
                        pe.wait_ge(s["xde"], NG * c + NG)
                        chunk_state(c, 0)
                    pe.wait_ge(s["xdt"], NG * c + NG)
                    pe.wait_ge(s["x_copied"], NG * c + NG)
                    for g in range(NG):
                        pe.wait_ge(s["weights"], NG * c + g + 1)
                        for r in range(HPG):
                            h = g * HPG + r
                            ins = pe.matmul(bank[3 + g][:, r * HD:(r + 1) * HD], decay[:, h, :],
                                            xdt[:, h * HD:(h + 1) * HD], start=True, stop=True)
                        ins.then_inc(s["yd_mm"], 1)
                    if c:
                        pe.wait_ge(s["seg"], 4 * c + 4)
                        for g in range(NG):
                            pe.wait_ge(s["st_out"], NG * (c - 1) + g + 1)
                            pe.matmul(bank[6 + g][:, :], xbcT[:, 10 + g, cs(c)], state[:, c % 2, g * GW:(g + 1) * GW],
                                      start=True, stop=True).then_inc(s["yo_mm"], 1)
                    if c < TT - 1:
                        pe.wait_ge(s["st_out"], NG * c + 1)
                        chunk_state(c, 1)

                def part3(c):
                    pe.wait_ge(s["yn"], c + 1)
                    for g in range(NG):
                        for j in range(4):
                            k = 4 * g + j
                            ins = pe.transpose(bank[3 + g][:, j * P:(j + 1) * P], y[:, k * P:(k + 1) * P], ident[:, :])
                        ins.then_inc(s["ytr_mm"], 1)

                for j in range(NSC):
                    sc_products(j)
                    if j == 0:
                        pe.wait_ge(s["adt"], 1)
                        for r, m in enumerate((tri, ones)):
                            pe.matmul(bank[7][:, r * TT * SH:(r + 1) * TT * SH], m[:, :],
                                      adt[:, :, :].rearrange("p c h -> p (c h)"), start=True, stop=True)\
                                .then_inc(s["cum_mm"], 1)
                        pe.wait_ge(s["cums"], 1)
                    else:
                        sc_mean(j - 1)
                    if j % 2 == 0:
                        if j:
                            part3(j // 2 - 1)
                        part1(j // 2)
                    else:
                        part2(j // 2)
                sc_mean(NSC - 1)
                pe.wait_ge(s["mean_out"], NSC)
                for i in range(4, 12):
                    cond_block(i)
                part3(TT - 1)
                pe.wait_ge(s["cond_out"], 5)
                pe.wait_ge(s["yo_out"], NG * (TT - 1))
                for m in range(KD):
                    ins = pe.matmul(bank[6 + m // 4][:, (m % 4) * P:(m % 4 + 1) * P],
                                    cond[:, 16 + m:17 + m].to_broadcast([P, P]), ident[:, :], start=True, stop=True)
                    if m % 4 == 3:
                        ins.then_inc(s["gate_mm"], 1)
                pe.wait_ge(s["gate"], 2)
                pe.wait_ge(s["ysc_norm"], NSC)
                pe.wait_ge(s["yT"], NG * TT)
                for h in range(2):
                    for kb in range(2):
                        w = weights(pe, "out", 2 * h + kb)
                        for c in range(TT):
                            for k in range(KD):
                                ins = pe.matmul(bank[4 * h + c][:, :], ymixT[:, 8 * kb + k, cs(c)], w[:, k, :],
                                                start=(kb == 0 and k == 0), stop=(kb == 1 and k == KD - 1))
                        ins.then_inc(s["out_mm"], 1)


def wait(eng, sem, value):
    if not (isinstance(value, int) and value <= 0):
        eng.wait_ge(sem, value)


UNROLL = 8
TOK = 8
GT = 32
QCH = 2 * HEADS
PLAIN = NKEYS - T // TOK


def router(nc, a, x_tm, cond, ident, eps_tile, h_dram, g_dram):
    with ExitStack() as ctx:
        def sb(name, shape, dt=F32):
            return ctx.enter_context(nc.sbuf_tensor(name, shape, dt))

        def sem(name):
            return ctx.enter_context(nc.semaphore(name))

        bank = [ctx.enter_context(nc.psum_tensor(f"rt_bank{i}", [P, 512], F32)) for i in range(8)]
        u2hi = sb("u2_hi", [P, KD, T], F32R)
        u2lo = sb("u2_lo", [P, KD, T], F32R)
        keys = sb("keys", [P, QCH, NKEYS])
        sc_all = sb("scores", [P, TT, QCH * NKEYS])
        raw = sb("u_raw", [P, 4, KD * P])
        whi = sb("u_hi", [P, 2, KD * P], F32R)
        wlo = sb("u_lo", [P, 2, KD * P], F32R)
        hout = sb("h_out", [P, 2, T])
        st = sb("search", [P, QCH * NKEYS])
        rp = sb("search_rest", [P, QCH * NKEYS])
        val = sb("top_values", [P, QCH, TOPK])
        idx = sb("top_index", [P, QCH, TOPK], U32)
        idf = sb("top_index_f", [P, QCH, TOPK])
        tv = sb("pair_values", [P, HEADS, TOPK])
        pos = sb("pair_index", [P, 3, PICKS], U32)
        pof = sb("pair_index_f", [P, 2, PICKS])
        pk = sb("picks", [P, 3, TT, PICKS])
        gsum = sb("gate_sums", [P, 2, TT * HEADS])
        pT = sb("picks_T", [P, 3, T])
        hotA = sb("one_hot_gate", [P, TOK, NKEYS])
        hotB = sb("one_hot", [P, TOK, NKEYS])
        iota = sb("iota", [P, NKEYS])
        lst = sb("ln_stats", [P, TT, 2, 6])
        lmv = sb("ln_mean_var", [P, TT, 2])
        lrs = sb("ln_rstd", [P, TT])
        with nc.sbuf_tensor("ln_rows", [P, 2, D], F32) as lnr, nc.sbuf_tensor("u2_plain", [P, 2, T], F32) as u2f:
            pass
        with nc.sbuf_tensor("queries_T", [P, QCH, T], F32) as qT:
            pass
        gst = sb("g_staging", [P, 2, NKEYS, GT])

        loaded = [sem(f"r_loaded{i}") for i in range(4)]
        h_saved = [sem(f"h_saved{i}") for i in range(2)]
        g_saved = [sem(f"g_saved{i}") for i in range(2)]
        s = {n: sem("r_" + n) for n in (
            "rows_in", "keys_in", "iota", "stats", "ln_ln", "ln_rstd", "x1", "tr_mm", "u2f", "hi_u2", "lo_u2", "hi", "lo",
            "h_mm", "h_act", "sc_mm", "sc_out", "shifted", "gexp", "gates", "pt_mm", "pT", "hot", "g_mm", "g_out",
            "ordered", "chain")}

        def chunk_dram(n):
            return a["w_query"][n] if isinstance(n, int) and n < QCH else a["u_T"][n - QCH]

        def each_chunk(eng, body):
            for n in range(QCH):
                body(n, 0, False)
            with eng.Fori(0, PLAIN // UNROLL) as r:
                for u in range(UNROLL):
                    body(r * UNROLL + (QCH + u), u, False)

        def g_chunks(eng, body):
            with eng.Fori(0, (NKEYS - PLAIN) // UNROLL) as r:
                for u in range(UNROLL):
                    body(r * UNROLL + (QCH + PLAIN + u), u, True)

        with nc.Block() as block:
            @block.sync
            def _(sp):
                for r, name in enumerate(("ln1_g", "ln1_b")):
                    sp.dma_start(lnr[:, r, :], a[name][0, :].partition_broadcast(P)).then_inc(s["rows_in"], 16)
                sp.dma_start(keys[:, :, :], a["keysT"]).then_inc(s["keys_in"], 16)

                def load(n, u, g):
                    slot = (n if isinstance(n, int) else u) % 4
                    wait(sp, s["lo"], n - 3)
                    sp.dma_start(raw[:, slot, :], chunk_dram(n).rearrange("p k e -> p (k e)"))\
                        .then_inc(loaded[slot], 16)

                each_chunk(sp, load)
                g_chunks(sp, load)

            @block.gpsimd
            def _(pool):
                pool.iota(iota[:, :], [[1, NKEYS]], base=0, channel_multiplier=0,
                          allow_small_or_imprecise_dtypes=True).then_inc(s["iota"], 1)

                def split_lo(n, u, g):
                    slot = (n if isinstance(n, int) else u) % 4
                    pool.wait_ge(s["hi"], n + 1)
                    wait(pool, s["h_mm"], n - 1)
                    pool.tensor_tensor(wlo[:, slot % 2, :], raw[:, slot, :], whi[:, slot % 2, :].bitcast(F32),
                                       ALU.subtract).then_inc(s["lo"], 1)

                each_chunk(pool, split_lo)
                g_chunks(pool, split_lo)

            @block.scalar
            def _(act):
                for c in range(TT):
                    act.wait_ge(s["stats"], c + 1)
                    act.activation(lrs[:, c:c + 1], lmv[:, c, 1:2], ACT.Ln, bias=eps_tile[:, 1:2])\
                        .then_inc(s["ln_ln"], 1)
                    act.wait_ge(s["ln_ln"], c + 1)
                    act.activation(lrs[:, c:c + 1], lrs[:, c:c + 1], ACT.Exp, scale=-0.5).then_inc(s["ln_rstd"], 1)
                for k in range(KD):
                    act.wait_ge(s["tr_mm"], k + 1)
                    wait(act, s["lo_u2"], k - 1)
                    act.activation(u2f[:, k % 2, :], bank[k % 2][:, :], ACT.Identity, scale=cond[:, 32 + k:33 + k],
                                   bias=cond[:, 24 + k:25 + k]).then_inc(s["u2f"], 1)
                    act.wait_ge(s["u2f"], k + 1)
                    act.activation(u2hi[:, k, :], u2f[:, k % 2, :], ACT.Copy).then_inc(s["hi_u2"], 1)

                def split_hi(n, u, g):
                    slot = (n if isinstance(n, int) else u) % 4
                    act.wait_ge(loaded[slot], (n // 4) * 16 + 16 if isinstance(n, int) else (n + (4 - slot)) * 4)
                    wait(act, s["h_mm"], n - 1)
                    act.activation(whi[:, slot % 2, :], raw[:, slot, :], ACT.Copy).then_inc(s["hi"], 1)

                def query_out(n):
                    act.wait_ge(s["h_mm"], n + 1)
                    if n == 0:
                        act.wait_ge(s["lo_u2"], KD)
                    act.activation(qT[:, n, :], bank[n % 2][:, :], ACT.Copy).then_inc(s["h_act"], 1)

                def gelu_out(n, u, g):
                    act.wait_ge(s["h_mm"], n + 1)
                    act.wait_ge(h_saved[u % 2], (n - (QCH + u % 2)) * 8 + 16)
                    act.activation(hout[:, u % 2, :], bank[u % 2][:, :], ACT.Gelu).then_inc(s["h_act"], 1)
                    act.wait_ge(s["h_act"], n + 1)
                    act.dma_start(h_dram[n - QCH], hout[:, u % 2, :]).then_inc(h_saved[u % 2], 16)
                    if g and u % 4 == 3:
                        act.wait_ge(s["g_out"], (n - (QCH + PLAIN)) * 2 + 2)
                        act.dma_start(g_dram[(n - (QCH + PLAIN + u)) // 4 + u // 4],
                                      gst[:, u // 4, :, :]).then_inc(g_saved[u // 4], 16)

                act.sem_inc(h_saved[0], 16)
                act.sem_inc(h_saved[1], 16)
                for n in range(QCH):
                    split_hi(n, 0, False)
                    if n:
                        query_out(n - 1)
                split_hi(QCH, 0, False)
                query_out(QCH - 1)
                for c in range(TT):
                    for b in range(4):
                        act.wait_ge(s["sc_mm"], 4 * c + b + 1)
                        act.activation(sc_all[:, c, b * 512:(b + 1) * 512], bank[2 + b][:, :], ACT.Copy)\
                            .then_inc(s["sc_out"], 1)
                with act.Fori(0, PLAIN // UNROLL) as r:
                    for u in range(UNROLL):
                        n = r * UNROLL + (QCH + u)
                        split_hi(n + 1, (u + 1) % UNROLL, False)
                        gelu_out(n, u, False)
                act.wait_ge(s["shifted"], TT)
                act.activation(pk[:, 2, :, :], pk[:, 2, :, :], ACT.Exp).then_inc(s["gexp"], 1)
                turns = (NKEYS - PLAIN) // UNROLL
                with act.Fori(0, turns - 1) as r:
                    for u in range(UNROLL):
                        n = r * UNROLL + (QCH + PLAIN + u)
                        split_hi(n + 1, (u + 1) % UNROLL, True)
                        gelu_out(n, u, True)
                for u in range(UNROLL):
                    n = (turns - 1) * UNROLL + QCH + PLAIN + u
                    if u < UNROLL - 1:
                        split_hi(n + 1, u + 1, True)
                    gelu_out(n, u, True)
                for i in range(2):
                    act.wait_ge(h_saved[i], 16 + 16 * (NKEYS // 2))
                    act.wait_ge(g_saved[i], 16 + 16 * (T // GT // 2))

            @block.vector
            def _(dve):
                links = [0]

                def link(ins, base=0):
                    links[0] += 1
                    ins.then_inc(s["chain"], 1)
                    dve.wait_ge(s["chain"], base + links[0])

                dve.wait_ge(s["rows_in"], 32)
                for c in range(TT):
                    for h in range(2):
                        ins = dve.bn_stats(lst[:, c, h, :], x_tm[:, c, h * 512:(h + 1) * 512])
                    link(ins)
                    dve.bn_aggr(lmv[:, c, :], lst[:, c, :, :]).then_inc(s["stats"], 1)
                for c in range(TT):
                    dve.wait_ge(s["ln_rstd"], c + 1)
                    xs = x_tm[:, c, :]
                    link(dve.tensor_scalar(xs, xs, lmv[:, c, 0:1], lrs[:, c:c + 1], ALU.subtract, ALU.mult))
                    link(dve.tensor_tensor(xs, xs, lnr[:, 0, :], ALU.mult))
                    dve.tensor_tensor(xs, xs, lnr[:, 1, :], ALU.add).then_inc(s["x1"], 1)
                for k in range(KD):
                    dve.wait_ge(s["hi_u2"], k + 1)
                    dve.tensor_tensor(u2lo[:, k, :], u2f[:, k % 2, :], u2hi[:, k, :].bitcast(F32), ALU.subtract)\
                        .then_inc(s["lo_u2"], 1)

                straight = links[0]
                s3 = st[:, :].rearrange("p (m n) -> p m n", n=NKEYS)
                r3 = rp[:, :].rearrange("p (m n) -> p m n", n=NKEYS)
                c3 = st[:, :].rearrange("p (h n) -> p h n", n=TOPK * TOPK)
                q3 = rp[:, :].rearrange("p (h n) -> p h n", n=TOPK * TOPK)
                e4 = st[:, :].rearrange("p (h k a) -> p h k a", h=HEADS, k=TOPK)
                v4 = val[:, :, :].rearrange("p (h w) k -> p h w k", w=2)
                i4 = idf[:, :, :].rearrange("p (h w) k -> p h w k", w=2)

                def top16(values, indices, source, rest, n):
                    def each(f):
                        for m in range(n):
                            ins = f(m)
                        step(ins)
                    dve.sem_inc(s["ordered"], 1)
                    each(lambda m: dve.max(values[:, m, 0:8], source[:, m, :]))
                    dve.sem_inc(s["ordered"], 1)
                    for m in range(n):
                        dve.max_index(indices[:, m, 0:8], values[:, m, 0:8], source[:, m, :])
                    each(lambda m: dve.match_replace(rest[:, m, :], values[:, m, 0:8], source[:, m, :], FLOOR))
                    dve.sem_inc(s["ordered"], 1)
                    each(lambda m: dve.max(values[:, m, 8:16], rest[:, m, :]))
                    dve.sem_inc(s["ordered"], 1)
                    each(lambda m: dve.max_index(indices[:, m, 8:16], values[:, m, 8:16], rest[:, m, :]))

                count = [0]
                STEPS = 1 + 4 + 1 + 1 + 4 + 1 + 1 + 3 * 2

                with dve.Fori(0, TT) as c:
                    def step(ins):
                        count[0] += 1
                        ins.then_inc(s["chain"], 1)
                        dve.wait_ge(s["chain"], c * STEPS + (straight + count[0]))

                    dve.wait_ge(s["sc_out"], c * 4 + 4)
                    step(dve.tensor_copy(st[:, :], sc_all[:, bass.ds(c, 1), :].rearrange("p c n -> p (c n)")))
                    top16(val, idx, s3, r3, QCH)
                    step(dve.tensor_copy(idf[:, :, :], idx[:, :, :]))
                    step(dve.tensor_tensor(e4, v4[:, :, 0, :].unsqueeze(3).to_broadcast([P, HEADS, TOPK, TOPK]),
                                           v4[:, :, 1, :].unsqueeze(2).to_broadcast([P, HEADS, TOPK, TOPK]), ALU.add))
                    p3 = pos[:, 0, :].rearrange("p (h k) -> p h k", k=TOPK)
                    top16(tv, p3, c3, q3, HEADS)
                    dve.tensor_scalar(pos[:, 1, :], pos[:, 0, :], 4, None, ALU.logical_shift_right)
                    step(dve.tensor_scalar(pos[:, 2, :], pos[:, 0, :], 15, None, ALU.bitwise_and))
                    step(dve.tensor_copy(pof[:, :, :], pos[:, 1:3, :]))
                    for w in range(2):
                        pw = pof[:, w, :].rearrange("p (h k) -> p h k", k=TOPK)
                        step(dve.tensor_tensor(
                            e4, pw.unsqueeze(3).to_broadcast([P, HEADS, TOPK, TOPK]),
                            iota[:, 0:TOPK].unsqueeze(1).unsqueeze(1).to_broadcast([P, HEADS, TOPK, TOPK]),
                            ALU.is_equal))
                        step(dve.tensor_tensor(
                            e4, e4, i4[:, :, w, :].unsqueeze(2).to_broadcast([P, HEADS, TOPK, TOPK]), ALU.mult))
                        step(dve.tensor_reduce(
                            pk[:, w, bass.ds(c, 1), :].rearrange("p c k -> p (c k)"),
                            st[:, :].rearrange("p (k a) -> p k a", a=TOPK), AX_X, ALU.add))
                    dve.tensor_tensor(
                        pk[:, 2, bass.ds(c, 1), :].rearrange("p c (h k) -> p (c h) k", k=TOPK), tv[:, :, :],
                        tv[:, :, 0:1].to_broadcast([P, HEADS, TOPK]), ALU.subtract).then_inc(s["shifted"], 1)
                    dve.wait_ge(s["shifted"], c + 1)
                assert count[0] == STEPS, count
                links[0] = straight + TT * STEPS
                g3 = pk[:, 2, :, :].rearrange("p c (h k) -> p (c h) k", k=TOPK)
                dve.wait_ge(s["gexp"], 1)
                link(dve.tensor_reduce(gsum[:, 0, :], g3, AX_X, ALU.add))
                link(dve.reciprocal(gsum[:, 1, :], gsum[:, 0, :]))
                dve.tensor_tensor(g3, g3, gsum[:, 1, :].unsqueeze(2).to_broadcast([P, TT * HEADS, TOPK]), ALU.mult)\
                    .then_inc(s["gates"], 1)
                for w in range(3):
                    dve.wait_ge(s["pt_mm"], w + 1)
                    dve.tensor_copy(pT[:, w, :], bank[2 + w][:, :]).then_inc(s["pT"], 1)
                dve.wait_ge(s["pT"], 3)
                dve.wait_ge(s["iota"], 1)

                for i in range(2):
                    dve.sem_inc(g_saved[i], 16)
                def gates_of(n, u, g):
                    base = (n - (QCH + PLAIN)) * TOK
                    for t in range(TOK):
                        dve.tensor_scalar(hotB[:, t, :], iota[:, :], pT[:, 1, bass.ds(base + t, 1)], None, ALU.is_equal)
                        ins = dve.tensor_scalar(hotA[:, t, :], iota[:, :], pT[:, 0, bass.ds(base + t, 1)],
                                                pT[:, 2, bass.ds(base + t, 1)], ALU.is_equal, ALU.mult)
                    ins.then_inc(s["hot"], 1)
                    for b in range(2):
                        dve.wait_ge(s["g_mm"], (n - (QCH + PLAIN)) * 2 + (b + 1))
                        if u % 4 == 0 and b == 0:
                            dve.wait_ge(g_saved[u // 4], (n - (QCH + PLAIN + u)) * 2 + 16)
                        col = (u % 4) * TOK + 4 * b
                        dve.tensor_copy(gst[:, u // 4, :, col:col + 4],
                                        bank[6 + b][:, :].rearrange("p (t i) -> p i t", t=4)).then_inc(s["g_out"], 1)

                g_chunks(dve, gates_of)

            @block.tensor
            def _(pe):
                pe.wait_ge(s["x1"], TT)
                for k in range(KD):
                    wait(pe, s["u2f"], k - 1)
                    for c in range(TT):
                        ins = pe.transpose(bank[k % 2][:, c * P:(c + 1) * P], x_tm[:, c, k * P:(k + 1) * P], ident[:, :])
                    ins.then_inc(s["tr_mm"], 1)
                pe.wait_ge(s["lo_u2"], KD)
                pe.wait_ge(s["u2f"], KD)

                def products(n, u, g):
                    slot = (n if isinstance(n, int) else u) % 2
                    pe.wait_ge(s["lo"], n + 1)
                    wait(pe, s["h_act"], n - 1)
                    for k in range(KD):
                        ks = slice(k * P, (k + 1) * P)
                        pe.matmul(bank[slot][:, :], whi[:, slot, ks], u2hi[:, k, :], start=(k == 0), stop=False)
                        pe.matmul(bank[slot][:, :], whi[:, slot, ks], u2lo[:, k, :], start=False, stop=False)
                        ins = pe.matmul(bank[slot][:, :], wlo[:, slot, ks], u2hi[:, k, :], start=False,
                                        stop=(k == KD - 1))
                    ins.then_inc(s["h_mm"], 1)
                    if g:
                        pe.wait_ge(s["hot"], n - (QCH + PLAIN - 1))
                        for t in range(TOK):
                            ins = pe.matmul(bank[6 + t // 4][:, (t % 4) * P:(t % 4 + 1) * P], hotB[:, t, :],
                                            hotA[:, t, :], start=True, stop=True)
                            if t % 4 == 3:
                                ins.then_inc(s["g_mm"], 1)

                for n in range(QCH):
                    products(n, 0, False)
                pe.wait_ge(s["keys_in"], 16)
                pe.wait_ge(s["h_act"], QCH)
                for c in range(TT):
                    for b in range(4):
                        wait(pe, s["sc_out"], 4 * (c - 1) + b + 1)
                        for r in range(4):
                            m = 4 * b + r
                            ins = pe.matmul(bank[2 + b][:, r * P:(r + 1) * P], qT[:, m, c * P:(c + 1) * P],
                                            keys[:, m, :], start=True, stop=True)
                        ins.then_inc(s["sc_mm"], 1)
                with pe.Fori(0, PLAIN // UNROLL) as r:
                    for u in range(UNROLL):
                        products(r * UNROLL + (QCH + u), u, False)
                pe.wait_ge(s["gates"], 1)
                pe.wait_ge(s["sc_out"], 4 * TT)
                for w in range(3):
                    for c in range(TT):
                        ins = pe.transpose(bank[2 + w][:, c * P:(c + 1) * P], pk[:, w, c, :], ident[:, :])
                    ins.then_inc(s["pt_mm"], 1)
                g_chunks(pe, products)


def experts(nc, a, x_tm, cond, ident, eps_tile, h_dram, g_dram, out):
    with ExitStack() as ctx:
        def sb(name, shape, dt=F32):
            return ctx.enter_context(nc.sbuf_tensor(name, shape, dt))

        def sem(name):
            return ctx.enter_context(nc.semaphore(name))

        bank = [ctx.enter_context(nc.psum_tensor(f"ex_bank{i}", [P, 512], F32)) for i in range(8)]
        vraw = sb("v_raw", [P, 4, D])
        vhi = sb("v_hi", [P, 2, D], F32R)
        vlo = sb("v_lo", [P, 2, D], F32R)
        hin = sb("h_in", [P, 2, 4, T])
        gin = sb("g_in", [P, 2, T // GT, 4, GT])
        act_f = sb("act", [P, 2, T])
        ahi = sb("act_hi", [P, 2, T], F32R)
        alo = sb("act_lo", [P, 2, T], F32R)
        zero = sb("zero", [P, 512], mybir.dt.bfloat16)
        gate = sb("gate2_row", [P, D])
        lnr = sb("ln2_rows", [P, 2, D])
        t = sb("scratch", [P, 2, D])
        lst = sb("ln2_stats", [P, TT, 2, 6])
        lmv = sb("ln2_mean_var", [P, TT, 2])
        lrs = sb("ln2_rstd", [P, TT])
        v_in = [sem(f"v_in{i}") for i in range(4)]
        h_in = [sem(f"h_in{i}") for i in range(2)]
        g_in = [sem(f"g_in{i}") for i in range(2)]
        s = {n: sem("e_" + n) for n in (
            "zero", "rows_in", "v_hi", "v_lo", "act", "a_hi", "a_lo", "mm", "gate_mm", "gate", "end", "stats", "ln_ln",
            "ln_rstd", "y", "stored", "chain")}

        def each(eng, body):
            for u in range(UNROLL):
                body(u, u)
            with eng.Fori(1, NKEYS // UNROLL) as r:
                for u in range(UNROLL):
                    body(r * UNROLL + u, u)

        with nc.Block() as block:
            @block.sync
            def _(sp):
                def load(n, u):
                    if u % 4 == 0:
                        wait(sp, s["act"], n - 4)
                        half = u // 4
                        sp.dma_start(hin[:, half, :, :], h_dram[bass.ds(n, 4)].rearrange("i p t -> p i t"))\
                            .then_inc(h_in[half], 16)
                        sp.dma_start(gin[:, half, :, :, :],
                                     g_dram[:, :, bass.ds(n, 4), :].rearrange("b p i t -> p b i t"))\
                            .then_inc(g_in[half], 16)
                    wait(sp, s["v_lo"], n - 3)
                    sp.dma_start(vraw[:, u % 4, :], a["v"][n]).then_inc(v_in[u % 4], 16)

                each(sp, load)
                for r, name in enumerate(("ln2_g", "ln2_b")):
                    sp.dma_start(lnr[:, r, :], a[name][0, :].partition_broadcast(P)).then_inc(s["rows_in"], 16)
                for c in range(TT):
                    sp.wait_ge(s["y"], c + 1)
                    sp.dma_start(out[0, c * P:(c + 1) * P, :], x_tm[:, c, :]).then_inc(s["stored"], 16)
                sp.wait_ge(s["stored"], 16 * TT)

            @block.gpsimd
            def _(pool):
                pool.memset(zero[:, :], 0.0).then_inc(s["zero"], 1)

                def split_v_lo(n, u):
                    pool.wait_ge(s["v_hi"], n + 1)
                    wait(pool, s["mm"], n - 1)
                    pool.tensor_tensor(vlo[:, u % 2, :], vraw[:, u % 4, :], vhi[:, u % 2, :].bitcast(F32),
                                       ALU.subtract).then_inc(s["v_lo"], 1)

                each(pool, split_v_lo)

            @block.scalar
            def _(act):
                for h in range(2):
                    act.wait_ge(s["gate_mm"], h + 1)
                    act.activation(gate[:, h * 512:(h + 1) * 512], bank[h][:, :], ACT.Copy).then_inc(s["gate"], 1)

                def split_hi(n, u):
                    act.wait_ge(v_in[u % 4], (n - u + 4 * (u // 4 + 1)) * 4)
                    wait(act, s["mm"], n - 1)
                    act.activation(vhi[:, u % 2, :], vraw[:, u % 4, :], ACT.Copy).then_inc(s["v_hi"], 1)
                    act.wait_ge(s["act"], n + 1)
                    act.activation(ahi[:, u % 2, :], act_f[:, u % 2, :], ACT.Copy).then_inc(s["a_hi"], 1)

                each(act, split_hi)
                for c in range(TT):
                    act.wait_ge(s["stats"], c + 1)
                    act.activation(lrs[:, c:c + 1], lmv[:, c, 1:2], ACT.Ln, bias=eps_tile[:, 1:2])\
                        .then_inc(s["ln_ln"], 1)
                    act.wait_ge(s["ln_ln"], c + 1)
                    act.activation(lrs[:, c:c + 1], lrs[:, c:c + 1], ACT.Exp, scale=-0.5).then_inc(s["ln_rstd"], 1)

            @block.vector
            def _(dve):
                def gated(n, u):
                    half, i = u // 4, u % 4
                    if i == 0:
                        dve.wait_ge(h_in[half], n * 2 + (16 - 2 * u))
                        dve.wait_ge(g_in[half], n * 2 + (16 - 2 * u))
                    dve.tensor_tensor(act_f[:, u % 2, :].rearrange("p (b t) -> p b t", t=GT),
                                      hin[:, half, i, :].rearrange("p (b t) -> p b t", t=GT),
                                      gin[:, half, :, i, :], ALU.mult).then_inc(s["act"], 1)
                    dve.wait_ge(s["a_hi"], n + 1)
                    wait(dve, s["mm"], n - 1)
                    dve.tensor_tensor(alo[:, u % 2, :], act_f[:, u % 2, :], ahi[:, u % 2, :].bitcast(F32),
                                      ALU.subtract).then_inc(s["a_lo"], 1)
                    dve.wait_ge(s["a_lo"], n + 1)

                each(dve, gated)
                links = [0]

                def link(ins):
                    links[0] += 1
                    ins.then_inc(s["chain"], 1)
                    dve.wait_ge(s["chain"], links[0])

                dve.wait_ge(s["end"], 1)
                dve.wait_ge(s["gate"], 2)
                dve.wait_ge(s["rows_in"], 32)
                for c in range(TT):
                    xs = x_tm[:, c, :]
                    for h in range(2):
                        hs = slice(h * 512, (h + 1) * 512)
                        link(dve.tensor_tensor(t[:, c % 2, hs], bank[2 * c + h][:, :], gate[:, hs], ALU.mult))
                    link(dve.scalar_tensor_tensor(out=xs, in0=xs, scalar=ALPHA, in1=t[:, c % 2, :], op0=ALU.mult,
                                                  op1=ALU.add))
                    for h in range(2):
                        ins = dve.bn_stats(lst[:, c, h, :], x_tm[:, c, h * 512:(h + 1) * 512])
                    link(ins)
                    dve.bn_aggr(lmv[:, c, :], lst[:, c, :, :]).then_inc(s["stats"], 1)
                    dve.wait_ge(s["ln_rstd"], c + 1)
                    link(dve.tensor_scalar(xs, xs, lmv[:, c, 0:1], lrs[:, c:c + 1], ALU.subtract, ALU.mult))
                    link(dve.tensor_tensor(xs, xs, lnr[:, 0, :], ALU.mult))
                    dve.tensor_tensor(xs, xs, lnr[:, 1, :], ALU.add).then_inc(s["y"], 1)

            @block.tensor
            def _(pe):
                for m in range(KD):
                    ins = pe.matmul(bank[m // 4][:, (m % 4) * P:(m % 4 + 1) * P],
                                    cond[:, 40 + m:41 + m].to_broadcast([P, P]), ident[:, :], start=True, stop=True)
                    if m % 4 == 3:
                        ins.then_inc(s["gate_mm"], 1)
                pe.wait_ge(s["zero"], 1)
                pe.wait_ge(s["gate"], 2)
                for b in range(8):
                    pe.matmul(bank[b][:, :], zero[:, 0:P], zero[:, :], start=True, stop=False)

                def products(n, u):
                    w = u % 2
                    pe.wait_ge(s["v_lo"], n + 1)
                    pe.wait_ge(s["a_lo"], n + 1)
                    for c in range(TT):
                        ts = slice(c * P, (c + 1) * P)
                        for left, right in ((ahi, vhi), (ahi, vlo), (alo, vhi)):
                            for h in range(2):
                                ins = pe.matmul(bank[2 * c + h][:, :], left[:, w, ts],
                                                right[:, w, h * 512:(h + 1) * 512], start=False, stop=False)
                    ins.then_inc(s["mm"], 1)

                each(pe, products)
                for b in range(8):
                    ins = pe.matmul(bank[b][:, :], zero[:, 0:P], zero[:, :], start=False, stop=True)
                ins.then_inc(s["end"], 1)


def layer(nc, a, out):
    h_dram = nc.dram_tensor("h_dram", (NKEYS, NKEYS, T), F32, kind="Internal").ap()
    g_dram = nc.dram_tensor("g_dram", (T // GT, NKEYS, NKEYS, GT), F32, kind="Internal").ap()
    with ExitStack() as ctx:
        def sb(name, shape):
            return ctx.enter_context(nc.sbuf_tensor(name, shape, F32))

        x_tm, cond = sb("x_tokens", [P, TT, D]), sb("cond", [P, 48])
        ident, eps_tile = sb("identity", [P, P]), sb("eps", [P, 2])
        mixer(nc, a, x_tm, cond, ident, eps_tile)
        router(nc, a, x_tm, cond, ident, eps_tile, h_dram, g_dram)
        experts(nc, a, x_tm, cond, ident, eps_tile, h_dram, g_dram, out)


def laid_out(x, c, w_cond, b_cond, w_in, sc_conv_w, ssm_conv_w, ssm_conv_b, dt_bias, a_log, d_skip, sc_norm_w,
             ssm_norm_w, w_out, ln1_g, ln1_b, w_query, sub_keys1, sub_keys2, expert_u, expert_v, ln2_g, ln2_b):
    import numpy as np

    def blocks(w, n):
        return w.reshape(KD, P, n, -1).transpose(2, 1, 0, 3)

    def columns(v):
        return v.reshape(-1, P).T

    w = w_in[0]
    keys = np.stack([sub_keys1[0], sub_keys2[0]], axis=1).reshape(2 * HEADS, NKEYS, P)
    arrays = {
        "x": x, "xT": x[0].T.reshape(KD, P, T).transpose(1, 0, 2), "cT": columns(c[0]),
        "w_cond": blocks(w_cond[0], 12), "b_condT": columns(b_cond[0]),
        "w_sc": w[:, 0:3 * D].reshape(KD, P, 3, NSC, P).transpose(3, 1, 0, 2, 4).reshape(NSC, P, KD, 3 * P),
        "w_z": blocks(w[:, 3 * D:4 * D], 2), "w_xbc": blocks(w[:, 4 * D:4 * D + KX * P], 3),
        "w_dt": w[:, 4 * D + KX * P:].reshape(KD, P, SH).transpose(1, 0, 2),
        "sc_conv_wT": sc_conv_w[0].reshape(K_SC, NSC, P).transpose(2, 1, 0),
        "ssm_conv_wT": ssm_conv_w[0].reshape(K_SSM, KX, P).transpose(2, 1, 0),
        "ssm_conv_bT": columns(ssm_conv_b[0]), "sc_norm_wT": columns(sc_norm_w[0]),
        "ssm_norm_wT": columns(ssm_norm_w[0]), "dt_bias": dt_bias, "a_log": a_log, "d_skip": d_skip,
        "w_out": w_out[0].reshape(2, KD, P, 2, 512).transpose(3, 0, 2, 1, 4).reshape(4, P, KD, 512),
        "ln1_g": ln1_g, "ln1_b": ln1_b, "ln2_g": ln2_g, "ln2_b": ln2_b,
        "w_query": blocks(w_query[0], 2 * HEADS), "keysT": keys.transpose(2, 0, 1),
        "u_T": expert_u[0].reshape(NKEYS, NKEYS, KD, P).transpose(0, 3, 2, 1), "v": expert_v[0].reshape(NKEYS, NKEYS, D),
    }
    return {k: np.ascontiguousarray(v) for k, v in arrays.items()}


def kernel(**inputs):
    import numpy as np
    import concourse.bacc as bacc
    from concourse.bass_utils import run_bass_kernel_spmd

    arrays = laid_out(**{k: np.asarray(v) for k, v in inputs.items()})
    nc = bacc.Bacc("TRN2", target_bir_lowering=False, num_devices=1)
    a = {n: nc.dram_tensor("in_" + n, v.shape, F32, kind="ExternalInput").ap() for n, v in arrays.items()}
    out = nc.dram_tensor("out", (1, T, D), F32, kind="ExternalOutput").ap()
    layer(nc, a, out)
    r = run_bass_kernel_spmd(nc, [{"in_" + n: v for n, v in arrays.items()}], core_ids=[0])
    return r.results[0]["out"]
```

```python
from contextlib import ExitStack

import concourse.bass as bass
from concourse import mybir

F32 = mybir.dt.float32
F32R = mybir.dt.float32r
U32 = mybir.dt.uint32
ALU = mybir.AluOpType
ACT = mybir.ActivationFunctionType
AX_X = mybir.AxisListType.X

P = 128
T, D = 512, 1024
TT, KD = T // P, D // P
HD = 64
SH = 16
NG = 2
HPG = SH // NG
GW = HPG * HD
KX = 12
NSC = 8
K_SC, K_SSM = 3, 4
HEADS, TOPK, NKEYS = 8, 16, 128
PICKS = HEADS * TOPK
LN_EPS, RMS_EPS = 1e-5, 1e-6
ALPHA = 2.0 ** 0.25
FLOOR = -3.0e38


def mixer(nc, a, x_tm, cond, ident, eps_tile):
    with ExitStack() as ctx:
        def sb(name, shape, dt=F32):
            return ctx.enter_context(nc.sbuf_tensor(name, shape, dt))

        def sem(name):
            return ctx.enter_context(nc.semaphore(name))

        bank = [ctx.enter_context(nc.psum_tensor(f"mix_bank{i}", [P, 512], F32)) for i in range(8)]
        u1hi = sb("u1_hi", [P, KD, T], F32R)
        u1lo = sb("u1_lo", [P, KD, T], F32R)
        raw = sb("w_raw", [P, 3, D])
        whi = sb("w_hi", [P, 2, D], F32R)
        wlo = sb("w_lo", [P, 2, D], F32R)
        craw = sb("w_cond_raw", [P, 2, D])
        csum = sb("cond_sum", [P, 2, P])
        xbcT = sb("xbcT", [P, KX, T])
        ymixT = sb("ymixT", [P, 16, T])
        zs = sb("z_silu", [P, TT, D])
        x_c = sb("x_chunk", [P, D])
        xdt = sb("x_dt", [P, D])
        xde = sb("x_dt_end", [P, D])
        state = sb("ssm_state", [P, D])
        y = sb("y_chunk", [P, D])
        btm = sb("b_tokens", [P, NG * P])
        cbm = sb("cb_masked", [P, NG, P])
        pad = sb("conv_in", [P, 2, T + K_SSM - 1])
        conv = sb("conv_out", [P, 2, T])
        csb = sb("sc_c_copy", [P, T])
        ysq = sb("sc_square", [P, T])
        rs = sb("sc_rstd", [P, T])
        tri = sb("causal", [P, P])
        ones = sb("ones", [P, P])
        grp = sb("head_mean", [P, P])
        cact = sb("c_act", [P, 2, KD])
        bcond = sb("b_cond", [P, 48])
        scw = sb("sc_conv_w", [P, NSC, K_SC])
        ssw = sb("ssm_conv_w", [P, KX, K_SSM])
        ssb = sb("ssm_conv_b", [P, KX])
        scn = sb("sc_norm_w", [P, NSC])
        ssn = sb("ssm_norm_w", [P, NSC])
        wdt = sb("w_dt", [P, KD, SH])
        wdthi = sb("w_dt_hi", [P, KD, SH], F32R)
        wdtlo = sb("w_dt_lo", [P, KD, SH], F32R)
        rows = sb("head_rows", [P, 3, SH])
        dtb = y[:, 0:8 * TT * SH].rearrange("p (r c h) -> p r c h", c=TT, h=SH)
        dt = sb("dt", [P, TT, SH])
        adt = sb("a_dt", [P, TT, SH])
        cums = sb("cums", [P, 3, TT, SH])
        ecums = sb("exp_cums", [P, 3, TT, SH])
        ssum = sb("y_square_sum", [P, 2, NG])
        with nc.sbuf_tensor("decay", [P, SH, P], F32) as decay:
            pass
        yhi = sb("ymix_hi", [P, 2, T], F32R)
        ylo = sb("ymix_lo", [P, 2, T], F32R)
        xT = x_tm[:, :, :].rearrange("p c d -> p (c d)").rearrange("p (k t) -> p k t", t=T)

        loaded = [sem(f"w_loaded{i}") for i in range(3)]
        c_loaded = [sem(f"cond_loaded{i}") for i in range(2)]
        s = {n: sem("m_" + n) for n in (
            "xT_in", "x_in", "wdt_in", "c_in", "par_in", "consts", "pads_zero", "cact", "cond_sum", "cond_mm",
            "cond_out", "u1", "u1hi", "u1lo", "hi", "lo", "unit", "wdt_hi", "wdt_lo", "xbc_copied", "conv_done",
            "xbc_act", "dt_mm", "dt_x", "dt_exp", "dt_w", "dt_ln", "adt", "z_out", "cum_mm", "cums", "ecums",
            "c_copied", "h_used", "ysc", "ysq", "mean_mm", "mean_out", "rstd", "ysc_norm", "xtr_mm", "x_copied",
            "xdt", "xde", "xskip", "row_mm", "seg", "dexp", "cb_mm", "btm", "cbm", "weights", "st_mm", "st_out",
            "yd_mm", "yo_mm", "yo_out", "y_gated", "ysum", "yln", "yrstd", "yn", "ytr_mm", "yT", "gate_mm", "gate",
            "yhi", "ylo", "tile_mm", "out", "chain")}

        XBC0, Z0, SC0 = 0, KX, KX + NG * 4
        OUT0 = SC0 + 3 * NSC
        UNITS = OUT0 + 16
        CA, CB = 16, 32

        def unit_dram(n):
            if n < Z0:
                return a["w_xbc"][n]
            if n < SC0:
                return a["w_z"][n - Z0]
            if n < OUT0:
                return a["w_sc"][n - SC0]
            return a["w_out"][n - OUT0]

        def cond_units_at(n):
            if n < KX:
                return range(CA + n, CA + n + 1)
            first = CA + KX + (n - KX) * 20 // 8
            return range(first, CA + KX + (n - KX + 1) * 20 // 8)

        def cs(c):
            return slice(c * P, (c + 1) * P)

        def per_head(ap, c, g):
            return ap[:, c, g * HPG:(g + 1) * HPG].unsqueeze(2).to_broadcast([P, HPG, HD])

        def heads(ap):
            return ap.rearrange("p (h d) -> p h d", d=HD)

        with nc.Block() as block:
            @block.sync
            def _(sp):
                sp.dma_start(cact[:, 0, :], a["cT"]).then_inc(s["c_in"], 16)

                def load_cond(i):
                    if i >= 2:
                        sp.wait_ge(s["cond_sum"], i - 1)
                    sp.dma_start(craw[:, i % 2, :], a["w_cond"][i].rearrange("p k n -> p (k n)"))\
                        .then_inc(c_loaded[i % 2], 16)

                for i in range(CA):
                    load_cond(i)
                    if i == 0:
                        sp.dma_start(xT, a["xT"]).then_inc(s["xT_in"], 16)
                for n in range(UNITS):
                    if n >= 3:
                        sp.wait_ge(s["lo"], n - 2)
                    sp.dma_start(raw[:, n % 3, :], unit_dram(n).rearrange("p k n -> p (k n)"))\
                        .then_inc(loaded[n % 3], 16)
                    if n < SC0:
                        for i in cond_units_at(n):
                            load_cond(i)
                    if n == SC0:
                        sp.wait_ge(s["u1lo"], KD)
                        sp.dma_start(x_tm[:, :, :], a["x"].rearrange("b (c p) d -> p (b c) d", p=P))\
                            .then_inc(s["x_in"], 16)

            @block.gpsimd
            def _(pool):
                pool.memset(ident[:, :], 0.0).then_inc(s["consts"], 1)
                pool.memset(tri[:, :], 1.0).then_inc(s["consts"], 1)
                pool.memset(ones[:, :], 1.0).then_inc(s["consts"], 1)
                pool.memset(grp[:, :], 0.0).then_inc(s["consts"], 1)
                pool.wait_ge(s["consts"], 4)
                pool.memset(grp[0:HD, 0:HD], 1.0 / HD).then_inc(s["consts"], 1)
                pool.wait_ge(s["consts"], 5)
                pool.memset(grp[HD:P, HD:P], 1.0 / HD).then_inc(s["consts"], 1)
                pool.wait_ge(s["consts"], 6)
                pool.affine_select(out=ident[:, :], in_=ident[:, :], compare_op=ALU.not_equal, fill=1.0, base=0,
                                   pattern=[[-1, P]], channel_multiplier=1).then_inc(s["consts"], 1)
                pool.affine_select(out=tri[:, :], in_=tri[:, :], compare_op=ALU.is_ge, fill=0.0, base=0,
                                   pattern=[[1, P]], channel_multiplier=-1).then_inc(s["consts"], 1)
                pool.wait_ge(s["wdt_hi"], 1)
                pool.tensor_tensor(wdtlo[:, :, :], wdt[:, :, :], wdthi[:, :, :].bitcast(F32), ALU.subtract)\
                    .then_inc(s["wdt_lo"], 1)

                def split_lo(n):
                    pool.wait_ge(s["hi"], n + 1)
                    if n >= 2:
                        pool.wait_ge(s["unit"], n - 1)
                    pool.tensor_tensor(wlo[:, n % 2, :], raw[:, n % 3, :], whi[:, n % 2, :].bitcast(F32),
                                       ALU.subtract).then_inc(s["lo"], 1)

                def leaving(c):
                    pool.wait_ge(s["ecums"], 1)
                    pool.wait_ge(s["xdt"], NG * c + NG)
                    if c:
                        pool.wait_ge(s["st_mm"], NG * c)
                    for g in range(NG):
                        pool.tensor_tensor(heads(xde[:, g * GW:(g + 1) * GW]), heads(xdt[:, g * GW:(g + 1) * GW]),
                                           per_head(ecums[:, 2], c, g), ALU.mult).then_inc(s["xde"], 1)

                def skip(c):
                    for g in range(NG):
                        pool.tensor_tensor(heads(x_c[:, g * GW:(g + 1) * GW]), heads(x_c[:, g * GW:(g + 1) * GW]),
                                           rows[:, 2, g * HPG:(g + 1) * HPG].unsqueeze(2).to_broadcast([P, HPG, HD]),
                                           ALU.mult).then_inc(s["xskip"], 1)

                for n in range(SC0):
                    split_lo(n)
                split_lo(SC0)
                split_lo(SC0 + 1)
                pool.wait_ge(s["par_in"], 16 * 9)
                for j in range(NSC):
                    n = SC0 + 3 * j
                    split_lo(n + 2)
                    split_lo(n + 3)
                    split_lo(n + 4)
                    if j % 2 == 0:
                        leaving(j // 2)
                        skip(j // 2)
                for n in range(OUT0 + 2, UNITS):
                    split_lo(n)

            @block.scalar
            def _(act):
                act.dma_start(bcond[:, :], a["b_condT"]).then_inc(s["par_in"], 16)
                act.dma_start(scw[:, :, :], a["sc_conv_wT"]).then_inc(s["par_in"], 16)
                act.dma_start(ssw[:, :, :], a["ssm_conv_wT"]).then_inc(s["par_in"], 16)
                act.dma_start(ssb[:, :], a["ssm_conv_bT"]).then_inc(s["par_in"], 16)
                act.dma_start(scn[:, :], a["sc_norm_wT"]).then_inc(s["par_in"], 16)
                act.dma_start(ssn[:, :], a["ssm_norm_wT"]).then_inc(s["par_in"], 16)
                for r, name in enumerate(("dt_bias", "a_log", "d_skip")):
                    act.dma_start(rows[:, r, :], a[name][0, :].partition_broadcast(P)).then_inc(s["par_in"], 16)
                act.dma_start(wdt[:, :, :], a["w_dt"]).then_inc(s["wdt_in"], 16)
                act.wait_ge(s["c_in"], 16)
                act.activation(cact[:, 1, :], cact[:, 0, :], ACT.Silu).then_inc(s["cact"], 1)
                act.wait_ge(s["wdt_in"], 16)
                act.activation(wdthi[:, :, :], wdt[:, :, :], ACT.Copy).then_inc(s["wdt_hi"], 1)
                act.wait_ge(s["par_in"], 16 * 9)

                def split_hi(n):
                    if n >= UNITS:
                        return
                    act.wait_ge(loaded[n % 3], 16 * (n // 3 + 1))
                    if n >= 2:
                        act.wait_ge(s["unit"], n - 1)
                    act.activation(whi[:, n % 2, :], raw[:, n % 3, :], ACT.Copy).then_inc(s["hi"], 1)

                split_hi(0)
                split_hi(1)
                for k in range(KD):
                    act.wait_ge(s["u1"], k + 1)
                    act.activation(u1hi[:, k, :], xT[:, k, :], ACT.Copy).then_inc(s["u1hi"], 1)

                def conv_silu(m):
                    act.wait_ge(s["conv_done"], m + 1)
                    act.activation(xbcT[:, m, :], conv[:, m % 2, :], ACT.Silu, bias=ssb[:, m:m + 1])\
                        .then_inc(s["xbc_act"], 1)

                act.wait_ge(s["pads_zero"], 1)
                for m in range(KX):
                    split_hi(XBC0 + m + 1) if m else None
                    act.wait_ge(s["unit"], XBC0 + m + 1)
                    if m >= 2:
                        act.wait_ge(s["conv_done"], m - 1)
                    act.activation(pad[:, m % 2, K_SSM - 1:], bank[m % 4][:, :], ACT.Copy).then_inc(s["xbc_copied"], 1)
                    if m:
                        conv_silu(m - 1)
                split_hi(Z0 + 1)
                conv_silu(KX - 1)
                for n in range(Z0, SC0):
                    if n > Z0:
                        split_hi(n + 1)
                    if (n - Z0) % 4 == 3:
                        half = (n - Z0) // 4
                        act.wait_ge(s["unit"], n + 1)
                        if n == SC0 - 1:
                            split_hi(SC0 + 1)
                        for c in range(TT):
                            act.activation(zs[:, c, half * 512:(half + 1) * 512], bank[c][:, :], ACT.Silu)\
                                .then_inc(s["z_out"], 1)
                act.wait_ge(s["dt_x"], 2)
                act.activation(dtb[:, 2], dtb[:, 1], ACT.Exp).then_inc(s["dt_exp"], 1)
                act.activation(dtb[:, 7, 0, :], rows[:, 1, :], ACT.Exp).then_inc(s["dt_exp"], 1)
                act.wait_ge(s["dt_w"], 1)
                act.activation(dtb[:, 4], dtb[:, 3], ACT.Ln).then_inc(s["dt_ln"], 1)
                eps_rms = eps_tile[:, 0:1]

                def sc_rstd(j):
                    act.wait_ge(s["mean_mm"], j + 1)
                    if j:
                        act.wait_ge(s["ysc_norm"], j)
                    act.activation(rs[:, :], bank[5][:, :], ACT.Ln, bias=eps_rms).then_inc(s["mean_out"], 1)
                    act.wait_ge(s["mean_out"], j + 1)
                    act.activation(rs[:, :], rs[:, :], ACT.Exp, scale=-0.5).then_inc(s["rstd"], 1)

                def chunk_copies(c):
                    for g in range(NG):
                        act.wait_ge(s["xtr_mm"], NG * c + g + 1)
                        if c:
                            act.wait_ge(s["y_gated"], c)
                            act.wait_ge(s["ysum"], NG * c)
                        act.activation(x_c[:, g * 512:(g + 1) * 512], bank[3 + g][:, :], ACT.Copy)\
                            .then_inc(s["x_copied"], 1)
                    act.wait_ge(s["cb_mm"], c + 1)
                    if c:
                        act.wait_ge(s["st_mm"], NG * c)
                    act.activation(btm[:, :], bank[5][:, 0:NG * P], ACT.Copy).then_inc(s["btm"], 1)

                def decays(c):
                    for q in range(4):
                        act.wait_ge(s["seg"], 4 * c + q + 1)
                        act.activation(decay[:, 4 * q:4 * q + 4, :], decay[:, 4 * q:4 * q + 4, :], ACT.Exp)\
                            .then_inc(s["dexp"], 1)

                def chunk_rstd(c):
                    act.wait_ge(s["y_gated"], c + 1)
                    for g in range(NG):
                        act.activation(x_c[:, g * GW:(g + 1) * GW], y[:, g * GW:(g + 1) * GW], ACT.Square,
                                       accum_out=ssum[:, 0, g:g + 1]).then_inc(s["ysum"], 1)
                    act.wait_ge(s["ysum"], NG * c + NG)
                    if c:
                        act.wait_ge(s["yn"], c)
                    act.activation(ssum[:, 1, :], ssum[:, 0, :], ACT.Ln, scale=1.0 / GW, bias=eps_rms)\
                        .then_inc(s["yln"], 1)
                    act.wait_ge(s["yln"], c + 1)
                    act.activation(ssum[:, 1, :], ssum[:, 1, :], ACT.Exp, scale=-0.5).then_inc(s["yrstd"], 1)

                for j in range(NSC):
                    n = SC0 + 3 * j
                    if j:
                        sc_rstd(j - 1)
                    split_hi(n + 2)
                    act.wait_ge(s["unit"], n + 1)
                    if j:
                        act.wait_ge(s["h_used"], j)
                    act.activation(csb[:, :], bank[1][:, :], ACT.Copy).then_inc(s["c_copied"], 1)
                    split_hi(n + 3)
                    if j % 2:
                        decays(j // 2)
                    elif j:
                        chunk_rstd(j // 2 - 1)
                    split_hi(n + 4)
                    act.wait_ge(s["ysc"], j + 1)
                    if j:
                        act.wait_ge(s["mean_mm"], j)
                    act.activation(ysq[:, :], ymixT[:, j, :], ACT.Square).then_inc(s["ysq"], 1)
                    if j == 0:
                        act.wait_ge(s["cums"], 2)
                        act.activation(ecums[:, :, :, :], cums[:, :, :, :], ACT.Exp).then_inc(s["ecums"], 1)
                    if j % 2 == 0:
                        chunk_copies(j // 2)
                sc_rstd(NSC - 1)
                chunk_rstd(TT - 1)
                for h in range(2):
                    act.wait_ge(s["gate_mm"], h + 1)
                    act.activation(state[:, h * 512:(h + 1) * 512], bank[6 + h][:, :], ACT.Copy)\
                        .then_inc(s["gate"], 1)

                def split_y(k):
                    if k >= NSC:
                        act.wait_ge(s["yT"], NG * TT)
                    act.wait_ge(s["ysc_norm"], min(k + 1, NSC))
                    if k >= 2:
                        act.wait_ge(s["unit"], OUT0 + k - 1)
                    act.activation(yhi[:, k % 2, :], ymixT[:, k, :], ACT.Copy).then_inc(s["yhi"], 1)

                split_y(0)
                split_y(1)
                for k in range(2, 16):
                    split_hi(OUT0 + k)
                    split_y(k)

            @block.vector
            def _(dve):
                links = [0]

                def link(ins):
                    links[0] += 1
                    ins.then_inc(s["chain"], 1)
                    dve.wait_ge(s["chain"], links[0])

                link(dve.memset(eps_tile[:, 0:1], RMS_EPS))
                link(dve.memset(eps_tile[:, 1:2], LN_EPS))
                dve.memset(pad[:, :, 0:K_SSM - 1], 0.0).then_inc(s["pads_zero"], 1)
                dve.wait_ge(s["cact"], 1)

                def sum_cond(i):
                    dve.wait_ge(c_loaded[i % 2], 16 * (i // 2 + 1))
                    if i >= 2:
                        dve.wait_ge(s["cond_mm"], i - 1)
                    o = csum[:, i % 2, :]
                    link(dve.tensor_scalar(o, craw[:, i % 2, 0:P], cact[:, 1, 0:1], None, ALU.mult))
                    for k in range(1, KD):
                        ins = dve.scalar_tensor_tensor(out=o, in0=craw[:, i % 2, k * P:(k + 1) * P],
                                                       scalar=cact[:, 1, k:k + 1], in1=o, op0=ALU.mult, op1=ALU.add)
                        if k < KD - 1:
                            link(ins)
                    ins.then_inc(s["cond_sum"], 1)

                for i in range(CA):
                    sum_cond(i)
                dve.wait_ge(s["par_in"], 16 * 9)
                dve.wait_ge(s["cond_mm"], CA)
                dve.tensor_tensor(cond[:, 0:CA], bank[5][:, 0:CA], bcond[:, 0:CA], ALU.add).then_inc(s["cond_out"], 1)
                dve.wait_ge(s["cond_out"], 1)
                link(dve.tensor_scalar(cond[:, 8:16], cond[:, 8:16], 1.0, None, ALU.add))
                dve.wait_ge(s["xT_in"], 16)

                def u1_lo(k):
                    dve.wait_ge(s["u1hi"], k + 1)
                    dve.tensor_tensor(u1lo[:, k, :], xT[:, k, :], u1hi[:, k, :].bitcast(F32), ALU.subtract)\
                        .then_inc(s["u1lo"], 1)

                for k in range(KD):
                    dve.tensor_scalar(xT[:, k, :], xT[:, k, :], cond[:, 8 + k:9 + k], cond[:, k:k + 1],
                                      ALU.mult, ALU.add).then_inc(s["u1"], 1)
                    if k:
                        u1_lo(k - 1)
                u1_lo(KD - 1)
                for m in range(KX):
                    for i in cond_units_at(XBC0 + m):
                        sum_cond(i)
                    dve.wait_ge(s["xbc_copied"], m + 1)
                    if m >= 2:
                        dve.wait_ge(s["xbc_act"], m - 1)
                    o = conv[:, m % 2, :]
                    link(dve.tensor_scalar(o, pad[:, m % 2, 0:T], ssw[:, m, 0:1], None, ALU.mult))
                    for k in range(1, K_SSM):
                        ins = dve.scalar_tensor_tensor(out=o, in0=pad[:, m % 2, k:k + T], scalar=ssw[:, m, k:k + 1],
                                                       in1=o, op0=ALU.mult, op1=ALU.add)
                        if k < K_SSM - 1:
                            link(ins)
                    ins.then_inc(s["conv_done"], 1)
                dve.wait_ge(s["dt_mm"], 1)
                link(dve.tensor_tensor(dtb[:, 0], bank[4][:, 0:TT * SH].rearrange("p (c h) -> p c h", h=SH),
                                       rows[:, 0:1, :].to_broadcast([P, TT, SH]), ALU.add))
                dve.tensor_scalar(dtb[:, 5], dtb[:, 0], -1.0, None, ALU.mult).then_inc(s["dt_x"], 1)
                dve.wait_ge(s["dt_x"], 1)
                dve.tensor_tensor(dtb[:, 1], dtb[:, 0], dtb[:, 5], ALU.min).then_inc(s["dt_x"], 1)
                for n in range(Z0, SC0):
                    for i in cond_units_at(n):
                        sum_cond(i)
                dve.wait_ge(s["cond_mm"], CA + CB)
                dve.tensor_tensor(cond[:, CA:48], bank[5][:, CA:48], bcond[:, CA:48], ALU.add).then_inc(s["cond_out"], 1)
                dve.wait_ge(s["cond_out"], 2)
                for lo in (16, 32, 40):
                    dve.tensor_scalar(cond[:, lo:lo + 8], cond[:, lo:lo + 8], 1.0, None, ALU.add)\
                        .then_inc(s["cond_out"], 1)
                dve.wait_ge(s["dt_exp"], 2)
                dve.tensor_scalar(dtb[:, 3], dtb[:, 2], 1.0, None, ALU.add).then_inc(s["dt_w"], 1)
                dve.wait_ge(s["dt_w"], 1)
                link(dve.tensor_scalar(dtb[:, 5], dtb[:, 3], -1.0, None, ALU.add))
                link(dve.tensor_tensor(dtb[:, 6], dtb[:, 2], dtb[:, 5], ALU.subtract))
                link(dve.reciprocal(dtb[:, 5], dtb[:, 3]))
                link(dve.tensor_tensor(dtb[:, 6], dtb[:, 6], dtb[:, 5], ALU.mult))
                link(dve.tensor_scalar(dtb[:, 5], dtb[:, 0], 0.0, None, ALU.max))
                link(dve.tensor_tensor(dtb[:, 6], dtb[:, 6], dtb[:, 5], ALU.add))
                dve.wait_ge(s["dt_ln"], 1)
                link(dve.tensor_tensor(dt[:, :, :], dtb[:, 4], dtb[:, 6], ALU.add))
                link(dve.tensor_tensor(dtb[:, 5], dt[:, :, :], dtb[:, 7, 0:1, :].to_broadcast([P, TT, SH]), ALU.mult))
                dve.tensor_scalar(adt[:, :, :], dtb[:, 5], -1.0, None, ALU.mult).then_inc(s["adt"], 1)
                dve.wait_ge(s["cum_mm"], 2)
                dve.tensor_copy(cums[:, 0:2, :, :], bank[7][:, 0:2 * TT * SH]
                                .rearrange("p (r c h) -> p r c h", r=2, h=SH)).then_inc(s["cums"], 1)
                dve.wait_ge(s["cums"], 1)
                dve.tensor_tensor(cums[:, 2], cums[:, 1], cums[:, 0], ALU.subtract).then_inc(s["cums"], 1)

                def sc_conv(j):
                    n = SC0 + 3 * j
                    dve.wait_ge(s["unit"], n + 2)
                    dve.wait_ge(s["c_copied"], j + 1)
                    dve.tensor_tensor(pad[:, j % 2, K_SSM - 1:], bank[2][:, :], csb[:, :], ALU.mult)\
                        .then_inc(s["h_used"], 1)
                    dve.wait_ge(s["h_used"], j + 1)
                    o = conv[:, j % 2, :]
                    for k in range(K_SC):
                        src = pad[:, j % 2, K_SSM - K_SC + k:K_SSM - K_SC + k + T]
                        if k == 0:
                            link(dve.tensor_scalar(o, src, scw[:, j, 0:1], None, ALU.mult))
                        else:
                            link(dve.scalar_tensor_tensor(out=o, in0=src, scalar=scw[:, j, k:k + 1], in1=o,
                                                          op0=ALU.mult, op1=ALU.add))

                def sc_out(j):
                    dve.wait_ge(s["unit"], SC0 + 3 * j + 3)
                    dve.tensor_tensor(ymixT[:, j, :], bank[0][:, :], conv[:, j % 2, :], ALU.mult)\
                        .then_inc(s["ysc"], 1)

                def sc_norm(j):
                    dve.wait_ge(s["rstd"], j + 1)
                    dve.scalar_tensor_tensor(out=ymixT[:, j, :], in0=ymixT[:, j, :], scalar=scn[:, j:j + 1],
                                             in1=rs[:, :], op0=ALU.mult, op1=ALU.mult).then_inc(s["ysc_norm"], 1)

                def part1(c):
                    for g in range(NG):
                        dve.wait_ge(s["x_copied"], NG * c + g + 1)
                        if c:
                            dve.wait_ge(s["yd_mm"], NG * c)
                            dve.wait_ge(s["xde"], NG * c)
                        dve.tensor_tensor(heads(xdt[:, g * GW:(g + 1) * GW]), heads(x_c[:, g * GW:(g + 1) * GW]),
                                          per_head(dt, c, g), ALU.mult).then_inc(s["xdt"], 1)
                    for q in range(4):
                        dve.wait_ge(s["row_mm"], 4 * c + q + 1)
                        if c:
                            dve.wait_ge(s["yd_mm"], NG * c)
                        for r in range(4):
                            h = 4 * q + r
                            ins = dve.tensor_scalar(decay[:, h, :], bank[6 + q % 2][:, r * P:(r + 1) * P],
                                                    cums[:, 0, c, h:h + 1], 0.0, ALU.subtract, ALU.min)
                        ins.then_inc(s["seg"], 1)
                    dve.wait_ge(s["btm"], c + 1)
                    dve.tensor_tensor(cbm[:, :, :], bank[5][:, 256:512].rearrange("p (g l) -> p g l", g=NG),
                                      tri[:, :].unsqueeze(1).to_broadcast([P, NG, P]), ALU.mult)\
                        .then_inc(s["cbm"], 1)

                def chunk_weights(c):
                    for g in range(NG):
                        dve.wait_ge(s["dexp"], 4 * c + 2 * g + 2)
                        dve.wait_ge(s["cbm"], c + 1)
                        dg = decay[:, g * HPG:(g + 1) * HPG, :]
                        dve.tensor_tensor(dg, dg, cbm[:, g, :].unsqueeze(1).to_broadcast([P, HPG, P]), ALU.mult)\
                            .then_inc(s["weights"], 1)

                def state_update(c, g):
                    st = state[:, g * GW:(g + 1) * GW]
                    if c:
                        dve.wait_ge(s["yo_mm"], NG * (c - 1) + g + 1)
                        link(dve.tensor_tensor(heads(st), heads(st), per_head(ecums[:, 1], c, g), ALU.mult))
                        dve.wait_ge(s["st_mm"], NG * c + g + 1)
                        dve.tensor_tensor(st, st, bank[5][:, :], ALU.add).then_inc(s["st_out"], 1)
                    else:
                        dve.wait_ge(s["st_mm"], g + 1)
                        dve.tensor_copy(st, bank[5][:, :]).then_inc(s["st_out"], 1)
                    dve.wait_ge(s["st_out"], NG * c + g + 1)

                def part2(c):
                    if c < TT - 1:
                        state_update(c, 0)
                    if c:
                        dve.wait_ge(s["ytr_mm"], NG * c)
                        for g in range(NG):
                            dve.wait_ge(s["yo_mm"], NG * (c - 1) + g + 1)
                            dve.tensor_tensor(heads(y[:, g * GW:(g + 1) * GW]), heads(bank[6 + g][:, :]),
                                              per_head(ecums[:, 0], c, g), ALU.mult).then_inc(s["yo_out"], 1)
                        dve.wait_ge(s["yo_out"], NG * c)
                        for g in range(NG):
                            dve.wait_ge(s["yd_mm"], NG * c + g + 1)
                            yg = y[:, g * GW:(g + 1) * GW]
                            link(dve.tensor_tensor(yg, yg, bank[3 + g][:, :], ALU.add))
                    else:
                        for g in range(NG):
                            dve.wait_ge(s["yd_mm"], g + 1)
                            link(dve.tensor_copy(y[:, g * GW:(g + 1) * GW], bank[3 + g][:, :]))
                    dve.wait_ge(s["xskip"], NG * c + NG)
                    link(dve.tensor_tensor(y[:, :], y[:, :], x_c[:, :], ALU.add))
                    dve.tensor_tensor(y[:, :], y[:, :], zs[:, c, :], ALU.mult).then_inc(s["y_gated"], 1)
                    if c < TT - 1:
                        state_update(c, 1)

                def chunk_norm(c):
                    dve.wait_ge(s["yrstd"], c + 1)
                    link(dve.tensor_scalar(y[:, 0:GW], y[:, 0:GW], ssum[:, 1, 0:1], None, ALU.mult))
                    dve.tensor_scalar(y[:, GW:D], y[:, GW:D], ssum[:, 1, 1:2], None, ALU.mult).then_inc(s["yn"], 1)

                def part3(c):
                    for g in range(NG):
                        dve.wait_ge(s["ytr_mm"], NG * c + g + 1)
                        dve.tensor_tensor(ymixT[:, 8 + 4 * g:12 + 4 * g, cs(c)],
                                          bank[3 + g][:, :].rearrange("p (j t) -> p j t", t=P),
                                          ssn[:, 4 * g:4 * g + 4].unsqueeze(2).to_broadcast([P, 4, P]), ALU.mult)\
                            .then_inc(s["yT"], 1)

                for j in range(NSC):
                    if j:
                        sc_norm(j - 1)
                    sc_conv(j)
                    if j % 2:
                        chunk_weights(j // 2)
                    elif j:
                        chunk_norm(j // 2 - 1)
                    sc_out(j)
                    if j % 2 == 0:
                        if j:
                            part3(j // 2 - 1)
                        part1(j // 2)
                    else:
                        part2(j // 2)
                sc_norm(NSC - 1)
                chunk_norm(TT - 1)
                part3(TT - 1)
                for k in range(16):
                    dve.wait_ge(s["yhi"], k + 1)
                    if k >= 2:
                        dve.wait_ge(s["unit"], OUT0 + k - 1)
                    dve.tensor_tensor(ylo[:, k % 2, :], ymixT[:, k, :], yhi[:, k % 2, :].bitcast(F32), ALU.subtract)\
                        .then_inc(s["ylo"], 1)
                dve.wait_ge(s["x_in"], 16)
                dve.wait_ge(s["gate"], 2)
                for c in range(TT):
                    dve.wait_ge(s["tile_mm"], c + 1)
                    for h in range(2):
                        hs = slice(h * 512, (h + 1) * 512)
                        link(dve.tensor_tensor(y[:, hs], bank[2 * c + h][:, :], state[:, hs], ALU.mult))
                    xs = x_tm[:, c, :]
                    dve.scalar_tensor_tensor(out=xs, in0=xs, scalar=ALPHA, in1=y[:, :], op0=ALU.mult, op1=ALU.add)\
                        .then_inc(s["out"], 1)
                    dve.wait_ge(s["out"], c + 1)

            @block.tensor
            def _(pe):
                pe.wait_ge(s["consts"], 8)

                def cond_column(i):
                    pe.wait_ge(s["cond_sum"], i + 1)
                    pe.matmul(bank[5][:, i:i + 1], csum[:, i % 2, :], ones[:, 0:1], start=True, stop=True)\
                        .then_inc(s["cond_mm"], 1)

                def channel_unit(n, b, each_k=None):
                    pe.wait_ge(s["lo"], n + 1)
                    for k in range(KD):
                        ks = slice(k * P, (k + 1) * P)
                        if each_k:
                            each_k(k)
                        pe.matmul(bank[b][:, :], whi[:, n % 2, ks], u1hi[:, k, :], start=(k == 0), stop=False)
                        pe.matmul(bank[b][:, :], whi[:, n % 2, ks], u1lo[:, k, :], start=False, stop=False)
                        ins = pe.matmul(bank[b][:, :], wlo[:, n % 2, ks], u1hi[:, k, :], start=False,
                                        stop=(k == KD - 1))
                    ins.then_inc(s["unit"], 1)

                for i in range(CA):
                    cond_column(i)
                for m in range(KX):
                    if m >= 4:
                        pe.wait_ge(s["xbc_copied"], m - 3)
                    channel_unit(XBC0 + m, m % 4, (lambda k: pe.wait_ge(s["u1lo"], k + 1)) if m == 0 else None)
                    if m == 0:
                        pe.wait_ge(s["cond_out"], 1)
                    for i in cond_units_at(XBC0 + m):
                        cond_column(i)
                pe.wait_ge(s["wdt_lo"], 1)
                for c in range(TT):
                    for k in range(KD):
                        for left, right in ((u1hi, wdthi), (u1hi, wdtlo), (u1lo, wdthi)):
                            ins = pe.matmul(bank[4][:, c * SH:(c + 1) * SH], left[:, k, cs(c)], right[:, k, :],
                                            start=(k == 0 and right is wdthi and left is u1hi),
                                            stop=(k == KD - 1 and left is u1lo))
                ins.then_inc(s["dt_mm"], 1)
                for n in range(Z0, SC0):
                    q = (n - Z0) % 4
                    pe.wait_ge(s["lo"], n + 1)
                    for c in range(TT):
                        if q == 0:
                            if n == Z0:
                                pe.wait_ge(s["xbc_copied"], KX - 3 + c)
                            else:
                                pe.wait_ge(s["z_out"], c + 1)
                        for k in range(2):
                            kk = 2 * q + k
                            for left, right in ((u1hi, whi), (u1hi, wlo), (u1lo, whi)):
                                ins = pe.matmul(bank[c][:, :], left[:, kk, cs(c)],
                                                right[:, n % 2, k * 512:(k + 1) * 512],
                                                start=(kk == 0 and left is u1hi and right is whi),
                                                stop=(kk == KD - 1 and left is u1lo))
                    ins.then_inc(s["unit"], 1)
                    for i in cond_units_at(n):
                        cond_column(i)

                def sc_mean(j):
                    pe.wait_ge(s["ysq"], j + 1)
                    if j % 2 == 0:
                        pe.wait_ge(s["btm"], j // 2 + 1)
                        pe.wait_ge(s["cbm"], j // 2 + 1)
                    elif j < NSC - 1:
                        pe.wait_ge(s["st_out"], NG * (j // 2) + NG)
                    pe.matmul(bank[5][:, :], grp[:, :], ysq[:, :], start=True, stop=True).then_inc(s["mean_mm"], 1)

                def sc_products(j):
                    n = SC0 + 3 * j
                    for r, (b, free) in enumerate(((1, "c_copied"), (2, "h_used"), (0, "ysc"))):
                        if j:
                            pe.wait_ge(s[free], j)
                        else:
                            pe.wait_ge(s["z_out"], TT + b + 1)
                        channel_unit(n + r, b)

                def part1(c):
                    for g in range(NG):
                        if c:
                            pe.wait_ge(s["yT"], NG * (c - 1) + g + 1)
                        for j in range(4):
                            ins = pe.transpose(bank[3 + g][:, j * P:(j + 1) * P], xbcT[:, 4 * g + j, cs(c)], ident[:, :])
                        ins.then_inc(s["xtr_mm"], 1)
                    pe.wait_ge(s["mean_out"], 2 * c) if c else pe.wait_ge(s["cond_out"], 2)
                    for g in range(NG):
                        pe.transpose(bank[5][:, g * P:(g + 1) * P], xbcT[:, 8 + g, cs(c)], ident[:, :])
                    for g in range(NG):
                        ins = pe.matmul(bank[5][:, 256 + g * P:256 + (g + 1) * P], xbcT[:, 8 + g, cs(c)],
                                        xbcT[:, 10 + g, cs(c)], start=True, stop=True)
                    ins.then_inc(s["cb_mm"], 1)
                    for q in range(4):
                        if q >= 2:
                            pe.wait_ge(s["seg"], 4 * c + q - 1)
                        elif c >= 2:
                            pe.wait_ge(s["yo_out"], NG * (c - 1))
                        elif c == 1:
                            pe.wait_ge(s["seg"], 4)
                        for r in range(4):
                            ins = pe.matmul(bank[6 + q % 2][:, r * P:(r + 1) * P],
                                            adt[:, c, 4 * q + r:4 * q + r + 1].to_broadcast([P, P]), tri[:, :],
                                            start=True, stop=True)
                        ins.then_inc(s["row_mm"], 1)

                def chunk_state(c, g):
                    pe.matmul(bank[5][:, :], btm[:, g * P:(g + 1) * P], xde[:, g * GW:(g + 1) * GW],
                              start=True, stop=True).then_inc(s["st_mm"], 1)

                def part2(c):
                    pe.wait_ge(s["mean_out"], 2 * c + 1)
                    if c < TT - 1:
                        pe.wait_ge(s["xde"], NG * c + NG)
                        chunk_state(c, 0)
                    pe.wait_ge(s["xdt"], NG * c + NG)
                    if c:
                        pe.wait_ge(s["seg"], 4 * c + 4)
                        for g in range(NG):
                            pe.wait_ge(s["st_out"], NG * (c - 1) + g + 1)
                            pe.matmul(bank[6 + g][:, :], xbcT[:, 10 + g, cs(c)], state[:, g * GW:(g + 1) * GW],
                                      start=True, stop=True).then_inc(s["yo_mm"], 1)
                    for g in range(NG):
                        pe.wait_ge(s["weights"], NG * c + g + 1)
                        for r in range(HPG):
                            h = g * HPG + r
                            ins = pe.matmul(bank[3 + g][:, r * HD:(r + 1) * HD], decay[:, h, :],
                                            xdt[:, h * HD:(h + 1) * HD], start=True, stop=True)
                        ins.then_inc(s["yd_mm"], 1)
                    if c < TT - 1:
                        pe.wait_ge(s["st_out"], NG * c + 1)
                        chunk_state(c, 1)

                def part3(c):
                    pe.wait_ge(s["yn"], c + 1)
                    for g in range(NG):
                        for j in range(4):
                            k = 4 * g + j
                            ins = pe.transpose(bank[3 + g][:, j * P:(j + 1) * P], y[:, k * P:(k + 1) * P], ident[:, :])
                        ins.then_inc(s["ytr_mm"], 1)

                for j in range(NSC):
                    if j:
                        sc_mean(j - 1)
                    sc_products(j)
                    if j == 0:
                        pe.wait_ge(s["adt"], 1)
                        for r, m in enumerate((tri, ones)):
                            pe.matmul(bank[7][:, r * TT * SH:(r + 1) * TT * SH], m[:, :],
                                      adt[:, :, :].rearrange("p c h -> p (c h)"), start=True, stop=True)\
                                .then_inc(s["cum_mm"], 1)
                        pe.wait_ge(s["cums"], 1)
                    if j % 2 == 0:
                        if j:
                            part3(j // 2 - 1)
                        part1(j // 2)
                    else:
                        part2(j // 2)
                sc_mean(NSC - 1)
                part3(TT - 1)
                pe.wait_ge(s["cond_out"], 5)
                pe.wait_ge(s["yo_out"], NG * (TT - 1))
                for m in range(KD):
                    ins = pe.matmul(bank[6 + m // 4][:, (m % 4) * P:(m % 4 + 1) * P],
                                    cond[:, 16 + m:17 + m].to_broadcast([P, P]), ident[:, :], start=True, stop=True)
                    if m % 4 == 3:
                        ins.then_inc(s["gate_mm"], 1)
                pe.wait_ge(s["gate"], 2)
                pe.wait_ge(s["mean_out"], NSC)
                pe.wait_ge(s["yT"], NG * TT)
                for k in range(16):
                    pe.wait_ge(s["lo"], OUT0 + k + 1)
                    pe.wait_ge(s["ylo"], k + 1)
                    w = (OUT0 + k) % 2
                    for c in range(TT):
                        for left, right in ((yhi, whi), (yhi, wlo), (ylo, whi)):
                            for h in range(2):
                                ins = pe.matmul(bank[2 * c + h][:, :], left[:, k % 2, cs(c)],
                                                right[:, w, h * 512:(h + 1) * 512],
                                                start=(k == 0 and left is yhi and right is whi),
                                                stop=(k == 15 and left is ylo))
                        if k == 15:
                            ins.then_inc(s["tile_mm"], 1)
                    if k < 15:
                        ins.then_inc(s["unit"], 1)


def wait(eng, sem, value):
    if not (isinstance(value, int) and value <= 0):
        eng.wait_ge(sem, value)


UNROLL = 8
TOK = 8
GT = 32
QCH = 2 * HEADS
PLAIN = NKEYS - T // TOK


def router(nc, a, x_tm, cond, ident, eps_tile, h_dram, g_dram):
    with ExitStack() as ctx:
        def sb(name, shape, dt=F32):
            return ctx.enter_context(nc.sbuf_tensor(name, shape, dt))

        def sem(name):
            return ctx.enter_context(nc.semaphore(name))

        bank = [ctx.enter_context(nc.psum_tensor(f"rt_bank{i}", [P, 512], F32)) for i in range(8)]
        u2hi = sb("u2_hi", [P, KD, T], F32R)
        u2lo = sb("u2_lo", [P, KD, T], F32R)
        keys = sb("keys", [P, QCH, NKEYS])
        sc_all = sb("scores", [P, TT, QCH * NKEYS])
        raw = sb("u_raw", [P, 4, KD * P])
        whi = sb("u_hi", [P, 2, KD * P], F32R)
        wlo = sb("u_lo", [P, 2, KD * P], F32R)
        hout = sb("h_out", [P, 2, T])
        st = sb("search", [P, QCH * NKEYS])
        rp = sb("search_rest", [P, QCH * NKEYS])
        val = sb("top_values", [P, QCH, TOPK])
        idx = sb("top_index", [P, QCH, TOPK], U32)
        idf = sb("top_index_f", [P, QCH, TOPK])
        tv = sb("pair_values", [P, HEADS, TOPK])
        pos = sb("pair_index", [P, 3, PICKS], U32)
        pof = sb("pair_index_f", [P, 2, PICKS])
        pk = sb("picks", [P, 3, TT, PICKS])
        gsum = sb("gate_sums", [P, 2, TT * HEADS])
        pT = sb("picks_T", [P, 3, T])
        hotA = sb("one_hot_gate", [P, TOK, NKEYS])
        hotB = sb("one_hot", [P, TOK, NKEYS])
        iota = sb("iota", [P, NKEYS])
        lst = sb("ln_stats", [P, TT, 2, 6])
        lmv = sb("ln_mean_var", [P, TT, 2])
        lrs = sb("ln_rstd", [P, TT])
        with nc.sbuf_tensor("ln_rows", [P, 2, D], F32) as lnr, nc.sbuf_tensor("u2_plain", [P, 2, T], F32) as u2f:
            pass
        with nc.sbuf_tensor("queries_T", [P, QCH, T], F32) as qT:
            pass
        gst = sb("g_staging", [P, 2, NKEYS, GT])

        loaded = [sem(f"r_loaded{i}") for i in range(4)]
        h_saved = [sem(f"h_saved{i}") for i in range(2)]
        g_saved = [sem(f"g_saved{i}") for i in range(2)]
        s = {n: sem("r_" + n) for n in (
            "rows_in", "keys_in", "iota", "stats", "ln_ln", "ln_rstd", "x1", "tr_mm", "u2f", "hi_u2", "lo_u2", "hi", "lo",
            "h_mm", "h_act", "sc_mm", "sc_out", "shifted", "gexp", "gates", "pt_mm", "pT", "hot", "g_mm", "g_out",
            "ordered", "chain")}

        def chunk_dram(n):
            return a["w_query"][n] if isinstance(n, int) and n < QCH else a["u_T"][n - QCH]

        def each_chunk(eng, body):
            for n in range(QCH):
                body(n, 0, False)
            with eng.Fori(0, PLAIN // UNROLL) as r:
                for u in range(UNROLL):
                    body(r * UNROLL + (QCH + u), u, False)

        def g_chunks(eng, body):
            with eng.Fori(0, (NKEYS - PLAIN) // UNROLL) as r:
                for u in range(UNROLL):
                    body(r * UNROLL + (QCH + PLAIN + u), u, True)

        with nc.Block() as block:
            @block.sync
            def _(sp):
                for r, name in enumerate(("ln1_g", "ln1_b")):
                    sp.dma_start(lnr[:, r, :], a[name][0, :].partition_broadcast(P)).then_inc(s["rows_in"], 16)
                sp.dma_start(keys[:, :, :], a["keysT"]).then_inc(s["keys_in"], 16)

                def load(n, u, g):
                    slot = (n if isinstance(n, int) else u) % 4
                    wait(sp, s["lo"], n - 3)
                    sp.dma_start(raw[:, slot, :], chunk_dram(n).rearrange("p k e -> p (k e)"))\
                        .then_inc(loaded[slot], 16)

                each_chunk(sp, load)
                g_chunks(sp, load)

            @block.gpsimd
            def _(pool):
                pool.iota(iota[:, :], [[1, NKEYS]], base=0, channel_multiplier=0,
                          allow_small_or_imprecise_dtypes=True).then_inc(s["iota"], 1)

                def split_lo(n, u, g):
                    slot = (n if isinstance(n, int) else u) % 4
                    pool.wait_ge(s["hi"], n + 1)
                    wait(pool, s["h_mm"], n - 1)
                    pool.tensor_tensor(wlo[:, slot % 2, :], raw[:, slot, :], whi[:, slot % 2, :].bitcast(F32),
                                       ALU.subtract).then_inc(s["lo"], 1)

                each_chunk(pool, split_lo)
                g_chunks(pool, split_lo)

            @block.scalar
            def _(act):
                for c in range(TT):
                    act.wait_ge(s["stats"], c + 1)
                    act.activation(lrs[:, c:c + 1], lmv[:, c, 1:2], ACT.Ln, bias=eps_tile[:, 1:2])\
                        .then_inc(s["ln_ln"], 1)
                    act.wait_ge(s["ln_ln"], c + 1)
                    act.activation(lrs[:, c:c + 1], lrs[:, c:c + 1], ACT.Exp, scale=-0.5).then_inc(s["ln_rstd"], 1)
                for k in range(KD):
                    act.wait_ge(s["tr_mm"], k + 1)
                    wait(act, s["lo_u2"], k - 1)
                    act.activation(u2f[:, k % 2, :], bank[k % 2][:, :], ACT.Identity, scale=cond[:, 32 + k:33 + k],
                                   bias=cond[:, 24 + k:25 + k]).then_inc(s["u2f"], 1)
                    act.wait_ge(s["u2f"], k + 1)
                    act.activation(u2hi[:, k, :], u2f[:, k % 2, :], ACT.Copy).then_inc(s["hi_u2"], 1)

                def split_hi(n, u, g):
                    slot = (n if isinstance(n, int) else u) % 4
                    act.wait_ge(loaded[slot], (n // 4) * 16 + 16 if isinstance(n, int) else (n + (4 - slot)) * 4)
                    wait(act, s["h_mm"], n - 1)
                    act.activation(whi[:, slot % 2, :], raw[:, slot, :], ACT.Copy).then_inc(s["hi"], 1)

                def query_out(n):
                    act.wait_ge(s["h_mm"], n + 1)
                    if n == 0:
                        act.wait_ge(s["lo_u2"], KD)
                    act.activation(qT[:, n, :], bank[n % 2][:, :], ACT.Copy).then_inc(s["h_act"], 1)

                def gelu_out(n, u, g):
                    act.wait_ge(s["h_mm"], n + 1)
                    act.wait_ge(h_saved[u % 2], (n - (QCH + u % 2)) * 8 + 16)
                    act.activation(hout[:, u % 2, :], bank[u % 2][:, :], ACT.Gelu).then_inc(s["h_act"], 1)
                    act.wait_ge(s["h_act"], n + 1)
                    act.dma_start(h_dram[n - QCH], hout[:, u % 2, :]).then_inc(h_saved[u % 2], 16)
                    if g and u % 4 == 3:
                        act.wait_ge(s["g_out"], (n - (QCH + PLAIN)) * 2 + 2)
                        act.dma_start(g_dram[(n - (QCH + PLAIN + u)) // 4 + u // 4],
                                      gst[:, u // 4, :, :]).then_inc(g_saved[u // 4], 16)

                act.sem_inc(h_saved[0], 16)
                act.sem_inc(h_saved[1], 16)
                for n in range(QCH):
                    split_hi(n, 0, False)
                    if n:
                        query_out(n - 1)
                split_hi(QCH, 0, False)
                query_out(QCH - 1)
                for c in range(TT):
                    for b in range(4):
                        act.wait_ge(s["sc_mm"], 4 * c + b + 1)
                        act.activation(sc_all[:, c, b * 512:(b + 1) * 512], bank[2 + b][:, :], ACT.Copy)\
                            .then_inc(s["sc_out"], 1)
                with act.Fori(0, PLAIN // UNROLL) as r:
                    for u in range(UNROLL):
                        n = r * UNROLL + (QCH + u)
                        split_hi(n + 1, (u + 1) % UNROLL, False)
                        gelu_out(n, u, False)
                act.wait_ge(s["shifted"], TT)
                act.activation(pk[:, 2, :, :], pk[:, 2, :, :], ACT.Exp).then_inc(s["gexp"], 1)
                turns = (NKEYS - PLAIN) // UNROLL
                with act.Fori(0, turns - 1) as r:
                    for u in range(UNROLL):
                        n = r * UNROLL + (QCH + PLAIN + u)
                        split_hi(n + 1, (u + 1) % UNROLL, True)
                        gelu_out(n, u, True)
                for u in range(UNROLL):
                    n = (turns - 1) * UNROLL + QCH + PLAIN + u
                    if u < UNROLL - 1:
                        split_hi(n + 1, u + 1, True)
                    gelu_out(n, u, True)
                for i in range(2):
                    act.wait_ge(h_saved[i], 16 + 16 * (NKEYS // 2))
                    act.wait_ge(g_saved[i], 16 + 16 * (T // GT // 2))

            @block.vector
            def _(dve):
                links = [0]

                def link(ins, base=0):
                    links[0] += 1
                    ins.then_inc(s["chain"], 1)
                    dve.wait_ge(s["chain"], base + links[0])

                dve.wait_ge(s["rows_in"], 32)
                for c in range(TT):
                    for h in range(2):
                        ins = dve.bn_stats(lst[:, c, h, :], x_tm[:, c, h * 512:(h + 1) * 512])
                    link(ins)
                    dve.bn_aggr(lmv[:, c, :], lst[:, c, :, :]).then_inc(s["stats"], 1)
                for c in range(TT):
                    dve.wait_ge(s["ln_rstd"], c + 1)
                    xs = x_tm[:, c, :]
                    link(dve.tensor_scalar(xs, xs, lmv[:, c, 0:1], lrs[:, c:c + 1], ALU.subtract, ALU.mult))
                    link(dve.tensor_tensor(xs, xs, lnr[:, 0, :], ALU.mult))
                    dve.tensor_tensor(xs, xs, lnr[:, 1, :], ALU.add).then_inc(s["x1"], 1)
                for k in range(KD):
                    dve.wait_ge(s["hi_u2"], k + 1)
                    dve.tensor_tensor(u2lo[:, k, :], u2f[:, k % 2, :], u2hi[:, k, :].bitcast(F32), ALU.subtract)\
                        .then_inc(s["lo_u2"], 1)

                straight = links[0]
                s3 = st[:, :].rearrange("p (m n) -> p m n", n=NKEYS)
                r3 = rp[:, :].rearrange("p (m n) -> p m n", n=NKEYS)
                c3 = st[:, :].rearrange("p (h n) -> p h n", n=TOPK * TOPK)
                q3 = rp[:, :].rearrange("p (h n) -> p h n", n=TOPK * TOPK)
                e4 = st[:, :].rearrange("p (h k a) -> p h k a", h=HEADS, k=TOPK)
                v4 = val[:, :, :].rearrange("p (h w) k -> p h w k", w=2)
                i4 = idf[:, :, :].rearrange("p (h w) k -> p h w k", w=2)

                def top16(values, indices, source, rest, n):
                    def each(f):
                        for m in range(n):
                            ins = f(m)
                        step(ins)
                    dve.sem_inc(s["ordered"], 1)
                    each(lambda m: dve.max(values[:, m, 0:8], source[:, m, :]))
                    dve.sem_inc(s["ordered"], 1)
                    for m in range(n):
                        dve.max_index(indices[:, m, 0:8], values[:, m, 0:8], source[:, m, :])
                    each(lambda m: dve.match_replace(rest[:, m, :], values[:, m, 0:8], source[:, m, :], FLOOR))
                    dve.sem_inc(s["ordered"], 1)
                    each(lambda m: dve.max(values[:, m, 8:16], rest[:, m, :]))
                    dve.sem_inc(s["ordered"], 1)
                    each(lambda m: dve.max_index(indices[:, m, 8:16], values[:, m, 8:16], rest[:, m, :]))

                count = [0]
                STEPS = 1 + 4 + 1 + 1 + 4 + 1 + 1 + 3 * 2

                with dve.Fori(0, TT) as c:
                    def step(ins):
                        count[0] += 1
                        ins.then_inc(s["chain"], 1)
                        dve.wait_ge(s["chain"], c * STEPS + (straight + count[0]))

                    dve.wait_ge(s["sc_out"], c * 4 + 4)
                    step(dve.tensor_copy(st[:, :], sc_all[:, bass.ds(c, 1), :].rearrange("p c n -> p (c n)")))
                    top16(val, idx, s3, r3, QCH)
                    step(dve.tensor_copy(idf[:, :, :], idx[:, :, :]))
                    step(dve.tensor_tensor(e4, v4[:, :, 0, :].unsqueeze(3).to_broadcast([P, HEADS, TOPK, TOPK]),
                                           v4[:, :, 1, :].unsqueeze(2).to_broadcast([P, HEADS, TOPK, TOPK]), ALU.add))
                    p3 = pos[:, 0, :].rearrange("p (h k) -> p h k", k=TOPK)
                    top16(tv, p3, c3, q3, HEADS)
                    dve.tensor_scalar(pos[:, 1, :], pos[:, 0, :], 4, None, ALU.logical_shift_right)
                    step(dve.tensor_scalar(pos[:, 2, :], pos[:, 0, :], 15, None, ALU.bitwise_and))
                    step(dve.tensor_copy(pof[:, :, :], pos[:, 1:3, :]))
                    for w in range(2):
                        pw = pof[:, w, :].rearrange("p (h k) -> p h k", k=TOPK)
                        step(dve.tensor_tensor(
                            e4, pw.unsqueeze(3).to_broadcast([P, HEADS, TOPK, TOPK]),
                            iota[:, 0:TOPK].unsqueeze(1).unsqueeze(1).to_broadcast([P, HEADS, TOPK, TOPK]),
                            ALU.is_equal))
                        step(dve.tensor_tensor(
                            e4, e4, i4[:, :, w, :].unsqueeze(2).to_broadcast([P, HEADS, TOPK, TOPK]), ALU.mult))
                        step(dve.tensor_reduce(
                            pk[:, w, bass.ds(c, 1), :].rearrange("p c k -> p (c k)"),
                            st[:, :].rearrange("p (k a) -> p k a", a=TOPK), AX_X, ALU.add))
                    dve.tensor_tensor(
                        pk[:, 2, bass.ds(c, 1), :].rearrange("p c (h k) -> p (c h) k", k=TOPK), tv[:, :, :],
                        tv[:, :, 0:1].to_broadcast([P, HEADS, TOPK]), ALU.subtract).then_inc(s["shifted"], 1)
                    dve.wait_ge(s["shifted"], c + 1)
                assert count[0] == STEPS, count
                links[0] = straight + TT * STEPS
                g3 = pk[:, 2, :, :].rearrange("p c (h k) -> p (c h) k", k=TOPK)
                dve.wait_ge(s["gexp"], 1)
                link(dve.tensor_reduce(gsum[:, 0, :], g3, AX_X, ALU.add))
                link(dve.reciprocal(gsum[:, 1, :], gsum[:, 0, :]))
                dve.tensor_tensor(g3, g3, gsum[:, 1, :].unsqueeze(2).to_broadcast([P, TT * HEADS, TOPK]), ALU.mult)\
                    .then_inc(s["gates"], 1)
                for w in range(3):
                    dve.wait_ge(s["pt_mm"], w + 1)
                    dve.tensor_copy(pT[:, w, :], bank[2 + w][:, :]).then_inc(s["pT"], 1)
                dve.wait_ge(s["pT"], 3)
                dve.wait_ge(s["iota"], 1)

                for i in range(2):
                    dve.sem_inc(g_saved[i], 16)
                def gates_of(n, u, g):
                    base = (n - (QCH + PLAIN)) * TOK
                    for t in range(TOK):
                        dve.tensor_scalar(hotB[:, t, :], iota[:, :], pT[:, 1, bass.ds(base + t, 1)], None, ALU.is_equal)
                        ins = dve.tensor_scalar(hotA[:, t, :], iota[:, :], pT[:, 0, bass.ds(base + t, 1)],
                                                pT[:, 2, bass.ds(base + t, 1)], ALU.is_equal, ALU.mult)
                    ins.then_inc(s["hot"], 1)
                    for b in range(2):
                        dve.wait_ge(s["g_mm"], (n - (QCH + PLAIN)) * 2 + (b + 1))
                        if u % 4 == 0 and b == 0:
                            dve.wait_ge(g_saved[u // 4], (n - (QCH + PLAIN + u)) * 2 + 16)
                        col = (u % 4) * TOK + 4 * b
                        dve.tensor_copy(gst[:, u // 4, :, col:col + 4],
                                        bank[6 + b][:, :].rearrange("p (t i) -> p i t", t=4)).then_inc(s["g_out"], 1)

                g_chunks(dve, gates_of)

            @block.tensor
            def _(pe):
                pe.wait_ge(s["x1"], TT)
                for k in range(KD):
                    wait(pe, s["u2f"], k - 1)
                    for c in range(TT):
                        ins = pe.transpose(bank[k % 2][:, c * P:(c + 1) * P], x_tm[:, c, k * P:(k + 1) * P], ident[:, :])
                    ins.then_inc(s["tr_mm"], 1)
                pe.wait_ge(s["lo_u2"], KD)
                pe.wait_ge(s["u2f"], KD)

                def products(n, u, g):
                    slot = (n if isinstance(n, int) else u) % 2
                    pe.wait_ge(s["lo"], n + 1)
                    wait(pe, s["h_act"], n - 1)
                    for k in range(KD):
                        ks = slice(k * P, (k + 1) * P)
                        pe.matmul(bank[slot][:, :], whi[:, slot, ks], u2hi[:, k, :], start=(k == 0), stop=False)
                        pe.matmul(bank[slot][:, :], whi[:, slot, ks], u2lo[:, k, :], start=False, stop=False)
                        ins = pe.matmul(bank[slot][:, :], wlo[:, slot, ks], u2hi[:, k, :], start=False,
                                        stop=(k == KD - 1))
                    ins.then_inc(s["h_mm"], 1)
                    if g:
                        pe.wait_ge(s["hot"], n - (QCH + PLAIN - 1))
                        for t in range(TOK):
                            ins = pe.matmul(bank[6 + t // 4][:, (t % 4) * P:(t % 4 + 1) * P], hotB[:, t, :],
                                            hotA[:, t, :], start=True, stop=True)
                            if t % 4 == 3:
                                ins.then_inc(s["g_mm"], 1)

                for n in range(QCH):
                    products(n, 0, False)
                pe.wait_ge(s["keys_in"], 16)
                pe.wait_ge(s["h_act"], QCH)
                for c in range(TT):
                    for b in range(4):
                        wait(pe, s["sc_out"], 4 * (c - 1) + b + 1)
                        for r in range(4):
                            m = 4 * b + r
                            ins = pe.matmul(bank[2 + b][:, r * P:(r + 1) * P], qT[:, m, c * P:(c + 1) * P],
                                            keys[:, m, :], start=True, stop=True)
                        ins.then_inc(s["sc_mm"], 1)
                with pe.Fori(0, PLAIN // UNROLL) as r:
                    for u in range(UNROLL):
                        products(r * UNROLL + (QCH + u), u, False)
                pe.wait_ge(s["gates"], 1)
                pe.wait_ge(s["sc_out"], 4 * TT)
                for w in range(3):
                    for c in range(TT):
                        ins = pe.transpose(bank[2 + w][:, c * P:(c + 1) * P], pk[:, w, c, :], ident[:, :])
                    ins.then_inc(s["pt_mm"], 1)
                g_chunks(pe, products)


def experts(nc, a, x_tm, cond, ident, eps_tile, h_dram, g_dram, out):
    with ExitStack() as ctx:
        def sb(name, shape, dt=F32):
            return ctx.enter_context(nc.sbuf_tensor(name, shape, dt))

        def sem(name):
            return ctx.enter_context(nc.semaphore(name))

        bank = [ctx.enter_context(nc.psum_tensor(f"ex_bank{i}", [P, 512], F32)) for i in range(8)]
        vraw = sb("v_raw", [P, 4, D])
        vhi = sb("v_hi", [P, 2, D], F32R)
        vlo = sb("v_lo", [P, 2, D], F32R)
        hin = sb("h_in", [P, 2, 4, T])
        gin = sb("g_in", [P, 2, T // GT, 4, GT])
        act_f = sb("act", [P, 2, T])
        ahi = sb("act_hi", [P, 2, T], F32R)
        alo = sb("act_lo", [P, 2, T], F32R)
        zero = sb("zero", [P, 512], mybir.dt.bfloat16)
        gate = sb("gate2_row", [P, D])
        lnr = sb("ln2_rows", [P, 2, D])
        t = sb("scratch", [P, 2, D])
        lst = sb("ln2_stats", [P, TT, 2, 6])
        lmv = sb("ln2_mean_var", [P, TT, 2])
        lrs = sb("ln2_rstd", [P, TT])
        v_in = [sem(f"v_in{i}") for i in range(4)]
        h_in = [sem(f"h_in{i}") for i in range(2)]
        g_in = [sem(f"g_in{i}") for i in range(2)]
        s = {n: sem("e_" + n) for n in (
            "zero", "rows_in", "v_hi", "v_lo", "act", "a_hi", "a_lo", "mm", "gate_mm", "gate", "end", "stats", "ln_ln",
            "ln_rstd", "y", "stored", "chain")}

        def each(eng, body):
            for u in range(UNROLL):
                body(u, u)
            with eng.Fori(1, NKEYS // UNROLL) as r:
                for u in range(UNROLL):
                    body(r * UNROLL + u, u)

        with nc.Block() as block:
            @block.sync
            def _(sp):
                def load(n, u):
                    if u % 4 == 0:
                        wait(sp, s["act"], n - 4)
                        half = u // 4
                        sp.dma_start(hin[:, half, :, :], h_dram[bass.ds(n, 4)].rearrange("i p t -> p i t"))\
                            .then_inc(h_in[half], 16)
                        sp.dma_start(gin[:, half, :, :, :],
                                     g_dram[:, :, bass.ds(n, 4), :].rearrange("b p i t -> p b i t"))\
                            .then_inc(g_in[half], 16)
                    wait(sp, s["v_lo"], n - 3)
                    sp.dma_start(vraw[:, u % 4, :], a["v"][n]).then_inc(v_in[u % 4], 16)

                each(sp, load)
                for r, name in enumerate(("ln2_g", "ln2_b")):
                    sp.dma_start(lnr[:, r, :], a[name][0, :].partition_broadcast(P)).then_inc(s["rows_in"], 16)
                for c in range(TT):
                    sp.wait_ge(s["y"], c + 1)
                    sp.dma_start(out[0, c * P:(c + 1) * P, :], x_tm[:, c, :]).then_inc(s["stored"], 16)
                sp.wait_ge(s["stored"], 16 * TT)

            @block.gpsimd
            def _(pool):
                pool.memset(zero[:, :], 0.0).then_inc(s["zero"], 1)

                def split_v_lo(n, u):
                    pool.wait_ge(s["v_hi"], n + 1)
                    wait(pool, s["mm"], n - 1)
                    pool.tensor_tensor(vlo[:, u % 2, :], vraw[:, u % 4, :], vhi[:, u % 2, :].bitcast(F32),
                                       ALU.subtract).then_inc(s["v_lo"], 1)

                each(pool, split_v_lo)

            @block.scalar
            def _(act):
                for h in range(2):
                    act.wait_ge(s["gate_mm"], h + 1)
                    act.activation(gate[:, h * 512:(h + 1) * 512], bank[h][:, :], ACT.Copy).then_inc(s["gate"], 1)

                def split_hi(n, u):
                    act.wait_ge(v_in[u % 4], (n - u + 4 * (u // 4 + 1)) * 4)
                    wait(act, s["mm"], n - 1)
                    act.activation(vhi[:, u % 2, :], vraw[:, u % 4, :], ACT.Copy).then_inc(s["v_hi"], 1)
                    act.wait_ge(s["act"], n + 1)
                    act.activation(ahi[:, u % 2, :], act_f[:, u % 2, :], ACT.Copy).then_inc(s["a_hi"], 1)

                each(act, split_hi)
                for c in range(TT):
                    act.wait_ge(s["stats"], c + 1)
                    act.activation(lrs[:, c:c + 1], lmv[:, c, 1:2], ACT.Ln, bias=eps_tile[:, 1:2])\
                        .then_inc(s["ln_ln"], 1)
                    act.wait_ge(s["ln_ln"], c + 1)
                    act.activation(lrs[:, c:c + 1], lrs[:, c:c + 1], ACT.Exp, scale=-0.5).then_inc(s["ln_rstd"], 1)

            @block.vector
            def _(dve):
                def gated(n, u):
                    half, i = u // 4, u % 4
                    if i == 0:
                        dve.wait_ge(h_in[half], n * 2 + (16 - 2 * u))
                        dve.wait_ge(g_in[half], n * 2 + (16 - 2 * u))
                    dve.tensor_tensor(act_f[:, u % 2, :].rearrange("p (b t) -> p b t", t=GT),
                                      hin[:, half, i, :].rearrange("p (b t) -> p b t", t=GT),
                                      gin[:, half, :, i, :], ALU.mult).then_inc(s["act"], 1)
                    dve.wait_ge(s["a_hi"], n + 1)
                    wait(dve, s["mm"], n - 1)
                    dve.tensor_tensor(alo[:, u % 2, :], act_f[:, u % 2, :], ahi[:, u % 2, :].bitcast(F32),
                                      ALU.subtract).then_inc(s["a_lo"], 1)
                    dve.wait_ge(s["a_lo"], n + 1)

                each(dve, gated)
                links = [0]

                def link(ins):
                    links[0] += 1
                    ins.then_inc(s["chain"], 1)
                    dve.wait_ge(s["chain"], links[0])

                dve.wait_ge(s["end"], 1)
                dve.wait_ge(s["gate"], 2)
                dve.wait_ge(s["rows_in"], 32)
                for c in range(TT):
                    xs = x_tm[:, c, :]
                    for h in range(2):
                        hs = slice(h * 512, (h + 1) * 512)
                        link(dve.tensor_tensor(t[:, c % 2, hs], bank[2 * c + h][:, :], gate[:, hs], ALU.mult))
                    link(dve.scalar_tensor_tensor(out=xs, in0=xs, scalar=ALPHA, in1=t[:, c % 2, :], op0=ALU.mult,
                                                  op1=ALU.add))
                    for h in range(2):
                        ins = dve.bn_stats(lst[:, c, h, :], x_tm[:, c, h * 512:(h + 1) * 512])
                    link(ins)
                    dve.bn_aggr(lmv[:, c, :], lst[:, c, :, :]).then_inc(s["stats"], 1)
                    dve.wait_ge(s["ln_rstd"], c + 1)
                    link(dve.tensor_scalar(xs, xs, lmv[:, c, 0:1], lrs[:, c:c + 1], ALU.subtract, ALU.mult))
                    link(dve.tensor_tensor(xs, xs, lnr[:, 0, :], ALU.mult))
                    dve.tensor_tensor(xs, xs, lnr[:, 1, :], ALU.add).then_inc(s["y"], 1)

            @block.tensor
            def _(pe):
                for m in range(KD):
                    ins = pe.matmul(bank[m // 4][:, (m % 4) * P:(m % 4 + 1) * P],
                                    cond[:, 40 + m:41 + m].to_broadcast([P, P]), ident[:, :], start=True, stop=True)
                    if m % 4 == 3:
                        ins.then_inc(s["gate_mm"], 1)
                pe.wait_ge(s["zero"], 1)
                pe.wait_ge(s["gate"], 2)
                for b in range(8):
                    pe.matmul(bank[b][:, :], zero[:, 0:P], zero[:, :], start=True, stop=False)

                def products(n, u):
                    w = u % 2
                    pe.wait_ge(s["v_lo"], n + 1)
                    pe.wait_ge(s["a_lo"], n + 1)
                    for c in range(TT):
                        ts = slice(c * P, (c + 1) * P)
                        for left, right in ((ahi, vhi), (ahi, vlo), (alo, vhi)):
                            for h in range(2):
                                ins = pe.matmul(bank[2 * c + h][:, :], left[:, w, ts],
                                                right[:, w, h * 512:(h + 1) * 512], start=False, stop=False)
                    ins.then_inc(s["mm"], 1)

                each(pe, products)
                for b in range(8):
                    ins = pe.matmul(bank[b][:, :], zero[:, 0:P], zero[:, :], start=False, stop=True)
                ins.then_inc(s["end"], 1)


def layer(nc, a, out):
    h_dram = nc.dram_tensor("h_dram", (NKEYS, NKEYS, T), F32, kind="Internal").ap()
    g_dram = nc.dram_tensor("g_dram", (T // GT, NKEYS, NKEYS, GT), F32, kind="Internal").ap()
    with ExitStack() as ctx:
        def sb(name, shape):
            return ctx.enter_context(nc.sbuf_tensor(name, shape, F32))

        x_tm, cond = sb("x_tokens", [P, TT, D]), sb("cond", [P, 48])
        ident, eps_tile = sb("identity", [P, P]), sb("eps", [P, 2])
        mixer(nc, a, x_tm, cond, ident, eps_tile)
        router(nc, a, x_tm, cond, ident, eps_tile, h_dram, g_dram)
        experts(nc, a, x_tm, cond, ident, eps_tile, h_dram, g_dram, out)


def laid_out(x, c, w_cond, b_cond, w_in, sc_conv_w, ssm_conv_w, ssm_conv_b, dt_bias, a_log, d_skip, sc_norm_w,
             ssm_norm_w, w_out, ln1_g, ln1_b, w_query, sub_keys1, sub_keys2, expert_u, expert_v, ln2_g, ln2_b):
    import numpy as np

    def blocks(w, n):
        return w.reshape(KD, P, n, -1).transpose(2, 1, 0, 3)

    def columns(v):
        return v.reshape(-1, P).T

    w = w_in[0]
    keys = np.stack([sub_keys1[0], sub_keys2[0]], axis=1).reshape(2 * HEADS, NKEYS, P)
    arrays = {
        "x": x, "xT": x[0].T.reshape(KD, P, T).transpose(1, 0, 2), "cT": columns(c[0]),
        "w_cond": blocks(w_cond[0], 48), "b_condT": columns(b_cond[0]),
        "w_sc": w[:, 0:3 * D].reshape(KD, P, 3, NSC, P)[:, :, [1, 2, 0]].transpose(3, 2, 1, 0, 4)
        .reshape(3 * NSC, P, KD, P),
        "w_z": w[:, 3 * D:4 * D].reshape(4, 2, P, 2, 512).transpose(3, 0, 2, 1, 4).reshape(8, P, 2, 512),
        "w_xbc": blocks(w[:, 4 * D:4 * D + KX * P], KX),
        "w_dt": w[:, 4 * D + KX * P:].reshape(KD, P, SH).transpose(1, 0, 2),
        "sc_conv_wT": sc_conv_w[0].reshape(K_SC, NSC, P).transpose(2, 1, 0),
        "ssm_conv_wT": ssm_conv_w[0].reshape(K_SSM, KX, P).transpose(2, 1, 0),
        "ssm_conv_bT": columns(ssm_conv_b[0]), "sc_norm_wT": columns(sc_norm_w[0]),
        "ssm_norm_wT": columns(ssm_norm_w[0]), "dt_bias": dt_bias, "a_log": a_log, "d_skip": d_skip,
        "w_out": w_out[0].reshape(16, P, 1, D),
        "ln1_g": ln1_g, "ln1_b": ln1_b, "ln2_g": ln2_g, "ln2_b": ln2_b,
        "w_query": blocks(w_query[0], 2 * HEADS), "keysT": keys.transpose(2, 0, 1),
        "u_T": expert_u[0].reshape(NKEYS, NKEYS, KD, P).transpose(0, 3, 2, 1), "v": expert_v[0].reshape(NKEYS, NKEYS, D),
    }
    return {k: np.ascontiguousarray(v) for k, v in arrays.items()}


def kernel(**inputs):
    import numpy as np
    import concourse.bacc as bacc
    from concourse.bass_utils import run_bass_kernel_spmd

    arrays = laid_out(**{k: np.asarray(v) for k, v in inputs.items()})
    nc = bacc.Bacc("TRN2", target_bir_lowering=False, num_devices=1)
    a = {n: nc.dram_tensor("in_" + n, v.shape, F32, kind="ExternalInput").ap() for n, v in arrays.items()}
    out = nc.dram_tensor("out", (1, T, D), F32, kind="ExternalOutput").ap()
    layer(nc, a, out)
    r = run_bass_kernel_spmd(nc, [{"in_" + n: v for n, v in arrays.items()}], core_ids=[0])
    return r.results[0]["out"]
```

```python
from contextlib import ExitStack

import concourse.bass as bass
from concourse import mybir

F32 = mybir.dt.float32
F32R = mybir.dt.float32r
U32 = mybir.dt.uint32
ALU = mybir.AluOpType
ACT = mybir.ActivationFunctionType
AX_X = mybir.AxisListType.X

P = 128
T, D = 512, 1024
TT, KD = T // P, D // P
HD = 64
SH = 16
NG = 2
HPG = SH // NG
GW = HPG * HD
KX = 12
NSC = 8
K_SC, K_SSM = 3, 4
HEADS, TOPK, NKEYS = 8, 16, 128
PICKS = HEADS * TOPK
LN_EPS, RMS_EPS = 1e-5, 1e-6
ALPHA = 2.0 ** 0.25
FLOOR = -3.0e38
RAW = 4
CSLOTS = 8


def mixer(nc, a, x_tm, cond, fold, ident, eps_tile, ln, rows_dram):
    with ExitStack() as ctx:
        def sb(name, shape, dt=F32):
            return ctx.enter_context(nc.sbuf_tensor(name, shape, dt))

        def sem(name):
            return ctx.enter_context(nc.semaphore(name))

        bank = [ctx.enter_context(nc.psum_tensor(f"mix_bank{i}", [P, 512], F32)) for i in range(8)]
        u1hi = sb("u1_hi", [P, KD, T], F32R)
        u1lo = sb("u1_lo", [P, KD, T], F32R)
        raw = sb("w_raw", [P, RAW, D])
        whi = sb("w_hi", [P, 2, D], F32R)
        wlo = sb("w_lo", [P, 2, D], F32R)
        xbcT = sb("xbcT", [P, KX, T])
        ymixT = sb("ymixT", [P, 16, T])
        zs = sb("z_silu", [P, TT, D])
        x_c = sb("x_chunk", [P, D])
        xdt = sb("x_dt", [P, D])
        xde = sb("x_dt_end", [P, D])
        state = sb("ssm_state", [P, D])
        y = sb("y_chunk", [P, D])
        craw = ymixT[:, 0:2 * CSLOTS, :].rearrange("p (s h) t -> p s (h t)", h=2)
        cmore = (xbcT[:, :, :].rearrange("p (s h) t -> p s (h t)", h=2), zs[:, :, :])
        csum = state[:, :].rearrange("p (s n) -> p s n", n=P)
        btm = sb("b_tokens", [P, NG * P])
        cbm = sb("cb_masked", [P, NG, P])
        pad = sb("conv_in", [P, 2, T + K_SSM - 1])
        conv = sb("conv_out", [P, 2, T])
        csb = sb("sc_c_copy", [P, T])
        ysq = sb("sc_square", [P, T])
        rs = sb("sc_rstd", [P, T])
        tri = sb("causal", [P, P])
        ones = sb("ones", [P, P])
        grp = sb("head_mean", [P, P])
        cact = sb("c_act", [P, 2, KD])
        bcond = sb("b_cond", [P, 48])
        scw = sb("sc_conv_w", [P, NSC, K_SC])
        ssw = sb("ssm_conv_w", [P, KX, K_SSM])
        ssb = sb("ssm_conv_b", [P, KX])
        scn = sb("sc_norm_w", [P, NSC])
        ssn = sb("ssm_norm_w", [P, NSC])
        ln1 = sb("ln1_columns", [P, 2, KD])
        wdt = sb("w_dt", [P, KD, SH])
        wdthi = sb("w_dt_hi", [P, KD, SH], F32R)
        wdtlo = sb("w_dt_lo", [P, KD, SH], F32R)
        rows = sb("head_rows", [P, 3, SH])
        dtb = y[:, 0:8 * TT * SH].rearrange("p (r c h) -> p r c h", c=TT, h=SH)
        dt = sb("dt", [P, TT, SH])
        adt = sb("a_dt", [P, TT, SH])
        cums = sb("cums", [P, 3, TT, SH])
        cumsT = sb("cums_T", [TT * SH, P])
        ecums = sb("exp_cums", [P, 3, TT, SH])
        ssum = sb("y_square_sum", [P, 2, NG])
        with nc.sbuf_tensor("decay", [P, SH, P], F32) as decay:
            pass
        yhi = sb("ymix_hi", [P, 2, T], F32R)
        ylo = sb("ymix_lo", [P, 2, T], F32R)
        mixed = (y, xdt)
        xT = x_tm[:, :, :].rearrange("p c d -> p (c d)").rearrange("p (k t) -> p k t", t=T)

        loaded = [sem(f"w_loaded{i}") for i in range(RAW)]
        c_loaded = [sem(f"cond_loaded{i}") for i in range(2 * CSLOTS)]
        x_loaded = [sem(f"xT_loaded{i}") for i in range(2)]
        s = {n: sem("m_" + n) for n in (
            "x_in", "c_in", "par_in", "consts", "pads_zero", "cact", "cond_sum", "cond_mm",
            "cond_out", "u1", "u1hi", "u1lo", "hi", "lo", "unit", "wdt_hi", "wdt_lo", "xbc_copied", "conv_done",
            "xbc_act", "dt_rows", "dt_copied", "dt_mm", "dt_x", "dt_exp", "dt_w", "dt_ln", "adt", "z_out", "cum_mm", "cums", "ecums",
            "c_copied", "h_used", "ysc", "ysq", "mean_mm", "mean_out", "rstd", "ysc_norm", "xtr_mm", "x_copied",
            "xdt", "xde", "xskip", "cumT_mm", "cumT", "rows_in", "seg", "dexp", "cb_mm", "btm", "cbm", "weights", "st_mm", "st_out",
            "yd_mm", "yo_mm", "yo_out", "y_gated", "ysum", "yln", "yrstd", "yn", "ytr_mm", "yT", "gate_mm", "gate",
            "yhi", "ylo", "tile_mm", "mixed", "x_scaled", "out", "stats", "ln_ln", "ln_rstd", "shift", "chain")}

        XBC0, Z0, SC0 = 0, KX, KX + NG * 4
        OUT0 = SC0 + 3 * NSC
        UNITS = OUT0 + 16
        CA, CB = 16, 32
        PA, PX, PZ = CA // 2, KX // 2, CB // 2 - KX // 2

        def unit_dram(n):
            if n < Z0:
                return a["w_xbc"][n]
            if n < SC0:
                return a["w_z"][n - Z0]
            if n < OUT0:
                return a["w_sc"][n - SC0]
            return a["w_out"][n - OUT0]

        def pairs_at(n):
            if n < KX:
                return range(PA + n // 2, PA + (n + 1) // 2)
            return range(PA + PX + PZ * (n - KX) // (SC0 - KX), PA + PX + PZ * (n - KX + 1) // (SC0 - KX))

        def on_pe(q):
            return q in (1, 3, 5)

        def sums(q):
            return sum(not on_pe(u) for u in range(q + 1))

        def cond_slot(i):
            if i < CSLOTS:
                return craw, i, c_loaded[i], 16
            if i < 2 * CSLOTS:
                first = i - CSLOTS < KX // 2
                return cmore[not first], i - CSLOTS if first else i - CSLOTS - KX // 2, c_loaded[i], 16
            return craw, i % CSLOTS, c_loaded[i % CSLOTS], 16 * (i // CSLOTS)

        def cs(c):
            return slice(c * P, (c + 1) * P)

        def per_head(ap, c, g):
            return ap[:, c, g * HPG:(g + 1) * HPG].unsqueeze(2).to_broadcast([P, HPG, HD])

        def heads(ap):
            return ap.rearrange("p (h d) -> p h d", d=HD)

        with nc.Block() as block:
            @block.sync
            def _(sp):
                sp.dma_start(cact[:, 0, :], a["cT"]).then_inc(s["c_in"], 16)

                def load_cond(i):
                    if i >= CA:
                        sp.wait_ge(s["cond_mm"], (i % CSLOTS if i < CA + CSLOTS else i - CSLOTS) + 1)
                    region, slot, arrived, _ = cond_slot(i)
                    sp.dma_start(region[:, slot, :], a["w_cond"][i].rearrange("p k n -> p (k n)")).then_inc(arrived, 16)

                for i in range(CA):
                    load_cond(i)
                for n in range(UNITS):
                    if n >= RAW:
                        sp.wait_ge(s["lo"], n - RAW + 1)
                    sp.dma_start(raw[:, n % RAW, :], unit_dram(n).rearrange("p k n -> p (k n)"))\
                        .then_inc(loaded[n % RAW], 16)
                    if n == 0:
                        for h in range(2):
                            ks = slice(4 * h, 4 * h + 4)
                            sp.dma_start(xT[:, ks, :], a["xT"][:, ks, :]).then_inc(x_loaded[h], 16)
                    if n < SC0:
                        for q in pairs_at(n):
                            load_cond(2 * q)
                            load_cond(2 * q + 1)
                    if n == SC0:
                        sp.wait_ge(s["u1lo"], KD)
                        sp.dma_start(x_tm[:, :, :], a["x"].rearrange("b (c p) d -> p (b c) d", p=P))\
                            .then_inc(s["x_in"], 16)

            @block.gpsimd
            def _(pool):
                pool.memset(ident[:, :], 0.0).then_inc(s["consts"], 1)
                pool.memset(tri[:, :], 1.0).then_inc(s["consts"], 1)
                pool.memset(ones[:, :], 1.0).then_inc(s["consts"], 1)
                pool.memset(grp[:, :], 0.0).then_inc(s["consts"], 1)
                pool.wait_ge(s["consts"], 4)
                pool.memset(grp[0:HD, 0:HD], 1.0 / HD).then_inc(s["consts"], 1)
                pool.wait_ge(s["consts"], 5)
                pool.memset(grp[HD:P, HD:P], 1.0 / HD).then_inc(s["consts"], 1)
                pool.wait_ge(s["consts"], 6)
                pool.affine_select(out=ident[:, :], in_=ident[:, :], compare_op=ALU.not_equal, fill=1.0, base=0,
                                   pattern=[[-1, P]], channel_multiplier=1).then_inc(s["consts"], 1)
                pool.affine_select(out=tri[:, :], in_=tri[:, :], compare_op=ALU.is_ge, fill=0.0, base=0,
                                   pattern=[[1, P]], channel_multiplier=-1).then_inc(s["consts"], 1)
                pool.wait_ge(s["wdt_hi"], 1)
                pool.tensor_tensor(wdtlo[:, :, :], wdt[:, :, :], wdthi[:, :, :].bitcast(F32), ALU.subtract)\
                    .then_inc(s["wdt_lo"], 1)

                def split_lo(n):
                    pool.wait_ge(s["hi"], n + 1)
                    if n >= 2:
                        pool.wait_ge(s["unit"], n - 1)
                    pool.tensor_tensor(wlo[:, n % 2, :], raw[:, n % RAW, :], whi[:, n % 2, :].bitcast(F32),
                                       ALU.subtract).then_inc(s["lo"], 1)

                def leaving(c):
                    pool.wait_ge(s["ecums"], 1)
                    pool.wait_ge(s["xdt"], NG * c + NG)
                    if c:
                        pool.wait_ge(s["st_mm"], NG * c)
                    for g in range(NG):
                        pool.tensor_tensor(heads(xde[:, g * GW:(g + 1) * GW]), heads(xdt[:, g * GW:(g + 1) * GW]),
                                           per_head(ecums[:, 2], c, g), ALU.mult).then_inc(s["xde"], 1)

                def skip(c):
                    for g in range(NG):
                        pool.tensor_tensor(heads(x_c[:, g * GW:(g + 1) * GW]), heads(x_c[:, g * GW:(g + 1) * GW]),
                                           rows[:, 2, g * HPG:(g + 1) * HPG].unsqueeze(2).to_broadcast([P, HPG, HD]),
                                           ALU.mult).then_inc(s["xskip"], 1)

                for n in range(SC0):
                    split_lo(n)
                split_lo(SC0)
                split_lo(SC0 + 1)
                pool.wait_ge(s["par_in"], 16 * 12)
                for j in range(NSC):
                    n = SC0 + 3 * j
                    split_lo(n + 2)
                    split_lo(n + 3)
                    split_lo(n + 4)
                    if j % 2 == 0:
                        leaving(j // 2)
                        skip(j // 2)
                for n in range(OUT0 + 2, UNITS):
                    split_lo(n)
                for c in range(1, TT - 1):
                    pool.wait_ge(s["x_scaled"], c + 1)
                    pool.wait_ge(s["out"], c)
                    pool.wait_ge(s["mixed"], 2 * c + 2)
                    pool.tensor_tensor(x_tm[:, c, :], x_tm[:, c, :], mixed[c % 2][:, :], ALU.add).then_inc(s["out"], 1)

            @block.scalar
            def _(act):
                act.wait_ge(s["c_in"], 16)
                act.activation(cact[:, 1, :], cact[:, 0, :], ACT.Silu).then_inc(s["cact"], 1)
                act.dma_start(bcond[:, :], a["b_condT"]).then_inc(s["par_in"], 16)
                act.dma_start(scw[:, :, :], a["sc_conv_wT"]).then_inc(s["par_in"], 16)
                act.dma_start(ssw[:, :, :], a["ssm_conv_wT"]).then_inc(s["par_in"], 16)
                act.dma_start(ssb[:, :], a["ssm_conv_bT"]).then_inc(s["par_in"], 16)
                act.dma_start(scn[:, :], a["sc_norm_wT"]).then_inc(s["par_in"], 16)
                act.dma_start(ssn[:, :], a["ssm_norm_wT"]).then_inc(s["par_in"], 16)
                for r, name in enumerate(("dt_bias", "a_log", "d_skip")):
                    act.dma_start(rows[:, r, :], a[name][0, :].partition_broadcast(P)).then_inc(s["par_in"], 16)
                act.dma_start(ln1[:, 0, :], a["ln1_gT"]).then_inc(s["par_in"], 16)
                act.dma_start(ln1[:, 1, :], a["ln1_bT"]).then_inc(s["par_in"], 16)
                act.dma_start(wdt[:, :, :], a["w_dt"]).then_inc(s["par_in"], 16)
                act.wait_ge(s["par_in"], 16 * 12)
                act.activation(wdthi[:, :, :], wdt[:, :, :], ACT.Copy).then_inc(s["wdt_hi"], 1)
                act.wait_ge(s["par_in"], 16 * 12)

                def split_hi(n):
                    if n >= UNITS:
                        return
                    act.wait_ge(loaded[n % RAW], 16 * (n // RAW + 1))
                    if n >= 2:
                        act.wait_ge(s["unit"], n - 1)
                    act.activation(whi[:, n % 2, :], raw[:, n % RAW, :], ACT.Copy).then_inc(s["hi"], 1)

                split_hi(0)
                for k in range(KD):
                    act.wait_ge(s["u1"], k + 1)
                    act.activation(u1hi[:, k, :], xT[:, k, :], ACT.Copy).then_inc(s["u1hi"], 1)
                    if k == 1:
                        split_hi(1)

                def conv_silu(m):
                    act.wait_ge(s["conv_done"], m + 1)
                    act.activation(xbcT[:, m, :], conv[:, m % 2, :], ACT.Silu, bias=ssb[:, m:m + 1])\
                        .then_inc(s["xbc_act"], 1)

                act.wait_ge(s["pads_zero"], 1)
                for m in range(KX):
                    split_hi(XBC0 + m + 1) if m else None
                    act.wait_ge(s["unit"], XBC0 + m + 1)
                    if m >= 2:
                        act.wait_ge(s["conv_done"], m - 1)
                    act.activation(pad[:, m % 2, K_SSM - 1:], bank[m % 4][:, :], ACT.Copy).then_inc(s["xbc_copied"], 1)
                    if m:
                        conv_silu(m - 1)
                split_hi(Z0 + 1)
                act.wait_ge(s["dt_rows"], 1)
                act.activation(x_c[0:SH, 0:T], bank[4][0:SH, :], ACT.Copy).then_inc(s["dt_copied"], 1)
                conv_silu(KX - 1)
                for n in range(Z0, SC0):
                    if n > Z0:
                        split_hi(n + 1)
                    if (n - Z0) % 4 == 3:
                        half = (n - Z0) // 4
                        act.wait_ge(s["unit"], n + 1)
                        for c in range(TT):
                            if c == 1 and n == SC0 - 1:
                                split_hi(SC0 + 1)
                            act.activation(zs[:, c, half * 512:(half + 1) * 512], bank[c][:, :], ACT.Silu)\
                                .then_inc(s["z_out"], 1)
                act.wait_ge(s["dt_x"], 2)
                act.activation(dtb[:, 2], dtb[:, 1], ACT.Exp).then_inc(s["dt_exp"], 1)
                act.activation(dtb[:, 7, 0, :], rows[:, 1, :], ACT.Exp).then_inc(s["dt_exp"], 1)
                act.wait_ge(s["dt_w"], 1)
                act.activation(dtb[:, 4], dtb[:, 3], ACT.Ln).then_inc(s["dt_ln"], 1)
                act.preload_act_table_set("natural_log_exp_and_others")
                eps_rms = eps_tile[:, 0:1]

                def sc_rstd(j):
                    act.wait_ge(s["mean_mm"], j + 1)
                    if j:
                        act.wait_ge(s["ysc_norm"], j)
                    act.activation(rs[:, :], bank[5][:, :], ACT.Ln, bias=eps_rms).then_inc(s["mean_out"], 1)
                    act.wait_ge(s["mean_out"], j + 1)
                    act.activation(rs[:, :], rs[:, :], ACT.Exp, scale=-0.5).then_inc(s["rstd"], 1)

                def split_y(k):
                    if k >= NSC:
                        act.wait_ge(s["yT"], NG * TT)
                    act.wait_ge(s["ysc_norm"], min(k + 1, NSC))
                    if k >= 2:
                        act.wait_ge(s["unit"], OUT0 + k - 1)
                    act.activation(yhi[:, k % 2, :], ymixT[:, k, :], ACT.Copy).then_inc(s["yhi"], 1)

                def load_rows(c):
                    act.dma_start(decay[:, :, :].rearrange("p h l -> p (h l)"),
                                  rows_dram[c].rearrange("h l -> (h l)").partition_broadcast(P))\
                        .then_inc(s["rows_in"], 16)

                def chunk_copies(c):
                    for g in range(NG):
                        act.wait_ge(s["xtr_mm"], NG * c + g + 1)
                        if c:
                            act.wait_ge(s["y_gated"], c)
                            act.wait_ge(s["ysum"], NG * c)
                        act.activation(x_c[:, g * 512:(g + 1) * 512], bank[3 + g][:, :], ACT.Copy)\
                            .then_inc(s["x_copied"], 1)
                    act.wait_ge(s["cb_mm"], c + 1)
                    if c:
                        act.wait_ge(s["st_mm"], NG * c)
                    act.activation(btm[:, :], bank[5][:, 0:NG * P], ACT.Copy).then_inc(s["btm"], 1)

                def decays(c):
                    for q in range(4):
                        act.wait_ge(s["seg"], 4 * c + q + 1)
                        act.activation(decay[:, 4 * q:4 * q + 4, :], decay[:, 4 * q:4 * q + 4, :], ACT.Exp)\
                            .then_inc(s["dexp"], 1)

                def chunk_rstd(c):
                    act.wait_ge(s["y_gated"], c + 1)
                    for g in range(NG):
                        act.activation(x_c[:, g * GW:(g + 1) * GW], y[:, g * GW:(g + 1) * GW], ACT.Square,
                                       accum_out=ssum[:, 0, g:g + 1]).then_inc(s["ysum"], 1)
                    act.wait_ge(s["ysum"], NG * c + NG)
                    if c:
                        act.wait_ge(s["yn"], c)
                    act.activation(ssum[:, 1, :], ssum[:, 0, :], ACT.Ln, scale=1.0 / GW, bias=eps_rms)\
                        .then_inc(s["yln"], 1)
                    act.wait_ge(s["yln"], c + 1)
                    act.activation(ssum[:, 1, :], ssum[:, 1, :], ACT.Exp, scale=-0.5).then_inc(s["yrstd"], 1)

                for j in range(NSC):
                    n = SC0 + 3 * j
                    if j % 2:
                        decays(j // 2)
                    elif j:
                        chunk_rstd(j // 2 - 1)
                        load_rows(j // 2)
                    split_hi(n + 2)
                    act.wait_ge(s["unit"], n + 1)
                    if j:
                        act.wait_ge(s["h_used"], j)
                    act.activation(csb[:, :], bank[0][:, :], ACT.Copy).then_inc(s["c_copied"], 1)
                    if j:
                        sc_rstd(j - 1)
                    split_hi(n + 3)
                    split_hi(n + 4)
                    if j == 0:
                        act.wait_ge(s["cumT_mm"], 1)
                        act.activation(cumsT[:, :], bank[6][0:TT * SH, 0:P], ACT.Copy).then_inc(s["cumT"], 1)
                        act.wait_ge(s["cumT"], 1)
                        act.dma_start(rows_dram.rearrange("c h l -> (c h) l"), cumsT[:, :]).then_inc(s["rows_in"], 16)
                    if j == NSC - 1:
                        chunk_rstd(TT - 1)
                        split_y(0)
                    act.wait_ge(s["ysc"], j + 1)
                    if j:
                        act.wait_ge(s["mean_mm"], j)
                    act.activation(ysq[:, :], ymixT[:, j, :], ACT.Square).then_inc(s["ysq"], 1)
                    if j == 0:
                        act.wait_ge(s["rows_in"], 16)
                        load_rows(0)
                        act.wait_ge(s["cums"], 2)
                        act.activation(ecums[:, :, :, :], cums[:, :, :, :], ACT.Exp).then_inc(s["ecums"], 1)
                    if j % 2 == 0:
                        chunk_copies(j // 2)
                for h in range(2):
                    act.wait_ge(s["gate_mm"], h + 1)
                    act.activation(state[:, h * 512:(h + 1) * 512], bank[6 + h][:, :], ACT.Copy)\
                        .then_inc(s["gate"], 1)

                sc_rstd(NSC - 1)
                split_y(1)
                act.wait_ge(s["x_in"], 16)
                for k in range(2, 16):
                    split_hi(OUT0 + k)
                    split_y(k)
                    if k - 4 in range(TT):
                        act.activation(x_tm[:, k - 4, :], x_tm[:, k - 4, :], ACT.Copy, scale=ALPHA)\
                            .then_inc(s["x_scaled"], 1)

                def ln_rstd(c):
                    act.wait_ge(s["stats"], c + 1)
                    act.activation(ln["rstd"][:, c:c + 1], ln["mv"][:, c, 1:2], ACT.Ln, bias=eps_tile[:, 1:2])\
                        .then_inc(s["ln_ln"], 1)
                    act.wait_ge(s["ln_ln"], c + 1)
                    act.activation(ln["rstd"][:, c:c + 1], ln["rstd"][:, c:c + 1], ACT.Exp, scale=-0.5)\
                        .then_inc(s["ln_rstd"], 1)

                ln_rstd(0)
                for c in range(TT):
                    if c + 1 < TT:
                        ln_rstd(c + 1)
                    act.wait_ge(s["shift"], c + 1)
                    act.activation(x_tm[:, c, :], x_tm[:, c, :], ACT.Identity, scale=ln["rstd"][:, c:c + 1],
                                   bias=ln["shift"][:, c:c + 1])

            @block.vector
            def _(dve):
                links = [0]

                def link(ins):
                    links[0] += 1
                    ins.then_inc(s["chain"], 1)
                    dve.wait_ge(s["chain"], links[0])

                link(dve.memset(eps_tile[:, 0:1], RMS_EPS))
                link(dve.memset(eps_tile[:, 1:2], LN_EPS))
                dve.memset(pad[:, :, 0:K_SSM - 1], 0.0).then_inc(s["pads_zero"], 1)
                dve.wait_ge(s["cact"], 1)

                def sum_pair(q):
                    if on_pe(q):
                        return
                    i, cslot = 2 * q, 2 * q % CSLOTS
                    region, slot, arrived, count = cond_slot(i)
                    dve.wait_ge(arrived, count)
                    dve.wait_ge(cond_slot(i + 1)[2], count)
                    if i >= CSLOTS:
                        dve.wait_ge(s["cond_mm"], i - CSLOTS + 2)
                    o = csum[:, cslot:cslot + 2, :]
                    link(dve.tensor_scalar(o, region[:, slot:slot + 2, 0:P], cact[:, 1, 0:1], None, ALU.mult))
                    for k in range(1, KD):
                        ins = dve.scalar_tensor_tensor(out=o, in0=region[:, slot:slot + 2, k * P:(k + 1) * P],
                                                       scalar=cact[:, 1, k:k + 1], in1=o, op0=ALU.mult, op1=ALU.add)
                        if k < KD - 1:
                            link(ins)
                    ins.then_inc(s["cond_sum"], 1)

                for q in range(PA):
                    sum_pair(q)
                dve.wait_ge(s["par_in"], 16 * 12)
                dve.wait_ge(s["cond_mm"], CA)
                dve.tensor_tensor(cond[:, 0:CA], bank[5][:, 0:CA], bcond[:, 0:CA], ALU.add).then_inc(s["cond_out"], 1)
                dve.wait_ge(s["cond_out"], 1)
                link(dve.tensor_scalar(cond[:, 8:16], cond[:, 8:16], 1.0, None, ALU.add))

                def u1_lo(k):
                    dve.wait_ge(s["u1hi"], k + 1)
                    dve.tensor_tensor(u1lo[:, k, :], xT[:, k, :], u1hi[:, k, :].bitcast(F32), ALU.subtract)\
                        .then_inc(s["u1lo"], 1)

                for k in range(KD):
                    dve.wait_ge(x_loaded[k // 4], 16)
                    dve.tensor_scalar(xT[:, k, :], xT[:, k, :], cond[:, 8 + k:9 + k], cond[:, k:k + 1],
                                      ALU.mult, ALU.add).then_inc(s["u1"], 1)
                    if k:
                        u1_lo(k - 1)
                u1_lo(KD - 1)
                for m in range(KX):
                    for q in pairs_at(XBC0 + m):
                        sum_pair(q)
                    dve.wait_ge(s["xbc_copied"], m + 1)
                    if m >= 2:
                        dve.wait_ge(s["xbc_act"], m - 1)
                    o = conv[:, m % 2, :]
                    link(dve.tensor_scalar(o, pad[:, m % 2, 0:T], ssw[:, m, 0:1], None, ALU.mult))
                    for k in range(1, K_SSM):
                        ins = dve.scalar_tensor_tensor(out=o, in0=pad[:, m % 2, k:k + T], scalar=ssw[:, m, k:k + 1],
                                                       in1=o, op0=ALU.mult, op1=ALU.add)
                        if k < K_SSM - 1:
                            link(ins)
                    ins.then_inc(s["conv_done"], 1)
                dve.wait_ge(s["dt_mm"], 1)
                link(dve.tensor_tensor(dtb[:, 0], bank[6][:, 0:TT * SH].rearrange("p (c h) -> p c h", h=SH),
                                       rows[:, 0:1, :].to_broadcast([P, TT, SH]), ALU.add))
                dve.tensor_scalar(dtb[:, 5], dtb[:, 0], -1.0, None, ALU.mult).then_inc(s["dt_x"], 1)
                dve.wait_ge(s["dt_x"], 1)
                dve.tensor_tensor(dtb[:, 1], dtb[:, 0], dtb[:, 5], ALU.min).then_inc(s["dt_x"], 1)
                for n in range(Z0, SC0):
                    for q in pairs_at(n):
                        sum_pair(q)
                dve.wait_ge(s["cond_mm"], CA + CB)
                dve.tensor_tensor(cond[:, CA:48], bank[5][:, CA:48], bcond[:, CA:48], ALU.add).then_inc(s["cond_out"], 1)
                dve.wait_ge(s["cond_out"], 2)
                for lo in (16, 32, 40):
                    dve.tensor_scalar(cond[:, lo:lo + 8], cond[:, lo:lo + 8], 1.0, None, ALU.add)\
                        .then_inc(s["cond_out"], 1)
                dve.wait_ge(s["cond_out"], 5)
                link(dve.tensor_tensor(fold[:, 0, :], ln1[:, 0, :], cond[:, 32:40], ALU.mult))
                link(dve.tensor_tensor(fold[:, 1, :], ln1[:, 1, :], cond[:, 32:40], ALU.mult))
                link(dve.tensor_tensor(fold[:, 1, :], fold[:, 1, :], cond[:, 24:32], ALU.add))
                dve.wait_ge(s["dt_exp"], 2)
                dve.tensor_scalar(dtb[:, 3], dtb[:, 2], 1.0, None, ALU.add).then_inc(s["dt_w"], 1)
                dve.wait_ge(s["dt_w"], 1)
                link(dve.tensor_scalar(dtb[:, 5], dtb[:, 3], -1.0, None, ALU.add))
                link(dve.tensor_tensor(dtb[:, 6], dtb[:, 2], dtb[:, 5], ALU.subtract))
                link(dve.reciprocal(dtb[:, 5], dtb[:, 3]))
                link(dve.tensor_tensor(dtb[:, 6], dtb[:, 6], dtb[:, 5], ALU.mult))
                link(dve.tensor_scalar(dtb[:, 5], dtb[:, 0], 0.0, None, ALU.max))
                link(dve.tensor_tensor(dtb[:, 6], dtb[:, 6], dtb[:, 5], ALU.add))
                dve.wait_ge(s["dt_ln"], 1)
                link(dve.tensor_tensor(dt[:, :, :], dtb[:, 4], dtb[:, 6], ALU.add))
                link(dve.tensor_tensor(dtb[:, 5], dt[:, :, :], dtb[:, 7, 0:1, :].to_broadcast([P, TT, SH]), ALU.mult))
                dve.tensor_scalar(adt[:, :, :], dtb[:, 5], -1.0, None, ALU.mult).then_inc(s["adt"], 1)
                def sc_conv(j):
                    n = SC0 + 3 * j
                    dve.wait_ge(s["unit"], n + 2)
                    dve.wait_ge(s["c_copied"], j + 1)
                    dve.tensor_tensor(pad[:, j % 2, K_SSM - 1:], bank[1][:, :], csb[:, :], ALU.mult)\
                        .then_inc(s["h_used"], 1)
                    dve.wait_ge(s["h_used"], j + 1)
                    o = conv[:, j % 2, :]
                    for k in range(K_SC):
                        src = pad[:, j % 2, K_SSM - K_SC + k:K_SSM - K_SC + k + T]
                        if k == 0:
                            link(dve.tensor_scalar(o, src, scw[:, j, 0:1], None, ALU.mult))
                        else:
                            link(dve.scalar_tensor_tensor(out=o, in0=src, scalar=scw[:, j, k:k + 1], in1=o,
                                                          op0=ALU.mult, op1=ALU.add))

                def sc_out(j):
                    dve.wait_ge(s["unit"], SC0 + 3 * j + 3)
                    dve.tensor_tensor(ymixT[:, j, :], bank[2][:, :], conv[:, j % 2, :], ALU.mult)\
                        .then_inc(s["ysc"], 1)

                def sc_norm(j):
                    dve.wait_ge(s["rstd"], j + 1)
                    dve.scalar_tensor_tensor(out=ymixT[:, j, :], in0=ymixT[:, j, :], scalar=scn[:, j:j + 1],
                                             in1=rs[:, :], op0=ALU.mult, op1=ALU.mult).then_inc(s["ysc_norm"], 1)

                def part1(c):
                    for g in range(NG):
                        dve.wait_ge(s["x_copied"], NG * c + g + 1)
                        if c:
                            dve.wait_ge(s["xde"], NG * c)
                        dve.tensor_tensor(heads(xdt[:, g * GW:(g + 1) * GW]), heads(x_c[:, g * GW:(g + 1) * GW]),
                                          per_head(dt, c, g), ALU.mult).then_inc(s["xdt"], 1)
                    dve.wait_ge(s["btm"], c + 1)
                    dve.tensor_tensor(cbm[:, :, :], bank[5][:, 256:512].rearrange("p (g l) -> p g l", g=NG),
                                      tri[:, :].unsqueeze(1).to_broadcast([P, NG, P]), ALU.mult)\
                        .then_inc(s["cbm"], 1)
                    dve.wait_ge(s["rows_in"], 16 * (c + 2))
                    for h in range(SH):
                        ins = dve.tensor_scalar(decay[:, h, :], decay[:, h, :], cums[:, 0, c, h:h + 1], 0.0,
                                                ALU.subtract, ALU.min)
                        if h % 4 == 3:
                            ins.then_inc(s["seg"], 1)

                def chunk_weights(c):
                    for g in range(NG):
                        dve.wait_ge(s["dexp"], 4 * c + 2 * g + 2)
                        dve.wait_ge(s["cbm"], c + 1)
                        dg = decay[:, g * HPG:(g + 1) * HPG, :]
                        dve.tensor_tensor(dg, dg, cbm[:, g, :].unsqueeze(1).to_broadcast([P, HPG, P]), ALU.mult)\
                            .then_inc(s["weights"], 1)

                def state_update(c, g):
                    st = state[:, g * GW:(g + 1) * GW]
                    if c:
                        dve.wait_ge(s["yo_mm"], NG * (c - 1) + g + 1)
                        link(dve.tensor_tensor(heads(st), heads(st), per_head(ecums[:, 1], c, g), ALU.mult))
                        dve.wait_ge(s["st_mm"], NG * c + g + 1)
                        dve.tensor_tensor(st, st, bank[5][:, :], ALU.add).then_inc(s["st_out"], 1)
                    else:
                        dve.wait_ge(s["st_mm"], g + 1)
                        dve.tensor_copy(st, bank[5][:, :]).then_inc(s["st_out"], 1)
                    dve.wait_ge(s["st_out"], NG * c + g + 1)

                def part2(c):
                    if c < TT - 1:
                        state_update(c, 0)
                    if c:
                        dve.wait_ge(s["ytr_mm"], NG * c)
                        for g in range(NG):
                            dve.wait_ge(s["yo_mm"], NG * (c - 1) + g + 1)
                            dve.tensor_tensor(heads(y[:, g * GW:(g + 1) * GW]), heads(bank[6 + g][:, :]),
                                              per_head(ecums[:, 0], c, g), ALU.mult).then_inc(s["yo_out"], 1)
                        dve.wait_ge(s["yo_out"], NG * c)
                        for g in range(NG):
                            dve.wait_ge(s["yd_mm"], NG * c + g + 1)
                            yg = y[:, g * GW:(g + 1) * GW]
                            link(dve.tensor_tensor(yg, yg, bank[3 + g][:, :], ALU.add))
                    else:
                        for g in range(NG):
                            dve.wait_ge(s["yd_mm"], g + 1)
                            link(dve.tensor_copy(y[:, g * GW:(g + 1) * GW], bank[3 + g][:, :]))
                    dve.wait_ge(s["xskip"], NG * c + NG)
                    link(dve.tensor_tensor(y[:, :], y[:, :], x_c[:, :], ALU.add))
                    dve.tensor_tensor(y[:, :], y[:, :], zs[:, c, :], ALU.mult).then_inc(s["y_gated"], 1)
                    if c < TT - 1:
                        state_update(c, 1)

                def chunk_norm(c):
                    dve.wait_ge(s["yrstd"], c + 1)
                    link(dve.tensor_scalar(y[:, 0:GW], y[:, 0:GW], ssum[:, 1, 0:1], None, ALU.mult))
                    dve.tensor_scalar(y[:, GW:D], y[:, GW:D], ssum[:, 1, 1:2], None, ALU.mult).then_inc(s["yn"], 1)

                def part3(c):
                    for g in range(NG):
                        dve.wait_ge(s["ytr_mm"], NG * c + g + 1)
                        dve.tensor_tensor(ymixT[:, 8 + 4 * g:12 + 4 * g, cs(c)],
                                          bank[3 + g][:, :].rearrange("p (j t) -> p j t", t=P),
                                          ssn[:, 4 * g:4 * g + 4].unsqueeze(2).to_broadcast([P, 4, P]), ALU.mult)\
                            .then_inc(s["yT"], 1)

                def split_y(k):
                    dve.wait_ge(s["yhi"], k + 1)
                    if k >= 2:
                        dve.wait_ge(s["unit"], OUT0 + k - 1)
                    dve.tensor_tensor(ylo[:, k % 2, :], ymixT[:, k, :], yhi[:, k % 2, :].bitcast(F32), ALU.subtract)\
                        .then_inc(s["ylo"], 1)

                for j in range(NSC):
                    if j % 2:
                        chunk_weights(j // 2)
                    elif j:
                        chunk_norm(j // 2 - 1)
                        part3(j // 2 - 1)
                    sc_conv(j)
                    if j:
                        sc_norm(j - 1)
                    if j % 2:
                        part2(j // 2)
                    elif j == 0:
                        dve.wait_ge(s["cum_mm"], 2)
                        dve.tensor_copy(cums[:, 0:2, :, :], bank[7][:, 0:2 * TT * SH]
                                        .rearrange("p (r c h) -> p r c h", r=2, h=SH)).then_inc(s["cums"], 1)
                        dve.wait_ge(s["cums"], 1)
                        dve.tensor_tensor(cums[:, 2], cums[:, 1], cums[:, 0], ALU.subtract).then_inc(s["cums"], 1)
                    if j == NSC - 1:
                        split_y(0)
                    sc_out(j)
                    if j % 2 == 0:
                        part1(j // 2)

                chunk_norm(TT - 1)
                part3(TT - 1)
                sc_norm(NSC - 1)
                for k in range(1, 16):
                    split_y(k)
                dve.wait_ge(s["gate"], 2)

                def gated_mix(c):
                    dve.wait_ge(s["tile_mm"], c + 1)
                    if c >= 2:
                        dve.wait_ge(s["out"], c - 1)
                    for h in range(2):
                        hs = slice(h * 512, (h + 1) * 512)
                        dve.tensor_tensor(mixed[c % 2][:, hs], bank[2 * c + h][:, :], state[:, hs], ALU.mult)\
                            .then_inc(s["mixed"], 1)

                def add(c):
                    dve.wait_ge(s["x_scaled"], c + 1)
                    dve.wait_ge(s["mixed"], 2 * c + 2)
                    wait(dve, s["out"], c)
                    dve.tensor_tensor(x_tm[:, c, :], x_tm[:, c, :], mixed[c % 2][:, :], ALU.add).then_inc(s["out"], 1)

                def stats(c):
                    dve.wait_ge(s["out"], c + 1)
                    for h in range(2):
                        ins = dve.bn_stats(ln["stats"][:, c, h, :], x_tm[:, c, h * 512:(h + 1) * 512])
                    link(ins)
                    dve.bn_aggr(ln["mv"][:, c, :], ln["stats"][:, c, :, :]).then_inc(s["stats"], 1)

                def shift(c):
                    dve.wait_ge(s["ln_rstd"], c + 1)
                    dve.scalar_tensor_tensor(out=ln["shift"][:, c:c + 1], in0=ln["mv"][:, c, 0:1], scalar=-1.0,
                                             in1=ln["rstd"][:, c:c + 1], op0=ALU.mult, op1=ALU.mult)\
                        .then_inc(s["shift"], 1)

                gated_mix(0)
                for c in range(TT):
                    if c in (0, TT - 1):
                        add(c)
                    if c == 0:
                        gated_mix(1)
                    stats(c)
                    if c + 2 < TT:
                        gated_mix(c + 2)
                    if c:
                        shift(c - 1)
                shift(TT - 1)

            @block.tensor
            def _(pe):
                pe.wait_ge(s["consts"], 8)

                def cond_columns(q):
                    for i in (2 * q, 2 * q + 1):
                        if on_pe(q):
                            region, slot, arrived, count = cond_slot(i)
                            pe.wait_ge(arrived, count)
                            for k in range(KD):
                                ins = pe.matmul(bank[5][:, i:i + 1], region[:, slot, k * P:(k + 1) * P],
                                                cact[:, 1, k:k + 1], start=(k == 0), stop=(k == KD - 1))
                        else:
                            pe.wait_ge(s["cond_sum"], sums(q))
                            ins = pe.matmul(bank[5][:, i:i + 1], csum[:, i % CSLOTS, :], ones[:, 0:1], start=True,
                                            stop=True)
                        ins.then_inc(s["cond_mm"], 1)

                def channel_unit(n, b, each_k=None):
                    pe.wait_ge(s["lo"], n + 1)
                    for k in range(KD):
                        ks = slice(k * P, (k + 1) * P)
                        if each_k:
                            each_k(k)
                        pe.matmul(bank[b][:, :], whi[:, n % 2, ks], u1hi[:, k, :], start=(k == 0), stop=False)
                        pe.matmul(bank[b][:, :], whi[:, n % 2, ks], u1lo[:, k, :], start=False, stop=False)
                        ins = pe.matmul(bank[b][:, :], wlo[:, n % 2, ks], u1hi[:, k, :], start=False,
                                        stop=(k == KD - 1))
                    ins.then_inc(s["unit"], 1)

                pe.wait_ge(s["cact"], 1)
                for q in range(PA):
                    cond_columns(q)
                for m in range(KX):
                    if m >= 4:
                        pe.wait_ge(s["xbc_copied"], m - 3)
                    channel_unit(XBC0 + m, m % 4, (lambda k: pe.wait_ge(s["u1lo"], k + 1)) if m == 0 else None)
                    if m == 0:
                        pe.wait_ge(s["cond_out"], 1)
                    else:
                        for q in pairs_at(XBC0 + m - 1):
                            cond_columns(q)
                pe.wait_ge(s["wdt_lo"], 1)
                for k in range(KD):
                    for left, right in ((wdthi, u1hi), (wdthi, u1lo), (wdtlo, u1hi)):
                        ins = pe.matmul(bank[4][0:SH, :], left[:, k, :], right[:, k, :],
                                        start=(k == 0 and left is wdthi and right is u1hi),
                                        stop=(k == KD - 1 and left is wdtlo))
                ins.then_inc(s["dt_rows"], 1)
                for n in range(Z0, SC0):
                    q = (n - Z0) % 4
                    pe.wait_ge(s["lo"], n + 1)
                    for c in range(TT):
                        if q == 0:
                            if n == Z0:
                                pe.wait_ge(s["xbc_copied"], KX - 3 + c)
                            else:
                                pe.wait_ge(s["z_out"], c + 1)
                        for k in range(2):
                            kk = 2 * q + k
                            for left, right in ((u1hi, whi), (u1hi, wlo), (u1lo, whi)):
                                ins = pe.matmul(bank[c][:, :], left[:, kk, cs(c)],
                                                right[:, n % 2, k * 512:(k + 1) * 512],
                                                start=(kk == 0 and left is u1hi and right is whi),
                                                stop=(kk == KD - 1 and left is u1lo))
                    ins.then_inc(s["unit"], 1)
                    if n == Z0:
                        pe.wait_ge(s["dt_copied"], 1)
                        for c in range(TT):
                            ins = pe.transpose(bank[6][:, c * SH:(c + 1) * SH], x_c[0:SH, cs(c)], ident[0:SH, 0:SH])
                        ins.then_inc(s["dt_mm"], 1)
                    for q in pairs_at(n - 1):
                        cond_columns(q)

                def sc_mean(j):
                    pe.wait_ge(s["ysq"], j + 1)
                    if j % 2 == 0:
                        pe.wait_ge(s["btm"], j // 2 + 1)
                        pe.wait_ge(s["cbm"], j // 2 + 1)
                    elif j < NSC - 1:
                        pe.wait_ge(s["st_out"], NG * (j // 2) + NG)
                    pe.matmul(bank[5][:, :], grp[:, :], ysq[:, :], start=True, stop=True).then_inc(s["mean_mm"], 1)

                def sc_unit(j, r, free):
                    if j:
                        pe.wait_ge(s[free], j)
                    else:
                        pe.wait_ge(s["z_out"], TT + r + 1)
                    channel_unit(SC0 + 3 * j + r, r)

                def part1(c):
                    for g in range(NG):
                        if c:
                            pe.wait_ge(s["yT"], NG * (c - 1) + g + 1)
                        for j in range(4):
                            ins = pe.transpose(bank[3 + g][:, j * P:(j + 1) * P], xbcT[:, 4 * g + j, cs(c)], ident[:, :])
                        ins.then_inc(s["xtr_mm"], 1)
                    pe.wait_ge(s["mean_out"], 2 * c) if c else pe.wait_ge(s["cond_out"], 2)
                    for g in range(NG):
                        pe.transpose(bank[5][:, g * P:(g + 1) * P], xbcT[:, 8 + g, cs(c)], ident[:, :])
                    for g in range(NG):
                        ins = pe.matmul(bank[5][:, 256 + g * P:256 + (g + 1) * P], xbcT[:, 8 + g, cs(c)],
                                        xbcT[:, 10 + g, cs(c)], start=True, stop=True)
                    ins.then_inc(s["cb_mm"], 1)

                def chunk_state(c, g):
                    pe.matmul(bank[5][:, :], btm[:, g * P:(g + 1) * P], xde[:, g * GW:(g + 1) * GW],
                              start=True, stop=True).then_inc(s["st_mm"], 1)

                def part2(c):
                    pe.wait_ge(s["mean_out"], 2 * c + 1)
                    if c < TT - 1:
                        pe.wait_ge(s["xde"], NG * c + NG)
                        chunk_state(c, 0)
                    pe.wait_ge(s["xdt"], NG * c + NG)
                    if c:
                        if c == 1:
                            pe.wait_ge(s["cumT"], 1)
                        else:
                            pe.wait_ge(s["yo_out"], NG * (c - 1))
                        for g in range(NG):
                            pe.wait_ge(s["st_out"], NG * (c - 1) + g + 1)
                            pe.matmul(bank[6 + g][:, :], xbcT[:, 10 + g, cs(c)], state[:, g * GW:(g + 1) * GW],
                                      start=True, stop=True).then_inc(s["yo_mm"], 1)
                    for g in range(NG):
                        pe.wait_ge(s["weights"], NG * c + g + 1)
                        for r in range(HPG):
                            h = g * HPG + r
                            ins = pe.matmul(bank[3 + g][:, r * HD:(r + 1) * HD], decay[:, h, :],
                                            xdt[:, h * HD:(h + 1) * HD], start=True, stop=True)
                        ins.then_inc(s["yd_mm"], 1)
                    if c < TT - 1:
                        pe.wait_ge(s["st_out"], NG * c + 1)
                        chunk_state(c, 1)

                def part3(c):
                    pe.wait_ge(s["yn"], c + 1)
                    for g in range(NG):
                        for j in range(4):
                            k = 4 * g + j
                            ins = pe.transpose(bank[3 + g][:, j * P:(j + 1) * P], y[:, k * P:(k + 1) * P], ident[:, :])
                        ins.then_inc(s["ytr_mm"], 1)

                def out_unit(k, c):
                    w = (OUT0 + k) % 2
                    for left, right in ((yhi, whi), (yhi, wlo), (ylo, whi)):
                        for h in range(2):
                            ins = pe.matmul(bank[2 * c + h][:, :], left[:, k % 2, cs(c)],
                                            right[:, w, h * 512:(h + 1) * 512],
                                            start=(k == 0 and left is yhi and right is whi),
                                            stop=(k == 15 and left is ylo))
                    return ins

                for j in range(NSC):
                    sc_unit(j, 0, "c_copied")
                    if j:
                        sc_mean(j - 1)
                    if j == 0:
                        for q in pairs_at(SC0 - 1):
                            cond_columns(q)
                    elif j % 2 == 0:
                        part3(j // 2 - 1)
                    sc_unit(j, 1, "h_used")
                    if j % 2:
                        part2(j // 2)
                    sc_unit(j, 2, "ysc")
                    if j == 0:
                        pe.wait_ge(s["adt"], 1)
                        for r, m in enumerate((tri, ones)):
                            pe.matmul(bank[7][:, r * TT * SH:(r + 1) * TT * SH], m[:, :],
                                      adt[:, :, :].rearrange("p c h -> p (c h)"), start=True, stop=True)\
                                .then_inc(s["cum_mm"], 1)
                        pe.wait_ge(s["cums"], 1)
                        pe.transpose(bank[6][0:TT * SH, 0:P], cums[:, 0, :, :].rearrange("p c h -> p (c h)"),
                                     ident[:, :]).then_inc(s["cumT_mm"], 1)
                    if j % 2 == 0:
                        part1(j // 2)
                pe.wait_ge(s["cond_out"], 5)
                pe.wait_ge(s["yo_out"], NG * (TT - 1))
                for m in range(KD):
                    ins = pe.matmul(bank[6 + m // 4][:, (m % 4) * P:(m % 4 + 1) * P],
                                    cond[:, 16 + m:17 + m].to_broadcast([P, P]), ident[:, :], start=True, stop=True)
                    if m % 4 == 3:
                        ins.then_inc(s["gate_mm"], 1)
                pe.wait_ge(s["lo"], OUT0 + 1)
                pe.wait_ge(s["ylo"], 1)
                out_unit(0, 0)
                sc_mean(NSC - 1)
                part3(TT - 1)
                pe.wait_ge(s["gate"], 2)
                out_unit(0, 3)
                pe.wait_ge(s["yT"], NG * TT)
                out_unit(0, 1)
                pe.wait_ge(s["mean_out"], NSC)
                out_unit(0, 2).then_inc(s["unit"], 1)
                for k in range(1, 14):
                    pe.wait_ge(s["lo"], OUT0 + k + 1)
                    pe.wait_ge(s["ylo"], k + 1)
                    for c in range(TT):
                        ins = out_unit(k, c)
                    ins.then_inc(s["unit"], 1)
                pe.wait_ge(s["lo"], UNITS - 1)
                pe.wait_ge(s["ylo"], 15)
                for c in range(TT - 1):
                    out_unit(14, c)
                pe.wait_ge(s["lo"], UNITS)
                pe.wait_ge(s["ylo"], 16)
                for c in range(TT):
                    if c == TT - 1:
                        out_unit(14, c)
                    out_unit(15, c).then_inc(s["tile_mm"], 1)


def wait(eng, sem, value):
    if not (isinstance(value, int) and value <= 0):
        eng.wait_ge(sem, value)


UNROLL = 8
TOK = 8
GT = 32
QCH = 2 * HEADS
BEFORE, BESIDE = 48, T // TOK
AFTER = NKEYS - BEFORE - BESIDE
U_CHUNKS = QCH + NKEYS


def router(nc, a, x_tm, cond, fold, ident, stream, h_dram, g_dram):
    with ExitStack() as ctx:
        def sb(name, shape, dt=F32):
            return ctx.enter_context(nc.sbuf_tensor(name, shape, dt))

        def sem(name):
            return ctx.enter_context(nc.semaphore(name))

        bank = [ctx.enter_context(nc.psum_tensor(f"rt_bank{i}", [P, 512], F32)) for i in range(8)]
        u2hi = sb("u2_hi", [P, KD, T], F32R)
        u2lo = sb("u2_lo", [P, KD, T], F32R)
        keys = sb("keys", [P, QCH, NKEYS])
        hout = sb("h_out", [P, 2, T])
        st = sb("search", [P, QCH * NKEYS])
        rp = sb("search_rest", [P, QCH * NKEYS])
        val = sb("top_values", [P, QCH, TOPK])
        idx = sb("top_index", [P, QCH, TOPK], U32)
        idf = sb("top_index_f", [P, QCH, TOPK])
        tv = sb("pair_values", [P, HEADS, TOPK])
        pos = sb("pair_index", [P, 3, PICKS], U32)
        pof = sb("pair_index_f", [P, 2, PICKS])
        pk = sb("picks", [P, 3, TT, PICKS])
        gsum = sb("gate_sums", [P, 2, TT * HEADS])
        pT = sb("picks_T", [P, 3, T])
        ghi = sb("gates_T_hi", [P, T], F32R)
        glo = sb("gates_T_lo", [P, T])
        iota = sb("iota", [P, NKEYS])
        with nc.sbuf_tensor("u2_plain", [P, KD, T], F32) as u2f:
            pass
        with nc.sbuf_tensor("queries_T", [P, QCH, T], F32) as qT:
            pass
        glow = sb("g_low", [P, 2, 4, 2 * P])
        gst = sb("g_staging", [P, 2, NKEYS, GT])
        lnr = rp[:, :].rearrange("p (r d) -> p r d", d=D)
        raw, whi, wlo, sc_all = stream["raw"], stream["hi"], stream["lo"], stream["scores"]
        hotA, hotB, eqA = stream["hot_gates"], stream["hot_keys"], stream["hot_equal"]

        loaded, h_saved = stream["loaded"], stream["h_saved"]
        g_saved = [sem(f"g_saved{i}") for i in range(2)]
        s = {n: sem("r_" + n) for n in (
            "rows_in", "iota", "tr_mm", "u2_even", "u2_odd", "hi_u2", "lo_u2", "h_act", "sc_mm",
            "sc_out", "shifted", "gexp", "gates", "pt_mm", "pT", "gate_mm", "gate", "equal", "hot", "hot_low", "g_mm", "g_low", "g_out",
            "ordered", "chain")}
        s.update({"hi": stream["hi_done"], "lo": stream["lo_done"], "h_mm": stream["mm"]})

        def chunk_dram(n):
            return a["w_query"][n] if isinstance(n, int) and n < QCH else a["u_T"][n - QCH]

        def per_token(row, base):
            return row[:, bass.ds(base, TOK)].unsqueeze(2).to_broadcast([P, TOK, NKEYS])

        def turns(eng, first, count, body):
            with eng.Fori(0, count // UNROLL) as r:
                for u in range(UNROLL):
                    body(r * UNROLL + (first + u), u)

        G0 = QCH + BEFORE
        REST0 = G0 + BESIDE

        with nc.Block() as block:
            @block.sync
            def _(sp):
                def load(n, u):
                    slot = (n if isinstance(n, int) else u) % 4
                    wait(sp, s["lo"], n - 3)
                    sp.dma_start(raw[:, slot, :], chunk_dram(n).rearrange("p k e -> p (k e)"))\
                        .then_inc(loaded[slot], 16)

                for n in range(QCH):
                    load(n, 0)
                    if n == 3:
                        for r, name in enumerate(("ln1_g", "ln1_b")):
                            sp.dma_start(lnr[:, r, :], a[name][0, :].partition_broadcast(P)).then_inc(s["rows_in"], 16)
                        sp.dma_start(keys[:, :, :], a["keysT"]).then_inc(s["rows_in"], 16)
                turns(sp, QCH, NKEYS, load)
                for n in range(4):
                    sp.wait_ge(s["lo"], U_CHUNKS + n - 3)
                    sp.dma_start(raw[:, n, :], a["v"][n]).then_inc(loaded[n], 16)
                for i in range(2):
                    sp.wait_ge(g_saved[i], 16 + 16 * (T // GT // 2))
                    sp.wait_ge(h_saved[i], 16 + 16 * 4)
                for half in range(2):
                    load_group(sp, stream, h_dram, g_dram, 4 * half, half)

            @block.gpsimd
            def _(pool):
                pool.iota(iota[:, :], [[1, NKEYS]], base=0, channel_multiplier=0,
                          allow_small_or_imprecise_dtypes=True).then_inc(s["iota"], 1)

                def split_lo(n, u):
                    slot = (n if isinstance(n, int) else u) % 4
                    pool.wait_ge(s["hi"], n + 1)
                    wait(pool, s["h_mm"], n - 1)
                    pool.tensor_tensor(wlo[:, slot % 2, :], raw[:, slot, :], whi[:, slot % 2, :].bitcast(F32),
                                       ALU.subtract).then_inc(s["lo"], 1)

                def hot_low(n, u):
                    pool.wait_ge(s["equal"], n - (G0 - 1))
                    pool.tensor_tensor(hotA[:, u % 2, :, 1, :], eqA[:, u % 2, :, :],
                                       per_token(glo[:, :], (n - G0) * TOK), ALU.mult).then_inc(s["hot_low"], 1)

                for n in range(QCH):
                    split_lo(n, 0)
                turns(pool, QCH, BEFORE, split_lo)
                split_lo(G0, 0)
                hot_low(G0, 0)
                with pool.Fori(0, BESIDE // UNROLL - 1) as r:
                    for u in range(UNROLL):
                        n = r * UNROLL + (G0 + u)
                        split_lo(n + 1, (u + 1) % UNROLL)
                        hot_low(n + 1, (u + 1) % UNROLL)
                for u in range(1, UNROLL):
                    split_lo(REST0 - UNROLL + u, u)
                    hot_low(REST0 - UNROLL + u, u)
                turns(pool, REST0, AFTER, split_lo)
                split_lo(U_CHUNKS, 0)

            @block.scalar
            def _(act):
                def split_hi(n, u):
                    slot = (n if isinstance(n, int) else u) % 4
                    act.wait_ge(loaded[slot], (n // 4) * 16 + 16 if isinstance(n, int) else (n + (4 - slot)) * 4)
                    wait(act, s["h_mm"], n - 1)
                    act.activation(whi[:, slot % 2, :], raw[:, slot, :], ACT.Copy).then_inc(s["hi"], 1)

                for k in range(KD):
                    if k % 2 == 0:
                        act.wait_ge(s["tr_mm"], k + 1)
                        act.activation(u2f[:, k, :], bank[k][:, :], ACT.Identity, scale=fold[:, 0, k:k + 1],
                                       bias=fold[:, 1, k:k + 1]).then_inc(s["u2_even"], 1)
                        act.wait_ge(s["u2_even"], k // 2 + 1)
                    else:
                        act.wait_ge(s["u2_odd"], k // 2 + 1)
                    act.activation(u2hi[:, k, :], u2f[:, k, :], ACT.Copy).then_inc(s["hi_u2"], 1)
                    if k in (1, 5):
                        split_hi(k // 4, 0)

                def query_out(n):
                    act.wait_ge(s["h_mm"], n + 1)
                    split_hi(n + 2, 0)
                    if n == 0:
                        act.wait_ge(s["lo_u2"], KD)
                    act.activation(qT[:, n, :], bank[n % 2][:, :], ACT.Copy).then_inc(s["h_act"], 1)

                def save_g(n, u):
                    act.wait_ge(s["g_out"], (n - G0) * 4 + 4)
                    act.dma_start(g_dram[(n - (G0 + u)) // 4 + u // 4], gst[:, u // 4, :, :]).then_inc(g_saved[u // 4], 16)

                def gelu_out(n, u):
                    act.wait_ge(s["h_mm"], n + 1)
                    split_hi(n + 2, (u + 2) % UNROLL)
                    act.wait_ge(h_saved[u % 2], (n - (QCH + u % 2)) * 8 + 16)
                    act.activation(hout[:, u % 2, :], bank[u % 2][:, :], ACT.Gelu).then_inc(s["h_act"], 1)
                    act.wait_ge(s["h_act"], n + 1)
                    act.dma_start(h_dram[n - QCH], hout[:, u % 2, :]).then_inc(h_saved[u % 2], 16)

                def lower_parts(n, u):
                    for b in range(4):
                        act.wait_ge(s["g_mm"], (n - G0) * 4 + (4 + b + 1))
                        act.activation(glow[:, u % 2, b, :].rearrange("p (t i) -> p t i", t=2),
                                       bank[4 + b][:, :].rearrange("p (t w i) -> p t w i", t=2, w=2)[:, :, 1, :],
                                       ACT.Copy).then_inc(s["g_low"], 1)

                act.sem_inc(h_saved[0], 16)
                act.sem_inc(h_saved[1], 16)
                for n in range(QCH):
                    query_out(n)
                for c in range(TT):
                    for b in range(4):
                        act.wait_ge(s["sc_mm"], 4 * c + b + 1)
                        act.activation(sc_all[:, c, b * 512:(b + 1) * 512], bank[2 + b][:, :], ACT.Copy)\
                            .then_inc(s["sc_out"], 1)
                turns(act, QCH, BEFORE - UNROLL, gelu_out)
                act.wait_ge(s["shifted"], TT)
                act.activation(pk[:, 2, :, :], pk[:, 2, :, :], ACT.Exp).then_inc(s["gexp"], 1)
                for u in range(UNROLL):
                    gelu_out(G0 - UNROLL + u, u)
                for h in range(2):
                    act.wait_ge(s["gate_mm"], h + 1)
                    act.activation(stream["gate2"][:, h * 512:(h + 1) * 512], bank[5 + h][:, :], ACT.Copy)\
                        .then_inc(s["gate"], 1)
                with act.Fori(0, BESIDE // UNROLL) as r:
                    for u in range(UNROLL):
                        n = r * UNROLL + (G0 + u)
                        gelu_out(n, u)
                        lower_parts(n, u)
                        if u % 4 == 3:
                            save_g(n, u)
                turns(act, REST0, AFTER, gelu_out)

            @block.vector
            def _(dve):
                links = [0]

                def link(ins, base=0):
                    links[0] += 1
                    ins.then_inc(s["chain"], 1)
                    dve.wait_ge(s["chain"], base + links[0])

                for k in range(KD):
                    if k % 2 == 0:
                        dve.wait_ge(s["tr_mm"], k + 2)
                        dve.tensor_scalar(u2f[:, k + 1, :], bank[k + 1][:, :], fold[:, 0, k + 1:k + 2],
                                          fold[:, 1, k + 1:k + 2], ALU.mult, ALU.add).then_inc(s["u2_odd"], 1)
                    dve.wait_ge(s["hi_u2"], k + 1)
                    dve.tensor_tensor(u2lo[:, k, :], u2f[:, k, :], u2hi[:, k, :].bitcast(F32), ALU.subtract)\
                        .then_inc(s["lo_u2"], 1)
                dve.wait_ge(s["rows_in"], 48)
                for c in range(TT):
                    xs = x_tm[:, c, :]
                    link(dve.tensor_tensor(xs, xs, lnr[:, 0, :], ALU.mult))
                    link(dve.tensor_tensor(xs, xs, lnr[:, 1, :], ALU.add))
                    link(dve.tensor_scalar(xs, xs, ALPHA, None, ALU.mult))

                straight = links[0]
                s3 = st[:, :].rearrange("p (m n) -> p m n", n=NKEYS)
                r3 = rp[:, :].rearrange("p (m n) -> p m n", n=NKEYS)
                c3 = st[:, :].rearrange("p (h n) -> p h n", n=TOPK * TOPK)
                q3 = rp[:, :].rearrange("p (h n) -> p h n", n=TOPK * TOPK)
                e4 = st[:, :].rearrange("p (h k a) -> p h k a", h=HEADS, k=TOPK)
                v4 = val[:, :, :].rearrange("p (h w) k -> p h w k", w=2)
                i4 = idf[:, :, :].rearrange("p (h w) k -> p h w k", w=2)

                def top16(values, indices, source, rest, n):
                    def each(f):
                        for m in range(n):
                            ins = f(m)
                        step(ins)
                    dve.sem_inc(s["ordered"], 1)
                    each(lambda m: dve.max(values[:, m, 0:8], source[:, m, :]))
                    dve.sem_inc(s["ordered"], 1)
                    for m in range(n):
                        dve.max_index(indices[:, m, 0:8], values[:, m, 0:8], source[:, m, :])
                    each(lambda m: dve.match_replace(rest[:, m, :], values[:, m, 0:8], source[:, m, :], FLOOR))
                    dve.sem_inc(s["ordered"], 1)
                    each(lambda m: dve.max(values[:, m, 8:16], rest[:, m, :]))
                    dve.sem_inc(s["ordered"], 1)
                    each(lambda m: dve.max_index(indices[:, m, 8:16], values[:, m, 8:16], rest[:, m, :]))

                count = [0]
                STEPS = 1 + 4 + 1 + 1 + 4 + 1 + 1 + 3 * 2

                with dve.Fori(0, TT) as c:
                    def step(ins):
                        count[0] += 1
                        ins.then_inc(s["chain"], 1)
                        dve.wait_ge(s["chain"], c * STEPS + (straight + count[0]))

                    dve.wait_ge(s["sc_out"], c * 4 + 4)
                    step(dve.tensor_copy(st[:, :], sc_all[:, bass.ds(c, 1), :].rearrange("p c n -> p (c n)")))
                    top16(val, idx, s3, r3, QCH)
                    step(dve.tensor_copy(idf[:, :, :], idx[:, :, :]))
                    step(dve.tensor_tensor(e4, v4[:, :, 0, :].unsqueeze(3).to_broadcast([P, HEADS, TOPK, TOPK]),
                                           v4[:, :, 1, :].unsqueeze(2).to_broadcast([P, HEADS, TOPK, TOPK]), ALU.add))
                    p3 = pos[:, 0, :].rearrange("p (h k) -> p h k", k=TOPK)
                    top16(tv, p3, c3, q3, HEADS)
                    dve.tensor_scalar(pos[:, 1, :], pos[:, 0, :], 4, None, ALU.logical_shift_right)
                    step(dve.tensor_scalar(pos[:, 2, :], pos[:, 0, :], 15, None, ALU.bitwise_and))
                    step(dve.tensor_copy(pof[:, :, :], pos[:, 1:3, :]))
                    for w in range(2):
                        pw = pof[:, w, :].rearrange("p (h k) -> p h k", k=TOPK)
                        step(dve.tensor_tensor(
                            e4, pw.unsqueeze(3).to_broadcast([P, HEADS, TOPK, TOPK]),
                            iota[:, 0:TOPK].unsqueeze(1).unsqueeze(1).to_broadcast([P, HEADS, TOPK, TOPK]),
                            ALU.is_equal))
                        step(dve.tensor_tensor(
                            e4, e4, i4[:, :, w, :].unsqueeze(2).to_broadcast([P, HEADS, TOPK, TOPK]), ALU.mult))
                        step(dve.tensor_reduce(
                            pk[:, w, bass.ds(c, 1), :].rearrange("p c k -> p (c k)"),
                            st[:, :].rearrange("p (k a) -> p k a", a=TOPK), AX_X, ALU.add))
                    dve.tensor_tensor(
                        pk[:, 2, bass.ds(c, 1), :].rearrange("p c (h k) -> p (c h) k", k=TOPK), tv[:, :, :],
                        tv[:, :, 0:1].to_broadcast([P, HEADS, TOPK]), ALU.subtract).then_inc(s["shifted"], 1)
                    dve.wait_ge(s["shifted"], c + 1)
                assert count[0] == STEPS, count
                links[0] = straight + TT * STEPS
                g3 = pk[:, 2, :, :].rearrange("p c (h k) -> p (c h) k", k=TOPK)
                dve.wait_ge(s["gexp"], 1)
                link(dve.tensor_reduce(gsum[:, 0, :], g3, AX_X, ALU.add))
                link(dve.reciprocal(gsum[:, 1, :], gsum[:, 0, :]))
                dve.tensor_tensor(g3, g3, gsum[:, 1, :].unsqueeze(2).to_broadcast([P, TT * HEADS, TOPK]), ALU.mult)\
                    .then_inc(s["gates"], 1)
                for w in range(2):
                    dve.wait_ge(s["pt_mm"], w + 1)
                    dve.tensor_copy(pT[:, w, :], bank[2 + w][:, :]).then_inc(s["pT"], 1)
                dve.wait_ge(s["pt_mm"], 3)
                dve.tensor_copy(ghi[:, :], bank[4][:, :]).then_inc(s["pT"], 1)
                dve.wait_ge(s["pT"], 3)
                dve.tensor_tensor(glo[:, :], bank[4][:, :], ghi[:, :].bitcast(F32), ALU.subtract).then_inc(s["pT"], 1)
                dve.wait_ge(s["pT"], 4)
                dve.wait_ge(s["iota"], 1)

                for i in range(2):
                    dve.sem_inc(g_saved[i], 16)
                dve.sem_inc(s["g_mm"], 4)

                def hot_rows(n, u):
                    base = (n - G0) * TOK
                    wait(dve, s["g_mm"], (n - G0) * 4)
                    each_key = iota[:, :].unsqueeze(1).to_broadcast([P, TOK, NKEYS])
                    dve.tensor_tensor(eqA[:, u % 2, :, :], each_key, per_token(pT[:, 0, :], base), ALU.is_equal)\
                        .then_inc(s["equal"], 1)
                    dve.tensor_tensor(hotB[:, u % 2, :, :], each_key, per_token(pT[:, 1, :], base), ALU.is_equal)
                    dve.wait_ge(s["equal"], n - (G0 - 1))
                    dve.tensor_tensor(hotA[:, u % 2, :, 0, :], eqA[:, u % 2, :, :],
                                      per_token(ghi[:, :].bitcast(F32), base), ALU.mult).then_inc(s["hot"], 1)

                def stage_g(n, u):
                    for b in range(4):
                        dve.wait_ge(s["g_low"], (n - G0) * 4 + (b + 1))
                        if u % 4 == 0 and b == 0:
                            dve.wait_ge(g_saved[u // 4], (n - (G0 + u)) * 2 + 16)
                        col = (u % 4) * TOK + 2 * b
                        dve.tensor_tensor(gst[:, u // 4, :, col:col + 2],
                                          bank[4 + b][:, :].rearrange("p (t w i) -> p w i t", t=2, w=2)[:, 0, :, :],
                                          glow[:, u % 2, b, :].rearrange("p (t i) -> p i t", t=2),
                                          ALU.add).then_inc(s["g_out"], 1)

                hot_rows(G0, 0)
                with dve.Fori(0, BESIDE // UNROLL - 1) as r:
                    for u in range(UNROLL):
                        n = r * UNROLL + (G0 + u)
                        hot_rows(n + 1, (u + 1) % UNROLL)
                        stage_g(n, u)
                for u in range(UNROLL):
                    n = REST0 - UNROLL + u
                    if u < UNROLL - 1:
                        hot_rows(n + 1, u + 1)
                    stage_g(n, u)

            @block.tensor
            def _(pe):
                for k in range(KD):
                    for c in range(TT):
                        ins = pe.transpose(bank[k][:, c * P:(c + 1) * P], x_tm[:, c, k * P:(k + 1) * P], ident[:, :])
                    ins.then_inc(s["tr_mm"], 1)

                def products(n, u):
                    slot = (n if isinstance(n, int) else u) % 2
                    pe.wait_ge(s["lo"], n + 1)
                    wait(pe, s["h_act"], n - 1)
                    for k in range(KD):
                        ks = slice(k * P, (k + 1) * P)
                        if isinstance(n, int) and n == 0:
                            pe.wait_ge(s["lo_u2"], k + 1)
                        pe.matmul(bank[slot][:, :], whi[:, slot, ks], u2hi[:, k, :], start=(k == 0), stop=False)
                        pe.matmul(bank[slot][:, :], whi[:, slot, ks], u2lo[:, k, :], start=False, stop=False)
                        ins = pe.matmul(bank[slot][:, :], wlo[:, slot, ks], u2hi[:, k, :], start=False,
                                        stop=(k == KD - 1))
                    ins.then_inc(s["h_mm"], 1)

                for n in range(QCH):
                    products(n, 0)
                pe.wait_ge(s["rows_in"], 48)
                pe.wait_ge(s["h_act"], QCH)
                for c in range(TT):
                    for b in range(4):
                        wait(pe, s["sc_out"], 4 * (c - 1) + b + 1)
                        for r in range(4):
                            m = 4 * b + r
                            ins = pe.matmul(bank[2 + b][:, r * P:(r + 1) * P], qT[:, m, c * P:(c + 1) * P],
                                            keys[:, m, :], start=True, stop=True)
                        ins.then_inc(s["sc_mm"], 1)
                turns(pe, QCH, BEFORE, products)
                pe.wait_ge(s["gates"], 1)
                pe.wait_ge(s["sc_out"], 4 * TT)
                for w in range(3):
                    for c in range(TT):
                        ins = pe.transpose(bank[2 + w][:, c * P:(c + 1) * P], pk[:, w, c, :], ident[:, :])
                    ins.then_inc(s["pt_mm"], 1)
                for m in range(KD):
                    ins = pe.matmul(bank[5 + m // 4][:, (m % 4) * P:(m % 4 + 1) * P],
                                    cond[:, 40 + m:41 + m].to_broadcast([P, P]), ident[:, :], start=True, stop=True)
                    if m % 4 == 3:
                        ins.then_inc(s["gate_mm"], 1)
                products(G0, 0)
                pe.wait_ge(s["pT"], 4)
                pe.wait_ge(s["gate"], 2)

                def g_products(n, u):
                    pe.wait_ge(s["hot"], n - (G0 - 1))
                    pe.wait_ge(s["hot_low"], n - (G0 - 1))
                    wait(pe, s["g_out"], (n - G0) * 4)
                    for t in range(TOK):
                        ins = pe.matmul(bank[4 + t // 2][:, (t % 2) * 256:(t % 2 + 1) * 256], hotB[:, u % 2, t, :],
                                        hotA[:, u % 2, t, :, :].rearrange("p w i -> p (w i)"), start=True, stop=True)
                        if t % 2:
                            ins.then_inc(s["g_mm"], 1)

                g_products(G0, 0)
                for u in range(1, UNROLL):
                    products(G0 + u, u)
                    g_products(G0 + u, u)
                with pe.Fori(1, BESIDE // UNROLL) as r:
                    for u in range(UNROLL):
                        n = r * UNROLL + (G0 + u)
                        products(n, u)
                        g_products(n, u)
                turns(pe, REST0, AFTER, products)


def load_group(sp, stream, h_dram, g_dram, n, half):
    sp.dma_start(stream["h_in"][:, half, :, :], h_dram[bass.ds(n, 4)].rearrange("i p t -> p i t"))\
        .then_inc(stream["h_loaded"][half], 16)
    sp.dma_start(stream["g_in"][:, half, :, :, :], g_dram[:, :, bass.ds(n, 4), :].rearrange("b p i t -> p b i t"))\
        .then_inc(stream["g_loaded"][half], 16)


def experts(nc, a, x_tm, eps_tile, ln, stream, h_dram, g_dram, out):
    with ExitStack() as ctx:
        def sb(name, shape, dt=F32):
            return ctx.enter_context(nc.sbuf_tensor(name, shape, dt))

        def sem(name):
            return ctx.enter_context(nc.semaphore(name))

        bank = [ctx.enter_context(nc.psum_tensor(f"ex_bank{i}", [P, 512], F32)) for i in range(8)]
        act_f = sb("act", [P, 2, T])
        ahi = sb("act_hi", [P, 2, T], F32R)
        alo = sb("act_lo", [P, 2, T], F32R)
        lnr = sb("ln2_rows", [P, 2, D])
        t = sb("scratch", [P, 2, D])
        vraw, vhi, vlo, gate = stream["raw"], stream["hi"], stream["lo"], stream["gate2"]
        hin, gin, h_in, g_in = stream["h_in"], stream["g_in"], stream["h_loaded"], stream["g_loaded"]
        s = {n: sem("e_" + n) for n in (
            "rows_in", "act", "a_hi", "a_lo", "tile_mm", "mixed", "out", "stats", "ln_ln", "ln_rstd", "shift", "normed",
            "scaled", "y", "stored", "chain")}
        s.update({"v_hi": stream["hi_done"], "v_lo": stream["lo_done"], "mm": stream["mm"]})
        B0 = U_CHUNKS

        def each(eng, body):
            for u in range(UNROLL):
                body(u, u)
            with eng.Fori(1, NKEYS // UNROLL) as r:
                for u in range(UNROLL):
                    body(r * UNROLL + u, u)

        with nc.Block() as block:
            @block.sync
            def _(sp):
                def load(n, u):
                    if u % 4 == 0 and not (isinstance(n, int) and n < 8):
                        sp.wait_ge(s["act"], n - 4)
                        load_group(sp, stream, h_dram, g_dram, n, u // 4)
                    if not (isinstance(n, int) and n < 4):
                        sp.wait_ge(s["v_lo"], n + (B0 - 3))
                        sp.dma_start(vraw[:, u % 4, :], a["v"][n]).then_inc(stream["loaded"][u % 4], 16)

                for i in range(2):
                    sp.wait_ge(stream["h_saved"][i], 16 + 16 * (NKEYS // 2))
                each(sp, load)
                for r, name in enumerate(("ln2_g", "ln2_b")):
                    sp.dma_start(lnr[:, r, :], a[name][0, :].partition_broadcast(P)).then_inc(s["rows_in"], 16)
                for c in range(TT):
                    sp.wait_ge(s["y"], c + 1)
                    sp.dma_start(out[0, c * P:(c + 1) * P, :], x_tm[:, c, :]).then_inc(s["stored"], 16)
                sp.wait_ge(s["stored"], 16 * TT)

            @block.gpsimd
            def _(pool):
                def split_v_lo(n, u):
                    if isinstance(n, int) and n < 1:
                        return
                    pool.wait_ge(s["v_hi"], n + (B0 + 1))
                    pool.wait_ge(s["mm"], n + (B0 - 1))
                    pool.tensor_tensor(vlo[:, u % 2, :], vraw[:, u % 4, :], vhi[:, u % 2, :].bitcast(F32),
                                       ALU.subtract).then_inc(s["v_lo"], 1)

                each(pool, split_v_lo)
                for c in range(1, TT - 1):
                    pool.wait_ge(s["out"], c)
                    pool.wait_ge(s["mixed"], 2 * c + 2)
                    pool.tensor_tensor(x_tm[:, c, :], x_tm[:, c, :], t[:, c % 2, :], ALU.add).then_inc(s["out"], 1)
                pool.wait_ge(s["rows_in"], 32)
                for c in range(TT - 1):
                    pool.wait_ge(s["scaled"], c + 1)
                    pool.tensor_tensor(x_tm[:, c, :], x_tm[:, c, :], lnr[:, 1, :], ALU.add).then_inc(s["y"], 1)

            @block.scalar
            def _(act):
                def split_hi(n, u):
                    if not (isinstance(n, int) and n < 2):
                        act.wait_ge(stream["loaded"][u % 4], (n + (B0 + 4 - u % 4)) * 4)
                        act.wait_ge(s["mm"], n + (B0 - 1))
                        act.activation(vhi[:, u % 2, :], vraw[:, u % 4, :], ACT.Copy).then_inc(s["v_hi"], 1)
                    act.wait_ge(s["act"], n + 1)
                    act.activation(ahi[:, u % 2, :], act_f[:, u % 2, :], ACT.Copy).then_inc(s["a_hi"], 1)

                each(act, split_hi)
                act.preload_act_table_set("natural_log_exp_and_others")

                def ln_rstd(c):
                    act.wait_ge(s["stats"], c + 1)
                    act.activation(ln["rstd"][:, c:c + 1], ln["mv"][:, c, 1:2], ACT.Ln, bias=eps_tile[:, 1:2])\
                        .then_inc(s["ln_ln"], 1)
                    act.wait_ge(s["ln_ln"], c + 1)
                    act.activation(ln["rstd"][:, c:c + 1], ln["rstd"][:, c:c + 1], ACT.Exp, scale=-0.5)\
                        .then_inc(s["ln_rstd"], 1)

                ln_rstd(0)
                for c in range(TT):
                    if c + 1 < TT:
                        ln_rstd(c + 1)
                    act.wait_ge(s["shift"], c + 1)
                    act.activation(x_tm[:, c, :], x_tm[:, c, :], ACT.Identity, scale=ln["rstd"][:, c:c + 1],
                                   bias=ln["shift"][:, c:c + 1]).then_inc(s["normed"], 1)

            @block.vector
            def _(dve):
                def gated(n, u):
                    half, i = u // 4, u % 4
                    if i == 0:
                        dve.wait_ge(h_in[half], n * 2 + (16 - 2 * u))
                        dve.wait_ge(g_in[half], n * 2 + (16 - 2 * u))
                    dve.tensor_tensor(act_f[:, u % 2, :].rearrange("p (b t) -> p b t", t=GT),
                                      hin[:, half, i, :].rearrange("p (b t) -> p b t", t=GT),
                                      gin[:, half, :, i, :], ALU.mult).then_inc(s["act"], 1)
                    dve.wait_ge(s["a_hi"], n + 1)
                    dve.wait_ge(s["mm"], n + (B0 - 1))
                    dve.tensor_tensor(alo[:, u % 2, :], act_f[:, u % 2, :], ahi[:, u % 2, :].bitcast(F32),
                                      ALU.subtract).then_inc(s["a_lo"], 1)
                    dve.wait_ge(s["a_lo"], n + 1)

                each(dve, gated)
                links = [0]

                def link(ins):
                    links[0] += 1
                    ins.then_inc(s["chain"], 1)
                    dve.wait_ge(s["chain"], links[0])

                def gated_sum(c):
                    dve.wait_ge(s["tile_mm"], c + 1)
                    if c >= 2:
                        dve.wait_ge(s["out"], c - 1)
                    for h in range(2):
                        hs = slice(h * 512, (h + 1) * 512)
                        dve.tensor_tensor(t[:, c % 2, hs], bank[2 * c + h][:, :], gate[:, hs], ALU.mult)\
                            .then_inc(s["mixed"], 1)

                def add(c):
                    dve.wait_ge(s["mixed"], 2 * c + 2)
                    wait(dve, s["out"], c)
                    dve.tensor_tensor(x_tm[:, c, :], x_tm[:, c, :], t[:, c % 2, :], ALU.add).then_inc(s["out"], 1)

                def stats(c):
                    dve.wait_ge(s["out"], c + 1)
                    for h in range(2):
                        ins = dve.bn_stats(ln["stats"][:, c, h, :], x_tm[:, c, h * 512:(h + 1) * 512])
                    link(ins)
                    dve.bn_aggr(ln["mv"][:, c, :], ln["stats"][:, c, :, :]).then_inc(s["stats"], 1)

                def shift(c):
                    dve.wait_ge(s["ln_rstd"], c + 1)
                    dve.scalar_tensor_tensor(out=ln["shift"][:, c:c + 1], in0=ln["mv"][:, c, 0:1], scalar=-1.0,
                                             in1=ln["rstd"][:, c:c + 1], op0=ALU.mult, op1=ALU.mult)\
                        .then_inc(s["shift"], 1)

                def scaled(c):
                    dve.wait_ge(s["normed"], c + 1)
                    xs = x_tm[:, c, :]
                    dve.tensor_tensor(xs, xs, lnr[:, 0, :], ALU.mult).then_inc(s["scaled"], 1)
                    if c == TT - 1:
                        dve.wait_ge(s["scaled"], c + 1)
                        dve.wait_ge(s["y"], c)
                        dve.tensor_tensor(xs, xs, lnr[:, 1, :], ALU.add).then_inc(s["y"], 1)

                dve.wait_ge(s["rows_in"], 32)
                gated_sum(0)
                for c in range(TT):
                    if c in (0, TT - 1):
                        add(c)
                    if c == 0:
                        gated_sum(1)
                    stats(c)
                    if c + 2 < TT:
                        gated_sum(c + 2)
                    if c:
                        shift(c - 1)
                    if c >= 2:
                        scaled(c - 2)
                shift(TT - 1)
                scaled(TT - 2)
                scaled(TT - 1)

            @block.tensor
            def _(pe):
                def tile(n, u, c):
                    w, ts = u % 2, slice(c * P, (c + 1) * P)
                    first, last = isinstance(n, int) and n == 0, isinstance(n, int) and n == NKEYS - 1
                    for left, right in ((ahi, vhi), (ahi, vlo), (alo, vhi)):
                        for h in range(2):
                            ins = pe.matmul(bank[2 * c + h][:, :], left[:, w, ts], right[:, w, h * 512:(h + 1) * 512],
                                            start=(first and left is ahi and right is vhi),
                                            stop=(last and left is alo))
                    return ins

                def products(n, u):
                    pe.wait_ge(s["v_lo"], n + (B0 + 1))
                    pe.wait_ge(s["a_lo"], n + 1)
                    for c in range(TT):
                        ins = tile(n, u, c)
                    ins.then_inc(s["mm"], 1)

                for u in range(UNROLL):
                    products(u, u)
                with pe.Fori(1, NKEYS // UNROLL - 1) as r:
                    for u in range(UNROLL):
                        products(r * UNROLL + u, u)
                for u in range(UNROLL - 2):
                    products(NKEYS - UNROLL + u, u)
                pe.wait_ge(s["v_lo"], NKEYS + B0 - 1)
                pe.wait_ge(s["a_lo"], NKEYS - 1)
                for c in range(TT - 1):
                    tile(NKEYS - 2, 0, c)
                pe.wait_ge(s["v_lo"], NKEYS + B0)
                pe.wait_ge(s["a_lo"], NKEYS)
                for c in range(TT):
                    if c == TT - 1:
                        tile(NKEYS - 2, 0, c)
                    tile(NKEYS - 1, 1, c).then_inc(s["tile_mm"], 1)


def layer(nc, a, out):
    h_dram = nc.dram_tensor("h_dram", (NKEYS, NKEYS, T), F32, kind="Internal").ap()
    g_dram = nc.dram_tensor("g_dram", (T // GT, NKEYS, NKEYS, GT), F32, kind="Internal").ap()
    rows_dram = nc.dram_tensor("rows_dram", (TT, SH, P), F32, kind="Internal").ap()
    with ExitStack() as ctx:
        def sb(name, shape, dt=F32):
            return ctx.enter_context(nc.sbuf_tensor(name, shape, dt))

        def sem(name):
            return ctx.enter_context(nc.semaphore(name))

        x_tm, cond, fold = sb("x_tokens", [P, TT, D]), sb("cond", [P, 48]), sb("fold", [P, 2, KD])
        ident, eps_tile = sb("identity", [P, P]), sb("eps", [P, 2])
        ln = {"stats": sb("ln_stats", [P, TT, 2, 6]), "mv": sb("ln_mean_var", [P, TT, 2]),
              "rstd": sb("ln_rstd", [P, TT]), "shift": sb("ln_shift", [P, TT])}
        mixer(nc, a, x_tm, cond, fold, ident, eps_tile, ln, rows_dram)
        with nc.sbuf_tensor("scores", [P, TT, QCH * NKEYS], F32) as scores:
            pass
        with nc.sbuf_tensor("hot_gates", [P, 2, TOK, 2, NKEYS], F32R) as hot_gates, \
                nc.sbuf_tensor("hot_keys", [P, 2, TOK, NKEYS], F32R) as hot_keys, \
                nc.sbuf_tensor("hot_equal", [P, 2, TOK, NKEYS], F32) as hot_equal:
            pass
        stream = {
            "h_in": sb("h_in", [P, 2, 4, T]), "g_in": sb("g_in", [P, 2, T // GT, 4, GT]),
            "raw": sb("e_raw", [P, 4, D]), "hi": sb("e_hi", [P, 2, D], F32R), "lo": sb("e_lo", [P, 2, D], F32R),
            "gate2": sb("gate2_row", [P, D]), "scores": scores, "hot_gates": hot_gates, "hot_keys": hot_keys,
            "hot_equal": hot_equal,
            "loaded": [sem(f"chunk_loaded{i}") for i in range(4)], "h_saved": [sem(f"h_saved{i}") for i in range(2)],
            "h_loaded": [sem(f"h_loaded{i}") for i in range(2)], "g_loaded": [sem(f"g_loaded{i}") for i in range(2)],
            "hi_done": sem("chunk_hi"), "lo_done": sem("chunk_lo"), "mm": sem("chunk_mm"),
        }
        router(nc, a, x_tm, cond, fold, ident, stream, h_dram, g_dram)
        experts(nc, a, x_tm, eps_tile, ln, stream, h_dram, g_dram, out)


def laid_out(x, c, w_cond, b_cond, w_in, sc_conv_w, ssm_conv_w, ssm_conv_b, dt_bias, a_log, d_skip, sc_norm_w,
             ssm_norm_w, w_out, ln1_g, ln1_b, w_query, sub_keys1, sub_keys2, expert_u, expert_v, ln2_g, ln2_b):
    import numpy as np

    def blocks(w, n):
        return w.reshape(KD, P, n, -1).transpose(2, 1, 0, 3)

    def columns(v):
        return v.reshape(-1, P).T

    w = w_in[0]
    keys = np.stack([sub_keys1[0], sub_keys2[0]], axis=1).reshape(2 * HEADS, NKEYS, P)
    arrays = {
        "x": x, "xT": x[0].T.reshape(KD, P, T).transpose(1, 0, 2), "cT": columns(c[0]),
        "w_cond": blocks(w_cond[0], 48), "b_condT": columns(b_cond[0]),
        "w_sc": w[:, 0:3 * D].reshape(KD, P, 3, NSC, P)[:, :, [1, 2, 0]].transpose(3, 2, 1, 0, 4)
        .reshape(3 * NSC, P, KD, P),
        "w_z": w[:, 3 * D:4 * D].reshape(4, 2, P, 2, 512).transpose(3, 0, 2, 1, 4).reshape(8, P, 2, 512),
        "w_xbc": blocks(w[:, 4 * D:4 * D + KX * P], KX),
        "w_dt": w[:, 4 * D + KX * P:].reshape(KD, P, SH).transpose(1, 0, 2),
        "sc_conv_wT": sc_conv_w[0].reshape(K_SC, NSC, P).transpose(2, 1, 0),
        "ssm_conv_wT": ssm_conv_w[0].reshape(K_SSM, KX, P).transpose(2, 1, 0),
        "ssm_conv_bT": columns(ssm_conv_b[0]), "sc_norm_wT": columns(sc_norm_w[0]),
        "ssm_norm_wT": columns(ssm_norm_w[0]), "dt_bias": dt_bias, "a_log": a_log, "d_skip": d_skip,
        "w_out": w_out[0].reshape(16, P, 1, D),
        "ln1_gT": columns(ln1_g[0]), "ln1_bT": columns(ln1_b[0]), "ln1_g": ln1_g, "ln1_b": ln1_b, "ln2_g": ln2_g, "ln2_b": ln2_b,
        "w_query": blocks(w_query[0], 2 * HEADS), "keysT": keys.transpose(2, 0, 1),
        "u_T": expert_u[0].reshape(NKEYS, NKEYS, KD, P).transpose(0, 3, 2, 1), "v": expert_v[0].reshape(NKEYS, NKEYS, D),
    }
    return {k: np.ascontiguousarray(v) for k, v in arrays.items()}


def kernel(**inputs):
    import numpy as np
    import concourse.bacc as bacc
    from concourse.bass_utils import run_bass_kernel_spmd

    arrays = laid_out(**{k: np.asarray(v) for k, v in inputs.items()})
    nc = bacc.Bacc("TRN2", target_bir_lowering=False, num_devices=1)
    a = {n: nc.dram_tensor("in_" + n, v.shape, F32, kind="ExternalInput").ap() for n, v in arrays.items()}
    out = nc.dram_tensor("out", (1, T, D), F32, kind="ExternalOutput").ap()
    layer(nc, a, out)
    r = run_bass_kernel_spmd(nc, [{"in_" + n: v for n, v in arrays.items()}], core_ids=[0])
    return r.results[0]["out"]
```
